# Optimizing a Trainium2 kernel written in Bass

```python
import jax, jax.numpy as jnp
from jax import lax
import numpy as np

D_MODEL = 1024
BATCH = 1
SEQ = 128
DEPTH = 2
DEC_BATCH = 1
DEC_SEQ = 256
PAST_LEN = 128

GRID_W = 64
N_A_LAYERS = (DEPTH + 1) // 2
N_C_LAYERS = DEPTH // 2
MIX_W = D_MODEL
A_W = MIX_W // 2
HD_A = 64
H_A = A_W // HD_A
W_LORA = 64
A_LORA = 64
G_LORA = 128
A_COLS = 3 * A_W + 2 * W_LORA + 2 * A_LORA + G_LORA
B_W = MIX_W - A_W
H_B = 4
GD_B = B_W // H_B
CHUNK = 128
AB_COLS = A_COLS + 2 * B_W
CONV_W = 31
CONV_HALF = CONV_W // 2
N_KEYS = 128
N_EXPERTS = N_KEYS * N_KEYS
PEER_HEADS = 8
PEER_TOPK = 16
D_QUERY = 256
D_HALF = D_QUERY // 2
PEER_BLOCK = 128
EPS = 1e-6
LN_EPS = 1e-5
GN_EPS = 64e-5

kernel_name = 'hybrid_rwkv7_gmlp_conformer_peer_dit_step'

def _rmsnorm(x, g):
    xf = x.astype(jnp.float32)
    y = xf * lax.rsqrt(jnp.mean(xf * xf, axis=-1, keepdims=True) + EPS)
    return (y * g.astype(jnp.float32)).astype(x.dtype)

def _layernorm(x, g, b, eps=LN_EPS):
    xf = x.astype(jnp.float32)
    m = jnp.mean(xf, axis=-1, keepdims=True)
    v = jnp.mean(jnp.square(xf - m), axis=-1, keepdims=True)
    return ((xf - m) * lax.rsqrt(v + eps) * g.astype(jnp.float32) + b.astype(jnp.float32)).astype(x.dtype)

def _modulation(cvec, w, b):
    return (jax.nn.silu(cvec) @ w + b)[:, None, :]

def _centred_shift(z):
    zp = jnp.pad(z, ((0, 0), (1, 1), (0, 0)))
    return 0.5 * (zp[:, :-2] + zp[:, 2:])

def _wkv_scan(r, w, k, v, a, b, s0, reverse):
    def step(S, inp):
        rt, wt, kt, vt, at, bt = inp
        sa = jnp.einsum('nhij,nhj->nhi', S, at)
        S = S * wt[:, :, None, :] + sa[..., None] * bt[:, :, None, :] + vt[..., None] * kt[:, :, None, :]
        return S, jnp.einsum('nhij,nhj->nhi', S, rt)
    xs = tuple(jnp.moveaxis(t, 1, 0) for t in (r, w, k, v, a, b))
    s_fin, y = lax.scan(step, s0.astype(jnp.float32), xs, reverse=reverse)
    return s_fin, jnp.moveaxis(y, 0, 1)

def _rwkv7_bidir(za, s0, i, p):
    n, T, _ = za.shape
    za = za.astype(jnp.float32)
    za = za + p['mu_a'][i] * (_centred_shift(za) - za)
    sizes = [A_W, A_W, A_W, W_LORA, W_LORA, A_LORA, A_LORA]
    splits = [int(s) for s in np.cumsum(sizes)]
    r, k, v, wlo_f, wlo_b, alo_f, alo_b, glo = jnp.split(za, splits, axis=-1)
    hs = lambda t: t.reshape(n, T, H_A, HD_A)
    g = jax.nn.sigmoid(glo) @ p['g2'][i]
    kk = hs(k * p['k_k'][i])
    kk = kk / jnp.maximum(jnp.sqrt(jnp.sum(kk * kk, axis=-1, keepdims=True)), 1e-12)
    y_sum = 0.0
    bonus = 0.0
    finals = []
    for d, (wlo, alo, rev) in enumerate(((wlo_f, alo_f, False), (wlo_b, alo_b, True))):
        w_log = -jax.nn.softplus(-(p['w0'][i, d] + jnp.tanh(wlo) @ p['w2'][i, d])) - 0.5
        decay = jnp.exp(-jnp.exp(w_log))
        a = jax.nn.sigmoid(p['a0'][i, d] + alo @ p['a2'][i, d])
        kd = k * (1.0 + (a - 1.0) * p['k_a'][i])
        s_fin, y = _wkv_scan(hs(r), hs(decay), hs(kd), hs(v), -kk, kk * hs(a), s0[:, d], rev)
        y_sum = y_sum + y
        bonus = bonus + jnp.sum(hs(r * kd * p['r_k'][i]), axis=-1, keepdims=True) * hs(v)
        finals.append(s_fin)
    m = jnp.mean(y_sum, axis=-1, keepdims=True)
    var = jnp.mean(jnp.square(y_sum - m), axis=-1, keepdims=True)
    gn = ((y_sum - m) * lax.rsqrt(var + GN_EPS)).reshape(n, T, A_W) * p['lnx_g'][i] + p['lnx_b'][i]
    out = (gn + bonus.reshape(n, T, A_W)) * g
    return out, jnp.stack(finals, axis=1)

def _chunk_gmlp(u, vb, i, p):
    n, T, _ = u.shape
    vb = _layernorm(vb.reshape(n, T, H_B, GD_B), p['lnv_g'][i].reshape(H_B, GD_B), p['lnv_b'][i].reshape(H_B, GD_B))
    vb = vb.reshape(n, T // CHUNK, CHUNK, H_B, GD_B)
    sp = jnp.einsum('gpq,ncqgd->ncpgd', p['w_s'][i], vb) + p['b_s'][i].T[None, None, :, :, None]
    return u * sp.reshape(n, T, B_W)

def _mixer_ab(h, i, p, s0):
    z = h @ p['w_in_ab'][i]
    za = z[..., :A_COLS]
    u = z[..., A_COLS:A_COLS + B_W]
    vb = z[..., A_COLS + B_W:]
    ya, s_fin = _rwkv7_bidir(za, s0, i, p)
    yb = _chunk_gmlp(u, vb, i, p)
    y = jnp.concatenate([ya.astype(h.dtype), yb.astype(h.dtype)], axis=-1) @ p['w_out_ab'][i]
    return y, s_fin

def _conformer_conv(h, i, p, seg_len):
    n, T, D = h.shape
    z = h @ p['w_pw1'][i] + p['b_pw1'][i]
    z = z[..., :D] * jax.nn.sigmoid(z[..., D:])
    segs = T // seg_len
    zr = z.reshape(n * segs, seg_len, D)
    zr = lax.conv_general_dilated(zr, p['conv_k'][i][:, None, :].astype(zr.dtype), window_strides=(1,),
                                  padding=((CONV_HALF, CONV_HALF),), dimension_numbers=('NWC', 'WIO', 'NWC'),
                                  feature_group_count=D) + p['conv_b'][i]
    z = _layernorm(zr.reshape(n, T, D), p['lnc_g'][i], p['lnc_b'][i])
    return jax.nn.silu(z) @ p['w_pw2'][i] + p['b_pw2'][i]

def _peer(h, l, p):
    n, T, D = h.shape
    wq = p['w_query'][l]
    sk = p['sub_keys'][l].astype(jnp.float32)
    eu = p['expert_u'][l]
    ev = p['expert_v'][l]

    def block(xb):
        P = xb.shape[0]
        q = (xb @ wq).reshape(P, PEER_HEADS, 2, D_HALF).astype(jnp.float32)
        s = jnp.einsum('phcd,ckd->phck', q, sk)
        sv, si = lax.top_k(s, PEER_TOPK)
        cand = (sv[:, :, 0, :, None] + sv[:, :, 1, None, :]).reshape(P, PEER_HEADS, PEER_TOPK * PEER_TOPK)
        cidx = (si[:, :, 0, :, None] * N_KEYS + si[:, :, 1, None, :]).reshape(P, PEER_HEADS, PEER_TOPK * PEER_TOPK)
        fv, fi = lax.top_k(cand, PEER_TOPK)
        eidx = jnp.take_along_axis(cidx, fi, axis=-1)
        gate = jax.nn.softmax(fv, axis=-1)
        ue = eu[eidx]
        ve = ev[eidx]
        act = jax.nn.gelu(jnp.einsum('phkd,pd->phk', ue, xb).astype(jnp.float32), approximate=False)
        return jnp.einsum('phk,phkd->pd', (gate * act).astype(xb.dtype), ve)

    out = lax.map(block, h.reshape(-1, PEER_BLOCK, D))
    return out.reshape(n, T, D)

def _layer(x, mod, l, p, s0, seg_len):
    sh1, sc1, gt1, sh2, sc2, gt2 = jnp.split(mod.astype(x.dtype), 6, axis=-1)
    h = _rmsnorm(x, p['norm1'][l]) * (1 + sc1) + sh1
    s_fin = None
    if l % 2 == 0:
        y, s_fin = _mixer_ab(h, l // 2, p, s0)
    else:
        y = _conformer_conv(h, l // 2, p, seg_len)
    x = x + gt1 * y
    h = _rmsnorm(x, p['norm2'][l]) * (1 + sc2) + sh2
    x = x + gt2 * _peer(h, l, p)
    return x, s_fin

def setup_inputs(seed: int = 0) -> dict:
    key = jax.random.key(seed)
    ks = iter(jax.random.split(key, 64))
    f32 = jnp.float32

    def nrm(shape, scale):
        return jax.random.normal(next(ks), shape, f32) * scale

    def uni(shape, lo, hi):
        return jax.random.uniform(next(ks), shape, f32, lo, hi)

    D = D_MODEL
    return {
        'x_prompt': nrm((BATCH, SEQ, D), 1.0),
        'x_sample': nrm((DEC_BATCH, DEC_SEQ, D), 1.0),
        'state_rwkv': nrm((DEC_BATCH, N_A_LAYERS, 2, H_A, HD_A, HD_A), 0.5),
        'c': nrm((DEC_BATCH, D), 1.0),
        'c_ctx': nrm((D,), 1.0),
        'w_mod': nrm((DEPTH, D, 6 * D), 0.5 * D ** -0.5),
        'b_mod': nrm((DEPTH, 6 * D), 0.02),
        'norm1': 1.0 + nrm((DEPTH, D), 0.02),
        'norm2': 1.0 + nrm((DEPTH, D), 0.02),
        'norm_f': 1.0 + nrm((D,), 0.02),
        'w_in_ab': nrm((N_A_LAYERS, D, AB_COLS), D ** -0.5),
        'mu_a': uni((N_A_LAYERS, A_COLS), 0.0, 1.0),
        'w0': nrm((N_A_LAYERS, 2, A_W), 0.5),
        'w2': nrm((N_A_LAYERS, 2, W_LORA, A_W), 0.5 * W_LORA ** -0.5),
        'a0': nrm((N_A_LAYERS, 2, A_W), 0.3),
        'a2': nrm((N_A_LAYERS, 2, A_LORA, A_W), 0.5 * A_LORA ** -0.5),
        'g2': nrm((N_A_LAYERS, G_LORA, A_W), G_LORA ** -0.5),
        'k_k': 0.85 + nrm((N_A_LAYERS, A_W), 0.05),
        'k_a': 1.0 + nrm((N_A_LAYERS, A_W), 0.05),
        'r_k': nrm((N_A_LAYERS, A_W), 0.1),
        'lnx_g': 1.0 + nrm((N_A_LAYERS, A_W), 0.02),
        'lnx_b': nrm((N_A_LAYERS, A_W), 0.02),
        'lnv_g': 1.0 + nrm((N_A_LAYERS, B_W), 0.02),
        'lnv_b': nrm((N_A_LAYERS, B_W), 0.02),
        'w_s': nrm((N_A_LAYERS, H_B, CHUNK, CHUNK), CHUNK ** -0.5),
        'b_s': 1.0 + nrm((N_A_LAYERS, H_B, CHUNK), 0.1),
        'w_out_ab': nrm((N_A_LAYERS, MIX_W, D), MIX_W ** -0.5),
        'w_pw1': nrm((N_C_LAYERS, D, 2 * D), D ** -0.5),
        'b_pw1': nrm((N_C_LAYERS, 2 * D), 0.02),
        'conv_k': nrm((N_C_LAYERS, CONV_W, D), CONV_W ** -0.5),
        'conv_b': nrm((N_C_LAYERS, D), 0.02),
        'lnc_g': 1.0 + nrm((N_C_LAYERS, D), 0.02),
        'lnc_b': nrm((N_C_LAYERS, D), 0.02),
        'w_pw2': nrm((N_C_LAYERS, D, D), D ** -0.5),
        'b_pw2': nrm((N_C_LAYERS, D), 0.02),
        'w_query': nrm((DEPTH, D, PEER_HEADS * D_QUERY), D ** -0.5),
        'sub_keys': nrm((DEPTH, 2, N_KEYS, D_HALF), D_HALF ** -0.5),
        'expert_u': nrm((DEPTH, N_EXPERTS, D), D ** -0.5),
        'expert_v': nrm((DEPTH, N_EXPERTS, D), 0.5),
    }

def reference(x_prompt, x_sample, state_rwkv, c, c_ctx, w_mod, b_mod, norm1, norm2, norm_f,
              w_in_ab, mu_a, w0, w2, a0, a2, g2, k_k, k_a, r_k, lnx_g, lnx_b, lnv_g, lnv_b, w_s, b_s, w_out_ab,
              w_pw1, b_pw1, conv_k, conv_b, lnc_g, lnc_b, w_pw2, b_pw2,
              w_query, sub_keys, expert_u, expert_v):
    p = dict(norm1=norm1, norm2=norm2, w_in_ab=w_in_ab, mu_a=mu_a, w0=w0, w2=w2, a0=a0, a2=a2, g2=g2,
             k_k=k_k, k_a=k_a, r_k=r_k, lnx_g=lnx_g, lnx_b=lnx_b, lnv_g=lnv_g, lnv_b=lnv_b, w_s=w_s, b_s=b_s,
             w_out_ab=w_out_ab, w_pw1=w_pw1, b_pw1=b_pw1, conv_k=conv_k, conv_b=conv_b, lnc_g=lnc_g,
             lnc_b=lnc_b, w_pw2=w_pw2, b_pw2=b_pw2, w_query=w_query, sub_keys=sub_keys,
             expert_u=expert_u, expert_v=expert_v)

    xc = x_prompt
    n_ctx, ctx_len = x_prompt.shape[0], x_prompt.shape[1]
    zero_state = jnp.zeros((n_ctx, 2, H_A, HD_A, HD_A), jnp.float32)
    ctx_states = []
    for l in range(DEPTH):
        mod = _modulation(c_ctx[None, :], w_mod[l], b_mod[l])
        xc, s_fin = _layer(xc, mod, l, p, zero_state, ctx_len)
        if s_fin is not None:
            ctx_states.append(s_fin)
    y_prompt = _rmsnorm(xc, norm_f)
    new_state_rwkv = jnp.stack(ctx_states, axis=1).astype(x_prompt.dtype)

    rows = x_sample.shape[1] // GRID_W
    xs = x_sample
    for l in range(DEPTH):
        mod = _modulation(c, w_mod[l], b_mod[l])
        s0 = state_rwkv[:, l // 2] if l % 2 == 0 else None
        xs, _ = _layer(xs, mod, l, p, s0, x_sample.shape[1] // rows)
    y_sample = _rmsnorm(xs, norm_f)

    return (y_prompt, y_sample, new_state_rwkv)


_drawn_inputs = setup_inputs


def setup_inputs(seed=0):
    import zlib

    import numpy as np

    out = dict(_drawn_inputs(seed))
    spreads = {}
    factors = {'state_rwkv': 6.107,
     'norm2': 17.428,
     'norm_f': 23.387,
     'lnx_g': 80.566,
     'lnx_b': 87.957,
     'lnv_g': 36.368,
     'lnv_b': 35.715,
     'b_pw1': 8.0,
     'conv_b': 6.481,
     'lnc_g': 98.987,
     'lnc_b': 93.74,
     'b_pw2': 65.926,
     'b_s': 2.9,
     'r_k': 4.348}
    for name, (base, spread) in spreads.items():
        noise = np.random.default_rng([zlib.crc32(name.encode()), seed]).standard_normal(out[name].shape)
        drawn = base * np.exp(spread * noise) if base else spread * noise
        out[name] = __import__('jax').numpy.asarray(drawn.astype(out[name].dtype))
    for name, factor in factors.items():
        out[name] = (out[name] * factor).astype(out[name].dtype)
    return out
```

```python
from contextlib import ExitStack

import numpy as np

import concourse.bass as bass
from concourse import mybir

P = 128
D = 1024
DC = D // P
T_CTX, T_LAT = 128, 256
T = T_CTX + T_LAT
TB = T // P
GROUPS = ((0, T_CTX), (T_CTX, T))
A_W = 512
HEAD = 64
NP_ = A_W // P
A_CH = 15
IN_CH = 23
CHUNK = 64
NCH = T // CHUNK
TS = T + 1
LAT0 = T_CTX + 1
CONV_W, HALO = 31, 15
ROW = 64
NROW = T // ROW
ROWP = ROW + 2 * HALO
HEADS, TOPK, NK = 8, 16, 128
RING = 8
NHALF = 2
JH = NK // NHALF
OHR = 8

ALU = mybir.AluOpType
ACT = mybir.ActivationFunctionType
AX = mybir.AxisListType.X
F32 = mybir.dt.float32
U32 = mybir.dt.uint32

EPS, LN_EPS, GN_EPS = 1e-6, 1e-5, 64e-5
DECAY = float(np.exp(-0.5))
LOWEST = -3.4e38


SMALL = [
    ("ident", 128), ("mean_d", 128), ("mean_p", 128), ("head_sum", 128), ("head_mean", 128), ("iota", 128),
    ("strict", 128), ("incl", 128), ("bands", 12 * 64), ("eye64", 64), ("keep", 2 * TS), ("zeros", 128), ("ones", 128),
    ("b_mod", 96), ("norm1", 16), ("norm2", 16), ("norm_f", 8), ("mu", 15), ("w0", 8), ("a0", 8), ("k_k", 4),
    ("k_a", 4), ("r_k", 4), ("lnx_g", 4), ("lnx_b", 4), ("lnv_g", 4), ("lnv_b", 4), ("b_pw1", 16),
    ("conv_k", 8 * CONV_W), ("conv_b", 8), ("lnc_g", 8), ("lnc_b", 8), ("b_pw2", 8),
    ("w2", A_W), ("a2", A_W), ("g2", A_W), ("w_sT", 4 * P), ("b_s", 4 * P), ("sk", 2 * 2 * P), ("s0", 2 * NP_ * HEAD),
    ("cvec", 16),
]
SM = {}
_at = 0
for _name, _n in SMALL:
    SM[_name] = (_at, _n)
    _at += _n
NSMALL = _at

T_MOD, T_IN, T_OUT, T_Q0, T_PW1, T_PW2, T_Q1 = 0, 96, 119, 127, 143, 159, 167
N_DENSE = 183


def tile_plan():
    pos = {"mod": 0, "in": 96, "out": 119, "q0": 127}
    n = 143
    pos["e0"] = n
    n += 2 * NK
    pos["pw1"] = n
    pos["pw2"] = n + 16
    pos["q1"] = n + 24
    pos["e1"] = n + 40
    pos["end"] = n + 40 + 2 * NK
    return pos


POS = tile_plan()


class Steps:

    def __init__(self, eng, sem):
        self.eng, self.sem, self.n = eng, sem, 0

    def mark(self, ins):
        self.n += 1
        ins.then_inc(self.sem, 1)

    def settle(self):
        self.eng.wait_ge(self.sem, self.n)

    def link(self, ins):
        self.mark(ins)
        self.settle()


def tcol(c):
    return c * CHUNK + (1 if c * CHUNK >= T_CTX else 0)


SEG = ((0, 0, T_CTX), (T_CTX, LAT0, T_LAT))

SCAN = (
    ((("lat", 2), ("ctx", 0)), (("lat", 3), ("ctx", 1)), (("lat", 4),), (("lat", 5),)),
    ((("lat", 5), ("ctx", 1)), (("lat", 4), ("ctx", 0)), (("lat", 3),), (("lat", 2),)),
)
LEVELS = (2, 4, 8, 16, 32)


def pair_jobs(d):
    jobs = [("LT", "V"), ("LAK", "V"), ("MRB", "V"), ("MRK", "V")]
    if d == 0:
        jobs.append(("VTOK", "A"))
    jobs.append(("D0", "V"))
    for n in LEVELS:
        jobs.append(("F%d" % n, "A"))
        if n != LEVELS[-1]:
            jobs.append(("G%d" % n, "V"))
        jobs.append(("GT%d" % n, "V"))
    jobs += [("BTOK", "A"), ("KTOK", "A")]
    return [(name, g, e) for name, e in jobs for g in range(3)]


def scan_jobs(d):
    out = []
    for s in range(4):
        out += [("X", s, "A"), ("U", s, "A"), ("S", s, "V"), ("Y", s, "V")]
    return out


RW_JOBS = []
for _d in range(2):
    RW_JOBS += [(_d,) + j for j in pair_jobs(_d)] + [(_d,) + j for j in scan_jobs(_d)]
RW_AT = {j[:3]: i for i, j in enumerate(RW_JOBS)}
RW_EV = []
_c = {"A": 0, "V": 0}
for _j in RW_JOBS:
    _c[_j[3]] += 1
    RW_EV.append((_j[3], _c[_j[3]]))


def build_trunk(nc, x_t, small_d, w_tiles, e_u, e_v, y_t, s_new, dbg=None):
    ctx = ExitStack()
    with ctx:
        def sb(name, cols, dt=F32):
            return ctx.enter_context(nc.sbuf_tensor(name, [P, cols], dt))

        def sem(name):
            return ctx.enter_context(nc.semaphore(name))

        x_sb = sb("x_sb", DC * T)
        x3 = x_sb[:, :].rearrange("p (c t) -> p c t", t=T)
        h_sb = sb("h_sb", DC * T + 4)
        h3 = h_sb[:, 0:DC * T].rearrange("p (c t) -> p c t", t=T)
        ring = sb("ring", RING * D)
        small = sb("small", NSMALL)
        modv = sb("modv", 192)
        scale = sb("scale", 2 * 2 * 16)
        silc = sb("silc", 16)
        epsb = sb("epsb", 4)
        ARENA = 31600
        arena = sb("arena", ARENA)
        bank = [ctx.enter_context(nc.psum_tensor("bank%d" % i, [P, 512], F32)) for i in range(8)]

        def sm(name, a=0, b=None):
            o, n = SM[name]
            return small[:, o + a:o + (n if b is None else b)]

        def ar(o, n):
            assert o + n <= ARENA, (o, n)
            return arena[:, o:o + n]

        mod4 = modv[:, :].rearrange("p (l c g) -> p l c g", l=2, g=2)
        scale5 = scale[:, :].rearrange("p (l n c g) -> p l n c g", l=2, n=2, g=2)

        s_x = sem("x_landed")
        s_small = sem("small_landed")
        w_land = [sem("w_landed%d" % i) for i in range(RING)]
        w_used = sem("w_used")
        s_out = sem("stores_landed")
        pool_init = sem("pool_init")
        a_step = sem("act_step")
        v_step = sem("dve_step")
        g_step = sem("pool_step")
        silc_ready = sem("silc_ready")
        mod_evac = sem("mod_evacuated")
        mod_ready = sem("mod_ready")
        sq_ready = sem("squares_ready")
        ss_ready = sem("mean_square_ready")
        rt_ready = sem("root_ready")
        xn_ready = sem("x_normed")
        h_ready = sem("h_ready")
        z_evac = sem("z_evacuated")
        zs_ready = sem("z_shifted")
        act_ready = sem("act_readyputs_ready")
        kk_sq = sem("kk_squares")
        kk_ss = sem("kk_sums")
        kk_rt = sem("kk_roots")
        lw_mm = sem("lora_products")
        lw_ev = sem("lora_evacuated")
        lw_sum = sem("log_decay_summed")
        ex_ready = sem("exps_ready")
        sc_ready = sem("scaled_ready")
        rw_mm = sem("rwkv_job_product")
        rw_evA = sem("rwkv_job_evac_act")
        rw_evV = sem("rwkv_job_evac_dve")
        bands_used = sem("bands_done")
        lt_ready = sem("lt_ready")
        st_in = sem("stat_inputs")
        st_mm = sem("stat_products")
        st_rt = sem("stat_roots")
        gm_t = sem("gmlp_transposed")
        gm_te = sem("gmlp_transposed_evac")
        gm_mm = sem("gmlp_mixed")
        gm_ev = sem("gmlp_mixed_evac")
        mix_ready = sem("mixer_input_ready")
        conv_act = sem("conv_activated")
        gm_norm = sem("gmlp_normed")
        out_used = sem("expert_out_added")
        res_done = sem("residual_added")
        glu_g = sem("glu_gate_ready")
        glu_done = sem("glu_done")
        conv_done = sem("conv_done")
        conv_tap = sem("conv_taps_added")
        halo_done = sem("halo_done")
        pw2_ev = sem("pw2_evacuated")
        q_evac = sem("q_evacuated")
        s_mm = sem("scores_product")
        s_evac = sem("scores_evacuated")
        s_free = sem("scores_used")
        cand_max = sem("cand_max")
        e_ready = sem("gate_exp_ready")
        route = sem("routes_ready")
        route_t = sem("routes_transposed")
        route_e = sem("routes_evacuated")
        oh_ready = sem("one_hots_ready")
        tok_mm = sem("token_gate_product")
        g_evac = sem("gate_matrix_evacuated")
        gelu_done = sem("gelu_done")
        coef_ready = sem("coef_ready")
        out_evac = sem("expert_out_evacuated")
        out_t = sem("expert_out_transposed")
        y_ready = sem("y_ready")

        sq3 = ar(0, 3072).rearrange("p (c t) -> p c t", t=T)
        root = ar(3072, T)
        rstd = ar(3072 + T, T)

        o = 0
        ZS = o
        zs = ar(o, A_CH * TS).rearrange("p (c t) -> p c t", t=TS); o += A_CH * TS
        ZP = o
        zp = ar(o, A_CH * (TS + 2)).rearrange("p (c t) -> p c t", t=TS + 2)
        GM = ZP + A_CH * (TS + 2)
        gu = ar(GM, 4 * T).rearrange("p (c t) -> p c t", t=T)
        gv = ar(GM + 1536, 4 * T).rearrange("p (c t) -> p c t", t=T)
        gc = ar(GM + 3072, 4 * T).rearrange("p (c t) -> p c t", t=T)
        gs = ar(GM + 4608, 4 * T).rearrange("p (c t) -> p c t", t=T)
        gtok = ar(GM + 6144, 12 * P)
        yb = h_sb[:, 1540:1540 + 4 * T].rearrange("p (c t) -> p c t", t=T)
        kdsum = h_sb[:, 0:1540].rearrange("p (c t) -> p c t", t=TS)
        zshift = ar(GM + 7680, 2 * TS).rearrange("p (c t) -> p c t", t=TS)
        o = ZP

        def take(n):
            nonlocal o
            r = ar(o, n)
            o += n
            return r

        def c4(a):
            return a.rearrange("p (c t) -> p c t", t=TS)

        at_, bt_, kt_, rt_ = (c4(take(1540)) for _ in range(4))
        lak, mrb, mrk, dT, vtok = (take(1536) for _ in range(5))
        lt_o = o
        ltm, dm, fm, em = (take(1536) for _ in range(4))
        btok, ktok = ltm, fm
        xs_, us_ = ar(lt_o + 1536, 512), ar(lt_o + 1536 + 512, 512)
        tmp1, tmp2, tmp3 = (c4(ar(lt_o + i * 1540, 1540)) for i in range(3))
        ysum = c4(take(1540))
        nkk = c4(take(1540))
        tmp0 = c4(take(1540))
        state = take(2 * 2 * 256)
        pC = take(24)
        th = zs[:, 12, :]
        sg = zs[:, 14, :]
        gy = at_
        gq = bt_
        gmean = kt_
        ya3 = ar(ZP + 1540, 4 * T)
        zc = ar(0, DC * NROW * ROWP).rearrange("p (c r t) -> p c r t", c=DC, t=ROWP)
        CO = DC * NROW * ROWP
        acc = ar(CO, DC * T).rearrange("p (c t) -> p c t", t=T)
        acq = ar(CO + 3072, DC * T).rearrange("p (c t) -> p c t", t=T)
        accs = ar(CO + 6144, DC * T).rearrange("p (c t) -> p c t", t=T)
        mean_sb = ar(CO + 9216, T)
        lroot = ar(CO + 9216 + T, T)
        lrstd = ar(CO + 9216 + 2 * T, T)
        glug = ar(CO + 9216 + 3 * T, 2 * T).rearrange("p (c t) -> p c t", t=T)
        pw2t = ar(CO + 9216 + 5 * T, 2 * T).rearrange("p (c t) -> p c t", t=T)
        gate_m = ar(0, JH * T).rearrange("p (j t) -> p j t", t=T)
        o = JH * T
        oh_i = take(OHR * P).rearrange("p (s i) -> p s i", i=P)
        oh_j = take(OHR * JH).rearrange("p (s j) -> p s j", j=JH)
        ga = take(2 * T).rearrange("p (s t) -> p s t", t=T)
        coef = take(2 * T).rearrange("p (s t) -> p s t", t=T)
        routeT = take(3 * T).rearrange("p (k t) -> p k t", t=T)
        q_sb = take(2 * T).rearrange("p (s t) -> p s t", t=T)
        sc_sb = take(2 * T).rearrange("p (s b k) -> p s b k", s=2, k=P)
        o = 0
        sv = take(3 * 256).rearrange("p (b j k) -> p b j k", b=3, k=16)
        si = take(3 * 256).bitcast(U32).rearrange("p (b j k) -> p b j k", b=3, k=16)
        sif = take(3 * 256).rearrange("p (b j k) -> p b j k", b=3, k=16)
        stmp = take(2 * T).rearrange("p (s b k) -> p s b k", s=2, k=P)
        cand = take(3 * 2048).rearrange("p (b h k) -> p b h k", b=3, k=256)
        ctmp = take(2048).rearrange("p (h k) -> p h k", k=256)
        fv = take(T).rearrange("p (b h k) -> p b h k", b=3, k=16)
        fi = take(T).bitcast(U32).rearrange("p (b h k) -> p b h k", b=3, k=16)
        fa_u = take(T).bitcast(U32).rearrange("p (b h k) -> p b h k", b=3, k=16)
        fb_u = take(T).bitcast(U32).rearrange("p (b h k) -> p b h k", b=3, k=16)
        fa = take(T).rearrange("p (b h k) -> p b h k", b=3, k=16)
        fb = take(T).rearrange("p (b h k) -> p b h k", b=3, k=16)
        ge = take(T).rearrange("p (b h k) -> p b h k", b=3, k=16)
        gsum = take(24).rearrange("p (b h k) -> p b h k", b=3, k=1)
        routes = take(3 * T).rearrange("p (k b x) -> p k b x", k=3, b=3)
        oh1 = take(2048).rearrange("p (h k a) -> p h k a", h=8, a=16)
        oh2 = take(2048).rearrange("p (h k a) -> p h k a", h=8, a=16)
        otok = ar(0, 3072).rearrange("p (b c) -> p b c", b=3)

        block = ctx.enter_context(nc.Block())

        @block.sync
        def _(sp):
            def load(n, src):
                if n >= RING:
                    sp.wait_ge(w_used, n - RING + 1)
                sp.dma_start(ring[:, (n % RING) * D:(n % RING + 1) * D], src).then_inc(w_land[n % RING], 16)

            def experts(l, half, base):
                u = e_u[l]
                v = e_v[l]
                j0 = half * JH

                def vsrc(j):
                    return v[bass.ds(j, 1), :, :].rearrange("o i d -> (o i) d") if not isinstance(j, int) else v[j]

                def usrc(j):
                    return u[bass.ds(j, 1), :, :].rearrange("o i d -> (o i) d") if not isinstance(j, int) else u[j]

                load(base, u[j0])
                with sp.Fori(0, 15) as it:
                    for k in range(4):
                        for w in range(2):
                            n = base + 1 + 2 * k + w
                            sp.wait_ge(w_used, it * 8 + (n - RING + 1))
                            src = usrc(it * 4 + (j0 + k + 1)) if w == 0 else vsrc(it * 4 + (j0 + k))
                            sp.dma_start(ring[:, (n % RING) * D:(n % RING + 1) * D], src)\
                              .then_inc(w_land[n % RING], 16)
                n = base + 1 + 120
                for s in range(60, 63):
                    load(n, u[j0 + s + 1])
                    load(n + 1, v[j0 + s])
                    n += 2
                load(n, v[j0 + 63])

            sp.dma_start(small[:, :], small_d).then_inc(s_small, 16)
            for n in range(8):
                load(n, w_tiles[n])
            sp.dma_start(x3, x_t.rearrange("(c p) t -> p c t", p=P)).then_inc(s_x, 16)
            for n in range(8, 143):
                load(n, w_tiles[n])
            for half in range(NHALF):
                experts(0, half, POS["e0"] + half * 128)
            for n in range(POS["pw1"], POS["e1"]):
                load(n, w_tiles[n - POS["pw1"] + T_PW1])
            for half in range(NHALF):
                experts(1, half, POS["e1"] + half * 128)
            sp.wait_ge(rw_evV, RW_EV[RW_AT[(1, "S", 1)]][1])
            for d in range(2):
                sp.dma_start(s_new[d].rearrange("q p i -> p q i"),
                             small[:, SM["s0"][0] + d * 256:SM["s0"][0] + (d + 1) * 256]
                             .rearrange("p (q i) -> p q i", i=HEAD)).then_inc(s_out, 16)
            sp.wait_ge(y_ready, 1)
            sp.dma_start(y_t.rearrange("(c p) t -> p c t", p=P), h3).then_inc(s_out, 16)
            nst = 3
            if dbg is not None:
                sp.dma_start(dbg, arena[:, :]).then_inc(s_out, 16)
                nst = 4
            sp.wait_ge(s_out, 16 * nst)

        @block.gpsimd
        def _(pool):
            pool.memset(zp[:, :, 0:1], 0.0).then_inc(pool_init, 1)
            pool.memset(zp[:, :, T_CTX + 1:T_CTX + 2], 0.0).then_inc(pool_init, 1)
            pool.memset(zp[:, :, TS + 1:TS + 2], 0.0).then_inc(pool_init, 1)
            pool.memset(epsb[:, 0:1], EPS).then_inc(pool_init, 1)
            pool.memset(epsb[:, 1:2], LN_EPS).then_inc(pool_init, 1)
            pool.memset(epsb[:, 2:3], GN_EPS).then_inc(pool_init, 1)
            pool.wait_ge(h_ready, 24)
            pool.memset(zc[:, :, :, :], 0.0).then_inc(pool_init, 1)

        @block.scalar
        def _(act):
            st = Steps(act, a_step)
            norm_n = [0]

            def norm_act(l, which):
                u = norm_n[0]
                norm_n[0] += 1
                act.activation(sq3, x3, ACT.Square).then_inc(sq_ready, 1)
                act.wait_ge(ss_ready, u + 1)
                act.activation(root, bank[0][:, 0:T], ACT.Sqrt, bias=epsb[:, 0:1]).then_inc(rt_ready, 1)
                if which < 2:
                    act.wait_ge(xn_ready, u + 1)
                    for c in range(DC):
                        for g, (a, b) in enumerate(GROUPS):
                            ins = act.activation(h3[:, c, a:b], sq3[:, c, a:b], ACT.Identity,
                                                 scale=scale5[:, l, which, c, g:g + 1],
                                                 bias=mod4[:, l, 24 * which + c, g:g + 1])
                        ins.then_inc(h_ready, 1)

            act.sem_inc(g_evac, 2)
            act.sem_inc(gelu_done, 2)
            act.wait_ge(s_small, 16)
            act.activation(silc[:, :], sm("cvec"), ACT.Silu).then_inc(silc_ready, 1)
            act.wait_ge(s_x, 16)
            act.wait_ge(pool_init, 6)
            act.wait_ge(mod_ready, 3)
            norm_act(0, 0)
            for m in range(IN_CH):
                act.wait_ge(w_used, POS["in"] + m + 1)
                ps = bank[m % 4]
                if m < A_CH:
                    st.mark(act.activation(zp[:, m, 1:1 + T_CTX], ps[:, 0:T_CTX], ACT.Copy))
                    act.activation(zp[:, m, 1 + LAT0:1 + TS], ps[:, T_CTX:T], ACT.Copy).then_inc(z_evac, 1)
                else:
                    dst = gu[:, m - 15, :] if m < 19 else gv[:, m - 19, :]
                    act.activation(dst, ps[:, 0:T], ACT.Copy).then_inc(z_evac, 1)
            for g in range(4):
                act.wait_ge(st_in, g + 1)
                act.activation(gs[:, g, :], gc[:, g, :], ACT.Square).then_inc(act_ready, 1)
            for g in range(4):
                act.wait_ge(st_mm, 4 + g + 1)
                act.activation(gs[:, g, :], bank[4 + g][:, 0:T], ACT.Sqrt, bias=epsb[:, 1:2]).then_inc(st_rt, 1)
            for g in range(4):
                act.wait_ge(gm_t, g + 1)
                act.activation(gtok[:, g * T:(g + 1) * T], bank[g][:, 0:T], ACT.Copy).then_inc(gm_te, 1)
            act.wait_ge(zs_ready, A_CH)
            act.wait_ge(gm_ev, 4)
            act.activation(th, zs[:, 12, :], ACT.Tanh).then_inc(act_ready, 1)
            act.activation(sg, zs[:, 14, :], ACT.Sigmoid).then_inc(act_ready, 1)
            act.wait_ge(kk_sq, 1)
            act.activation(tmp2, nkk, ACT.Square).then_inc(act_ready, 1)
            for p in range(4):
                act.wait_ge(kk_ss, p + 1)
                act.activation(tmp1[:, p, :], bank[p][:, 0:TS], ACT.Sqrt).then_inc(kk_rt, 1)
            for d in range(2):
                if d == 1:
                    act.wait_ge(rw_mm, RW_AT[(0, "Y", 3)] + 1)
                else:
                    act.wait_ge(lw_sum, 1)
                for p in range(4):
                    act.wait_ge(lw_mm, 8 * d + 2 * p + 1)
                    act.activation(tmp1[:, p, :], bank[p][:, 0:TS], ACT.Sigmoid,
                                   bias=sm("w0", 4 * d + p, 4 * d + p + 1)).then_inc(lw_ev, 1)
                    act.wait_ge(lw_mm, 8 * d + 2 * p + 2)
                    act.activation(tmp2[:, p, :], bank[4 + p][:, 0:TS], ACT.Sigmoid,
                                   bias=sm("a0", 4 * d + p, 4 * d + p + 1)).then_inc(lw_ev, 1)
                act.wait_ge(lw_sum, 2 * d + 2)
                act.activation(rt_, tmp3, ACT.Exp, scale=-DECAY).then_inc(ex_ready, 1)
                act.activation(kt_, tmp3, ACT.Exp, scale=DECAY).then_inc(ex_ready, 1)
                act.wait_ge(lw_sum, 2 * d + 3)
                act.activation(at_, tmp1, ACT.Exp, scale=-DECAY).then_inc(ex_ready, 1)
                for j, (dd, name, g, e) in enumerate(RW_JOBS):
                    if dd != d or e != "A":
                        continue
                    act.wait_ge(rw_mm, j + 1)
                    ps = bank[j % 8]
                    if name == "VTOK":
                        dst = vtok[:, g * 512:(g + 1) * 512]
                    elif name == "BTOK":
                        dst = btok[:, g * 512:(g + 1) * 512]
                    elif name == "KTOK":
                        dst = ktok[:, g * 512:(g + 1) * 512]
                    elif name[0] == "F":
                        dst = fm[:, g * 512:(g + 1) * 512]
                    elif name == "X":
                        dst = xs_[:, :]
                    else:
                        dst = us_[:, :]
                    if name in ("X", "U"):
                        w = 256 * len(SCAN[d][g])
                        act.activation(dst[:, 0:w], ps[:, 0:w], ACT.Copy).then_inc(rw_evA, 1)
                    else:
                        act.activation(dst, ps[:, :], ACT.Copy).then_inc(rw_evA, 1)
            act.wait_ge(st_in, 5)
            act.activation(gq, gy, ACT.Square).then_inc(act_ready, 1)
            for p in range(4):
                act.wait_ge(st_mm, 12 + p + 1)
                act.activation(gmean[:, p, :], bank[4 + p][:, 0:TS], ACT.Sqrt, bias=epsb[:, 2:3]).then_inc(st_rt, 1)
            act.wait_ge(res_done, 1)
            norm_act(0, 1)

            def peer_act(l):
                q0 = POS["q%d" % l]
                for j in range(16):
                    act.wait_ge(w_used, q0 + j + 1)
                    if j >= 2:
                        act.wait_ge(s_mm, 16 * l + j - 1)
                    act.activation(q_sb[:, j % 2, :], bank[j % 2][:, 0:T], ACT.Copy).then_inc(q_evac, 1)
                    if j >= 1:
                        scores(l, j - 1)
                scores(l, 15)
                act.wait_ge(cand_max, l + 1)
                act.activation(ge, ge, ACT.Exp).then_inc(e_ready, 1)
                for k in range(3):
                    act.wait_ge(route_t, 3 * l + k + 1)
                    act.activation(routeT[:, k, :], bank[4 + k][:, 0:T], ACT.Copy).then_inc(route_e, 1)
                for half in range(NHALF):
                    G0 = (2 * l + half) * (T // 8)
                    if half == 1:
                        act.wait_ge(coef_ready, NK * l + JH + 2)
                    with act.Fori(0, T // 16) as it:
                        for k in range(2):
                            act.wait_ge(tok_mm, it * 16 + ((2 * l + half) * T + 8 * (k + 1) + OHR))
                            dst = gate_m[:, :, bass.ds(it * 16 + 8 * k, 8)].rearrange("p j t -> p t j")
                            act.activation(dst, bank[6 + k][:, :].rearrange("p (t j) -> p t j", j=JH), ACT.Copy)\
                               .then_inc(g_evac, 1)

                    base = POS["e%d" % l] + half * 128
                    Q0 = NK * l + JH * half

                    def gelu(wait_n, q, slot):
                        act.wait_ge(w_used, wait_n)
                        act.wait_ge(coef_ready, q + 1)
                        act.activation(ga[:, slot, :], bank[6 + slot][:, 0:T], ACT.Gelu).then_inc(gelu_done, 1)

                    gelu(base + 1, Q0, 0)
                    with act.Fori(0, 15) as it:
                        for k in range(4):
                            act.wait_ge(w_used, it * 8 + (base + 2 + 2 * k))
                            act.wait_ge(coef_ready, it * 4 + (Q0 + k + 2))
                            sl = (k + 1) % 2
                            act.activation(ga[:, sl, :], bank[6 + sl][:, 0:T], ACT.Gelu).then_inc(gelu_done, 1)
                    for s in range(60, 63):
                        gelu(base + 2 + 2 * s, Q0 + s + 1, (s + 1) % 2)
                act.wait_ge(w_used, POS["e%d" % l] + 256)
                for b in range(3):
                    for hf in range(2):
                        act.activation(otok[:, b, hf * 512:(hf + 1) * 512], bank[2 * b + hf][:, :], ACT.Copy)\
                           .then_inc(out_evac, 1)

            def scores(l, j):
                act.wait_ge(s_mm, 16 * l + j + 1)
                if 16 * l + j >= 2:
                    act.wait_ge(s_free, 16 * l + j - 1)
                act.activation(sc_sb[:, j % 2, :, :], bank[2 + j % 2][:, 0:T].rearrange("p (b k) -> p b k", k=P),
                               ACT.Copy).then_inc(s_evac, 1)

            peer_act(0)
            act.wait_ge(out_used, 16)
            norm_act(1, 0)
            for m in range(8):
                act.wait_ge(w_used, POS["pw1"] + 2 * m + 2)
                if m >= 2:
                    act.wait_ge(glu_done, m - 1)
                act.activation(glug[:, m % 2, :], bank[2 * (m % 2) + 1][:, 0:T], ACT.Sigmoid,
                               bias=sm("b_pw1", 8 + m, 9 + m)).then_inc(glu_g, 1)
            act.wait_ge(glu_done, 8)
            act.activation(zc[:, :, 0, HALO + ROW:ROWP], zc[:, :, 1, HALO:2 * HALO], ACT.Copy).then_inc(halo_done, 1)
            act.activation(zc[:, :, 1, 0:HALO], zc[:, :, 0, ROW:HALO + ROW], ACT.Copy).then_inc(halo_done, 1)
            act.wait_ge(st_in, 6)
            act.activation(acq, accs, ACT.Square).then_inc(act_ready, 1)
            act.wait_ge(st_mm, 18)
            act.activation(lroot, bank[5][:, 0:T], ACT.Sqrt, bias=epsb[:, 1:2]).then_inc(st_rt, 1)
            act.wait_ge(st_in, 7)
            for c in range(DC):
                act.activation(h3[:, c, :], accs[:, c, :], ACT.Silu, scale=sm("lnc_g", c, c + 1),
                               bias=sm("lnc_b", c, c + 1)).then_inc(conv_act, 1)
            for m in range(8):
                act.wait_ge(w_used, POS["pw2"] + m + 1)
                if m >= 2:
                    act.wait_ge(res_done, m)
                act.activation(pw2t[:, m % 2, :], bank[m % 4][:, 0:T], ACT.Identity,
                               bias=sm("b_pw2", m, m + 1)).then_inc(pw2_ev, 1)
            act.wait_ge(res_done, 9)
            norm_act(1, 1)
            peer_act(1)
            act.wait_ge(out_used, 32)
            norm_act(0, 2)

        @block.tensor
        def _(pe):
            norm_n = [0]

            def landed(n):
                pe.wait_ge(w_land[n % RING], 16 * (n // RING + 1))

            def wt(n, c):
                o = (n % RING) * D + c * P
                return ring[:, o:o + P]

            def norm_pe():
                u = norm_n[0]
                norm_n[0] += 1
                pe.wait_ge(sq_ready, u + 1)
                for c in range(DC):
                    mm = pe.matmul(bank[0][:, 0:T], sm("mean_d"), sq3[:, c, :], start=(c == 0), stop=(c == DC - 1))
                mm.then_inc(ss_ready, 1)

            def linear(n, out, rhs):
                landed(n)
                for c in range(DC):
                    mm = pe.matmul(out, wt(n, c), rhs[c], start=(c == 0), stop=(c == DC - 1))
                mm.then_inc(w_used, 1)

            hs = [h3[:, c, :] for c in range(DC)]
            pe.sem_inc(tok_mm, OHR)
            pe.wait_ge(silc_ready, 1)
            sil = silc[:, :].rearrange("p (c g) -> p c g", g=2)
            for n in range(96):
                linear(n, bank[1][:, 2 * n:2 * n + 2], [sil[:, c, :] for c in range(DC)])
            norm_pe()
            pe.wait_ge(h_ready, 8)
            for m in range(IN_CH):
                if m >= 4:
                    pe.wait_ge(z_evac, m - 3)
                linear(POS["in"] + m, bank[m % 4][:, 0:T], hs)
            pe.wait_ge(z_evac, IN_CH)
            for g in range(4):
                pe.matmul(bank[g][:, 0:T], sm("mean_p"), gv[:, g, :], start=True, stop=True).then_inc(st_mm, 1)
            for g in range(4):
                pe.wait_ge(act_ready, g + 1)
                pe.matmul(bank[4 + g][:, 0:T], sm("mean_p"), gs[:, g, :], start=True, stop=True).then_inc(st_mm, 1)
            for g in range(4):
                pe.wait_ge(gm_norm, g + 1)
                for b in range(3):
                    mm = pe.transpose(bank[g][:, b * P:(b + 1) * P], gc[:, g, b * P:(b + 1) * P], sm("ident"))
                mm.then_inc(gm_t, 1)
            for g in range(4):
                pe.wait_ge(gm_te, g + 1)
                for b in range(3):
                    out = bank[4 + g][:, b * P:(b + 1) * P]
                    pe.matmul(out, gtok[:, g * T + b * P:g * T + (b + 1) * P], sm("w_sT", g * P, (g + 1) * P),
                              start=True, stop=False)
                    mm = pe.matmul(out, sm("ones")[0:1], sm("b_s", g * P, (g + 1) * P)[0:1], start=False,
                                   stop=True)
                mm.then_inc(gm_mm, 1)
            pe.wait_ge(act_ready, 7)
            pe.wait_ge(gm_ev, 4)
            for p in range(4):
                pe.matmul(bank[p][:, 0:TS], sm("head_sum"), tmp2[:, p, :], start=True, stop=True).then_inc(kk_ss, 1)

            def H(hp):
                return slice(hp * 64, hp * 64 + 64)

            for d in range(2):
                q = slice(d * 64, d * 64 + 64)
                if d == 0:
                    pe.wait_ge(kk_rt, 4)
                else:
                    pe.wait_ge(rw_evA, RW_EV[RW_AT[(0, "U", 3)]][1])
                    pe.wait_ge(rw_evV, RW_EV[RW_AT[(0, "Y", 3)]][1])
                for p in range(4):
                    pe.matmul(bank[p][:, 0:TS], sm("w2", p * P, (p + 1) * P)[q], th[q], start=True, stop=True)\
                      .then_inc(lw_mm, 1)
                    pe.matmul(bank[4 + p][:, 0:TS], sm("a2", p * P, (p + 1) * P)[q], zs[q, 13, :], start=True,
                              stop=True).then_inc(lw_mm, 1)
                pe.wait_ge(lw_ev, 8 * d + 8)
                pe.wait_ge(sc_ready, d + 1)
                eye = sm("eye64")
                for j, (dd, name, g, e) in enumerate(RW_JOBS):
                    if dd != d:
                        continue
                    if j >= 8:
                        who, cnt = RW_EV[j - 8]
                        pe.wait_ge(rw_evA if who == "A" else rw_evV, cnt)
                    ps = bank[j % 8]

                    def unit(a, w, hp):
                        return a[H(hp), g * 512 + w * 64:g * 512 + w * 64 + 64]

                    def tok(a, w, hp):
                        c0 = tcol(2 * g + w // 4)
                        return a[H(hp), w % 4, c0:c0 + 64]

                    if name in ("X", "U", "S", "Y"):
                        s = g
                        for ci, (chain, c) in enumerate(SCAN[d][s]):
                            which = 0 if chain == "lat" else 1
                            g3, w0 = c // 2, (c % 2) * 4
                            for p in range(4):
                                w = w0 + p
                                c0 = tcol(c)
                                col = (ci * 4 + p) * 64
                                for hp in range(2):
                                    hh = H(hp)
                                    out = ps[hh, col:col + 64]
                                    so = (which * 2 + s % 2) * 256 + p * 64
                                    s_in = state[hh, so:so + 64]

                                    def un(a):
                                        return a[hh, g3 * 512 + w * 64:g3 * 512 + w * 64 + 64]

                                    if name == "X":
                                        if p == 0 and hp == 0 and ci == 0:
                                            pe.wait_ge(rw_evA, RW_EV[RW_AT[(d, "KTOK", 2)]][1])
                                            if s > 0:
                                                pe.wait_ge(rw_evV, RW_EV[RW_AT[(d, "S", s - 1)]][1])
                                        pe.matmul(out, at_[hh, p, c0:c0 + 64], s_in, start=True, stop=False)
                                        mm = pe.matmul(out, un(lak), un(vtok), start=False, stop=True)
                                    elif name == "U":
                                        if p == 0 and hp == 0 and ci == 0:
                                            pe.wait_ge(rw_evA, RW_EV[RW_AT[(d, "X", s)]][1])
                                        mm = pe.matmul(out, un(dT), xs_[hh, col:col + 64], start=True, stop=True)
                                    elif name == "S":
                                        if p == 0 and hp == 0 and ci == 0:
                                            pe.wait_ge(rw_evA, RW_EV[RW_AT[(d, "U", s)]][1])
                                        pe.matmul(out, eye[hh], s_in, start=True, stop=False)
                                        pe.matmul(out, un(btok), us_[hh, col:col + 64], start=False, stop=False)
                                        mm = pe.matmul(out, un(ktok), un(vtok), start=False, stop=True)
                                    else:
                                        pe.matmul(out, s_in, rt_[hh, p, c0:c0 + 64], start=True, stop=False)
                                        pe.matmul(out, us_[hh, col:col + 64], un(mrb), start=False, stop=False)
                                        mm = pe.matmul(out, un(vtok), un(mrk), start=False, stop=True)
                        mm.then_inc(rw_mm, 1)
                        continue
                    if name == "D0":
                        pe.wait_ge(lt_ready, 18 * d + g + 1)
                    if name[0] == "F":
                        lev = LEVELS.index(int(name[1:]))
                        pe.wait_ge(lt_ready, 18 * d + 3 * (lev + 1) + g + 1)
                    if name[0] == "G":
                        n = name.lstrip("GT")
                        pe.wait_ge(rw_evA, RW_EV[RW_AT[(d, "F" + n, g)]][1])
                    if name in ("BTOK", "KTOK"):
                        pe.wait_ge(rw_evV, RW_EV[RW_AT[(d, "GT32", 2)]][1])
                    for w in range(8):
                        for hp in range(2):
                            out = ps[H(hp), w * 64:w * 64 + 64]
                            if name == "LT":
                                a, b = tok(bt_, w, hp), tok(at_, w, hp)
                            elif name == "LAK":
                                a, b = tok(kt_, w, hp), tok(at_, w, hp)
                            elif name == "MRB":
                                a, b = tok(bt_, w, hp), tok(rt_, w, hp)
                            elif name == "MRK":
                                a, b = tok(kt_, w, hp), tok(rt_, w, hp)
                            elif name == "VTOK":
                                a, b = zs[H(hp), 8 + w % 4, tcol(2 * g + w // 4):tcol(2 * g + w // 4) + 64], eye[H(hp)]
                            elif name == "BTOK":
                                a, b = tok(bt_, w, hp), eye[H(hp)]
                            elif name == "KTOK":
                                a, b = tok(kt_, w, hp), eye[H(hp)]
                            elif name == "D0":
                                a, b = unit(em, w, hp), eye[H(hp)]
                            elif name[0] == "F":
                                a, b = unit(em, w, hp), unit(dm, w, hp)
                            elif name[:2] == "GT":
                                a, b = unit(fm, w, hp), unit(dT, w, hp)
                            else:
                                a, b = unit(dT, w, hp), unit(fm, w, hp)
                            mm = pe.matmul(out, a, b, start=True, stop=True)
                    mm.then_inc(rw_mm, 1)
            pe.wait_ge(rw_evV, RW_EV[RW_AT[(1, "Y", 3)]][1])
            pe.wait_ge(rw_evA, RW_EV[RW_AT[(1, "U", 3)]][1])
            for p in range(4):
                pe.matmul(bank[p][:, 0:TS], sm("head_mean"), ysum[:, p, :], start=True, stop=True).then_inc(st_mm, 1)
            pe.wait_ge(act_ready, 8)
            for p in range(4):
                pe.matmul(bank[4 + p][:, 0:TS], sm("head_mean"), gq[:, p, :], start=True, stop=True)\
                  .then_inc(st_mm, 1)
            pe.wait_ge(sc_ready, 3)
            for p in range(4):
                pe.matmul(bank[p][:, 0:TS], sm("head_sum"), tmp0[:, p, :], start=True, stop=True).then_inc(kk_ss, 1)
            pe.wait_ge(st_rt, 8)
            for p in range(4):
                pe.matmul(bank[4 + p][:, 0:TS], sm("g2", p * P, (p + 1) * P), sg, start=True, stop=True)\
                  .then_inc(kk_ss, 1)
            pe.wait_ge(mix_ready, 1)
            ys = [ya3[:, c * T:(c + 1) * T] for c in range(4)] + [yb[:, c, :] for c in range(4)]
            for m in range(8):
                linear(POS["out"] + m, bank[m][:, 0:T], ys)
            pe.wait_ge(res_done, 1)
            norm_pe()

            def peer_pe(l):
                q0 = POS["q%d" % l]

                def score(j):
                    c = j % 2
                    pe.wait_ge(q_evac, 16 * l + j + 1)
                    if 16 * l + j >= 2:
                        pe.wait_ge(s_evac, 16 * l + j - 1)
                    for b in range(3):
                        mm = pe.matmul(bank[2 + j % 2][:, b * P:(b + 1) * P], q_sb[:, j % 2, b * P:(b + 1) * P],
                                       sm("sk", (2 * l + c) * P, (2 * l + c + 1) * P), start=True, stop=True)
                    mm.then_inc(s_mm, 1)

                for j in range(16):
                    if j >= 2:
                        pe.wait_ge(q_evac, 16 * l + j - 1)
                    linear(q0 + j, bank[j % 2][:, 0:T], hs)
                    if j >= 1:
                        score(j - 1)
                score(15)
                pe.wait_ge(route, l + 1)
                for k in range(3):
                    for b in range(3):
                        mm = pe.transpose(bank[4 + k][:, b * P:(b + 1) * P], routes[:, k, b, :], sm("ident"))
                    mm.then_inc(route_t, 1)
                pe.wait_ge(route_e, 3 * l + 3)
                for b in range(6):
                    pe.matmul(bank[b][:, :], sm("zeros"), x_sb[:, 0:512], start=True, stop=True)
                for half in range(NHALF):
                    H0 = 2 * l + half
                    if half == 1:
                        pe.wait_ge(gelu_done, NK * l + JH + 2)
                    with pe.Fori(0, T // 16) as it:
                        for k in range(16):
                            if k % 8 == 0:
                                pe.wait_ge(g_evac, it * 2 + (H0 * (T // 8) + k // 8 + 1))
                            pe.wait_ge(oh_ready, it * 32 + (H0 * 2 * T + 2 * (k + 1)))
                            sl = k % OHR
                            pe.matmul(bank[6 + k // 8][:, (k % 8) * JH:(k % 8 + 1) * JH], oh_i[:, sl, :],
                                      oh_j[:, sl, :], start=True, stop=True).then_inc(tok_mm, 1)
                    base = POS["e%d" % l] + half * 128
                    Q0 = NK * l + JH * half

                    def up(n, q, slot, wl=None):
                        for c in range(DC):
                            mm = pe.matmul(bank[6 + slot][:, 0:T], wt(n, c), hs[c], start=(c == 0),
                                           stop=(c == DC - 1))
                        mm.then_inc(w_used, 1)

                    def down(n, slot):
                        for b in range(3):
                            for hf in range(2):
                                o = (n % RING) * D + hf * 512
                                mm = pe.matmul(bank[2 * b + hf][:, :], coef[:, slot, b * P:(b + 1) * P],
                                               ring[:, o:o + 512], start=False, stop=True, skip_group_check=True)
                        mm.then_inc(w_used, 1)

                    pe.wait_ge(g_evac, (H0 + 1) * (T // 8) + 2)
                    landed(base)
                    up(base, Q0, 0)
                    with pe.Fori(0, 15) as it:
                        for k in range(4):
                            n = base + 1 + 2 * k
                            pe.wait_ge(w_land[n % RING], it * 16 + 16 * (n // RING + 1))
                            pe.wait_ge(gelu_done, it * 4 + (Q0 + k + 2))
                            up(n, 0, (k + 1) % 2)
                            n += 1
                            pe.wait_ge(w_land[n % RING], it * 16 + 16 * (n // RING + 1))
                            pe.wait_ge(coef_ready, it * 4 + (Q0 + k + 3))
                            down(n, k % 2)
                    n = base + 121
                    for s in range(60, 63):
                        landed(n)
                        pe.wait_ge(gelu_done, Q0 + s + 2)
                        up(n, 0, (s + 1) % 2)
                        landed(n + 1)
                        pe.wait_ge(coef_ready, Q0 + s + 3)
                        down(n + 1, s % 2)
                        n += 2
                    landed(n)
                    pe.wait_ge(coef_ready, Q0 + JH + 2)
                    down(n, 1)
                pe.wait_ge(out_evac, 6 * l + 6)
                for c in range(DC):
                    if c >= 2:
                        pe.wait_ge(out_used, 16 * l + 2 * c - 2)
                    for b in range(3):
                        mm = pe.transpose(bank[6 + c % 2][:, b * P:(b + 1) * P], otok[:, b, c * P:(c + 1) * P],
                                          sm("ident"))
                    mm.then_inc(out_t, 1)

            pe.wait_ge(h_ready, 16)
            peer_pe(0)
            pe.wait_ge(out_used, 16)
            norm_pe()
            pe.wait_ge(h_ready, 24)
            for m in range(8):
                for w in range(2):
                    if m >= 2:
                        pe.wait_ge(glu_done, m - 1)
                    linear(POS["pw1"] + 2 * m + w, bank[2 * (m % 2) + w][:, 0:T], hs)
            pe.wait_ge(conv_done, 1)
            for c in range(DC):
                mm = pe.matmul(bank[4][:, 0:T], sm("mean_d"), acc[:, c, :], start=(c == 0), stop=(c == DC - 1))
            mm.then_inc(st_mm, 1)
            pe.wait_ge(act_ready, 9)
            for c in range(DC):
                mm = pe.matmul(bank[5][:, 0:T], sm("mean_d"), acq[:, c, :], start=(c == 0), stop=(c == DC - 1))
            mm.then_inc(st_mm, 1)
            pe.wait_ge(conv_act, 8)
            for m in range(8):
                if m >= 4:
                    pe.wait_ge(pw2_ev, m - 3)
                linear(POS["pw2"] + m, bank[m % 4][:, 0:T], hs)
            pe.wait_ge(res_done, 9)
            norm_pe()
            pe.wait_ge(h_ready, 32)
            peer_pe(1)
            pe.wait_ge(out_used, 32)
            norm_pe()

        @block.vector
        def _(dve):
            st = Steps(dve, v_step)
            norm_n = [0]
            dve.sem_inc(coef_ready, 2)

            def bc(ap, shape):
                return ap.to_broadcast(shape)

            def norm_dve(final=False):
                u = norm_n[0]
                norm_n[0] += 1
                dve.wait_ge(rt_ready, u + 1)
                st.link(dve.reciprocal(rstd, root))
                ins = dve.tensor_tensor(sq3, x3, rstd.unsqueeze(1).to_broadcast([P, DC, T]), ALU.mult)
                if not final:
                    ins.then_inc(xn_ready, 1)
                    return
                st.link(ins)
                dve.tensor_tensor(h3, sq3, sm("norm_f").unsqueeze(2).to_broadcast([P, DC, T]), ALU.mult)\
                   .then_inc(y_ready, 1)

            dve.wait_ge(w_used, 96)
            st.link(dve.tensor_tensor(modv[:, :].rearrange("p (c g) -> p c g", g=2),
                                      bank[1][:, 0:192].rearrange("p (c g) -> p c g", g=2),
                                      sm("b_mod").unsqueeze(2).to_broadcast([P, 96, 2]), ALU.add))
            for l in range(2):
                for n in range(2):
                    ins = dve.scalar_tensor_tensor(
                        scale5[:, l, n], mod4[:, l, 24 * n + 8:24 * n + 16], 1.0,
                        sm("norm%d" % (n + 1), 8 * l, 8 * l + 8).unsqueeze(2).to_broadcast([P, 8, 2]),
                        ALU.add, ALU.mult)
                    if (l, n) != (0, 0):
                        ins.then_inc(mod_ready, 1)
            norm_dve()

            dve.wait_ge(pool_init, 3)
            for m in range(A_CH):
                dve.wait_ge(z_evac, m + 1)
                t = zshift[:, m % 2, :]
                z = zp[:, m, 1:1 + TS]
                st.link(dve.tensor_tensor(t, zp[:, m, 0:TS], zp[:, m, 2:2 + TS], ALU.add))
                st.link(dve.scalar_tensor_tensor(t, t, 0.5, z, ALU.mult, ALU.subtract))
                dve.scalar_tensor_tensor(zs[:, m, :], t, sm("mu", m, m + 1), z, ALU.mult, ALU.add)\
                   .then_inc(zs_ready, 1)

            for g in range(4):
                dve.wait_ge(st_mm, g + 1)
                dve.tensor_tensor(gc[:, g, :], gv[:, g, :], bank[g][:, 0:T], ALU.subtract).then_inc(st_in, 1)
            for g in range(4):
                dve.wait_ge(st_rt, g + 1)
                st.link(dve.reciprocal(gs[:, g, :], gs[:, g, :]))
                st.link(dve.tensor_tensor(gc[:, g, :], gc[:, g, :], gs[:, g, :], ALU.mult))
                dve.tensor_scalar(gc[:, g, :], gc[:, g, :], sm("lnv_g", g, g + 1), sm("lnv_b", g, g + 1),
                                  ALU.mult, ALU.add).then_inc(gm_norm, 1)
            for g in range(4):
                dve.wait_ge(gm_mm, g + 1)
                dve.tensor_tensor(yb[:, g, :], gu[:, g, :], bank[4 + g][:, 0:T], ALU.mult).then_inc(gm_ev, 1)

            dve.wait_ge(zs_ready, A_CH)
            for p in range(4):
                ins = dve.tensor_scalar(nkk[:, p, :], zs[:, 4 + p, :], sm("k_k", p, p + 1), None, ALU.mult)
            ins.then_inc(kk_sq, 1)
            dve.wait_ge(kk_rt, 4)
            st.link(dve.tensor_scalar(tmp1, tmp1, 1e-12, None, ALU.max))
            st.link(dve.reciprocal(tmp1, tmp1))
            dve.scalar_tensor_tensor(nkk, nkk, -1.0, tmp1, ALU.mult, ALU.mult).then_inc(lw_sum, 1)
            dve.memset(ysum[:, :, T_CTX:LAT0], 0.0)

            for d in range(2):
                dve.wait_ge(lw_ev, 8 * d + 8)
                step = 1 if d == 0 else -1
                for p in range(4):
                    ins = dve.tensor_tensor_scan(tmp3[:, p, ::step], sm("keep", d * TS, (d + 1) * TS)[:, ::step],
                                                 tmp1[:, p, ::step], 0.0, ALU.mult, ALU.add)
                ins.then_inc(lw_sum, 1)
                dve.wait_ge(lw_sum, 2 * d + 2)
                dve.tensor_tensor(tmp1, tmp3, tmp1, ALU.subtract).then_inc(lw_sum, 1)
                st.mark(dve.scalar_tensor_tensor(bt_, nkk, -1.0, tmp2, ALU.mult, ALU.mult))
                st.settle()
                for p in range(4):
                    st.mark(dve.tensor_scalar(tmp2[:, p, :], tmp2[:, p, :], -1.0, sm("k_a", p, p + 1),
                                              ALU.add, ALU.mult))
                st.settle()
                st.link(dve.scalar_tensor_tensor(tmp2, tmp2, 1.0, zs[:, 4:8, :], ALU.add, ALU.mult))
                if d == 0:
                    st.link(dve.tensor_copy(kdsum, tmp2))
                else:
                    st.link(dve.tensor_tensor(kdsum, kdsum, tmp2, ALU.add))
                st4 = state.rearrange("p (w s x) -> p w s x", w=2, s=2)
                st.mark(dve.tensor_copy(st4[:, 0, 0, :], sm("s0", d * 256, d * 256 + 256)))
                st.mark(dve.memset(st4[:, 1, 0, :], 0.0))
                dve.wait_ge(ex_ready, 3 * d + 3)
                off = CHUNK - 1 if d == 0 else 0
                pC3 = pC.rearrange("p (c q) -> p c q", q=4)
                st.mark(dve.tensor_copy(pC3[:, 0:2, :], rt_[:, :, off:T_CTX:CHUNK].rearrange("p q c -> p c q")))
                st.mark(dve.tensor_copy(pC3[:, 2:6, :], rt_[:, :, LAT0 + off:TS:CHUNK].rearrange("p q c -> p c q")))
                st.mark(dve.tensor_tensor(bt_, bt_, kt_, ALU.mult))
                st.settle()
                dve.tensor_tensor(rt_, rt_, zs[:, 0:4, :], ALU.mult)
                dve.tensor_tensor(kt_, kt_, tmp2, ALU.mult)
                dve.tensor_tensor(at_, at_, nkk, ALU.mult).then_inc(sc_ready, 1)

                strict = sm("strict", 64 * d, 64 * d + 64).unsqueeze(1).to_broadcast([P, 8, 64])
                incl = sm("incl", 64 * d, 64 * d + 64).unsqueeze(1).to_broadcast([P, 8, 64])
                eye = sm("eye64").unsqueeze(1).to_broadcast([P, 8, 64])

                def band(lev):
                    o = (d * 6 + lev) * 64
                    return sm("bands", o, o + 64).unsqueeze(1).to_broadcast([P, 8, 64])

                for j, (dd, name, g, e) in enumerate(RW_JOBS):
                    if dd != d or e != "V":
                        continue
                    dve.wait_ge(rw_mm, j + 1)
                    ps = bank[j % 8]
                    ps3 = ps[:, :].rearrange("p (w t) -> p w t", t=64)

                    def grp(a):
                        return a[:, g * 512:(g + 1) * 512].rearrange("p (w t) -> p w t", t=64)

                    if name == "LT":
                        dve.tensor_tensor(grp(ltm), ps3, strict, ALU.mult).then_inc(rw_evV, 1)
                        dve.wait_ge(rw_evV, RW_EV[j][1])
                        dve.tensor_tensor(grp(em), grp(ltm), band(0), ALU.mult).then_inc(lt_ready, 1)
                    elif name == "LAK":
                        dve.tensor_tensor(grp(lak), ps3, strict, ALU.mult).then_inc(rw_evV, 1)
                    elif name == "MRB":
                        dve.tensor_tensor(grp(mrb), ps3, incl, ALU.mult).then_inc(rw_evV, 1)
                    elif name == "MRK":
                        dve.tensor_tensor(grp(mrk), ps3, incl, ALU.mult).then_inc(rw_evV, 1)
                    elif name == "D0":
                        dve.wait_ge(lt_ready, 18 * d + g + 1)
                        st.mark(dve.tensor_tensor(grp(dm), ps3, eye, ALU.add))
                        dve.tensor_tensor(grp(dT), grp(em), eye, ALU.add).then_inc(rw_evV, 1)
                        dve.wait_ge(rw_evV, RW_EV[j][1])
                        dve.tensor_tensor(grp(em), grp(ltm), band(1), ALU.mult).then_inc(lt_ready, 1)
                    elif name[:2] == "GT":
                        lev = LEVELS.index(int(name[2:]))
                        dve.tensor_tensor(grp(dT), grp(dT), ps3, ALU.add).then_inc(rw_evV, 1)
                        if lev + 1 < len(LEVELS):
                            dve.tensor_tensor(grp(em), grp(ltm), band(lev + 2), ALU.mult).then_inc(lt_ready, 1)
                    elif name[0] == "G":
                        dve.tensor_tensor(grp(dm), grp(dm), ps3, ALU.add).then_inc(rw_evV, 1)
                    elif name == "S":
                        s = g
                        n = len(SCAN[d][s])
                        for ci, (chain, c) in enumerate(SCAN[d][s]):
                            which = 0 if chain == "lat" else 1
                            if chain == "ctx" and s == 1:
                                dst = sm("s0", d * 256, d * 256 + 256)
                            else:
                                dst = st4[:, which, (s + 1) % 2, :]
                            ins = dve.tensor_tensor(
                                dst.rearrange("p (q i) -> p q i", i=HEAD),
                                ps[:, ci * 256:(ci + 1) * 256].rearrange("p (q i) -> p q i", i=HEAD),
                                pC3[:, c, :].unsqueeze(2).to_broadcast([P, 4, HEAD]), ALU.mult)
                            if ci < n - 1:
                                st.mark(ins)
                        ins.then_inc(rw_evV, 1)
                    else:
                        s = g
                        n = len(SCAN[d][s])
                        for ci, (chain, c) in enumerate(SCAN[d][s]):
                            c0 = tcol(c)
                            y = ysum[:, :, c0:c0 + 64]
                            yp = ps[:, ci * 256:(ci + 1) * 256].rearrange("p (q t) -> p q t", t=64)
                            if d == 0:
                                ins = dve.tensor_copy(y, yp)
                            else:
                                ins = dve.tensor_tensor(y, y, yp, ALU.add)
                            if ci < n - 1:
                                st.mark(ins)
                        ins.then_inc(rw_evV, 1)

            dve.wait_ge(rw_evV, RW_EV[RW_AT[(1, "Y", 3)]][1])
            st.settle()
            st.link(dve.tensor_tensor(tmp0, kdsum, zs[:, 0:4, :], ALU.mult))
            for p in range(4):
                ins = dve.tensor_scalar(tmp0[:, p, :], tmp0[:, p, :], sm("r_k", p, p + 1), None, ALU.mult)
            ins.then_inc(sc_ready, 1)
            for p in range(4):
                dve.wait_ge(st_mm, 8 + p + 1)
                ins = dve.tensor_tensor(gy[:, p, :], ysum[:, p, :], bank[p][:, 0:TS], ALU.subtract)
            ins.then_inc(st_in, 1)
            dve.wait_ge(st_in, 5)
            dve.wait_ge(st_rt, 8)
            st.link(dve.reciprocal(gmean, gmean))
            st.link(dve.tensor_tensor(gy, gy, gmean, ALU.mult))
            for p in range(4):
                st.mark(dve.tensor_scalar(gy[:, p, :], gy[:, p, :], sm("lnx_g", p, p + 1), sm("lnx_b", p, p + 1),
                                          ALU.mult, ALU.add))
            for p in range(4):
                dve.wait_ge(kk_ss, 4 + p + 1)
                st.mark(dve.tensor_tensor(rt_[:, p, :], zs[:, 8 + p, :], bank[p][:, 0:TS], ALU.mult))
            st.settle()
            st.link(dve.tensor_tensor(gy, gy, rt_, ALU.add))
            for p in range(4):
                dve.wait_ge(kk_ss, 8 + p + 1)
                for t0, c0, n in SEG:
                    ins = dve.tensor_tensor(ya3[:, p * T + t0:p * T + t0 + n], gy[:, p, c0:c0 + n],
                                            bank[4 + p][:, c0:c0 + n], ALU.mult)
            ins.then_inc(mix_ready, 1)

            def residual(l, gate, c, src, done):
                for g, (a, b) in enumerate(GROUPS):
                    ins = dve.scalar_tensor_tensor(x3[:, c, a:b], src[:, a:b], mod4[:, l, gate + c, g:g + 1],
                                                   x3[:, c, a:b], ALU.mult, ALU.add)
                    if done is not None:
                        ins.then_inc(done, 1)
                return ins

            for m in range(8):
                dve.wait_ge(w_used, POS["out"] + m + 1)
                ins = residual(0, 16, m, bank[m], None)
            ins.then_inc(res_done, 1)
            dve.wait_ge(res_done, 1)
            norm_dve()

            def top16(rows, vals, idxs, tmps, free=None):
                for r, v in zip(rows, vals):
                    st.mark(dve.max(v[:, 0:8], r))
                st.settle()
                for r, v, i, t in zip(rows, vals, idxs, tmps):
                    st.mark(dve.max_index(i[:, 0:8], v[:, 0:8], r))
                    st.mark(dve.match_replace(t, v[:, 0:8], r, LOWEST))
                st.settle()
                for n, (v, t) in enumerate(zip(vals, tmps)):
                    ins = dve.max(v[:, 8:16], t)
                    if n == 0 and free is not None:
                        ins.then_inc(free, 1)
                        dve.wait_ge(free, free_n[0])
                    else:
                        st.mark(ins)
                st.settle()
                for v, i, t in zip(vals, idxs, tmps):
                    st.mark(dve.max_index(i[:, 8:16], v[:, 8:16], t))

            free_n = [0]

            def peer_dve(l):
                for j in range(16):
                    dve.wait_ge(s_evac, 16 * l + j + 1)
                    free_n[0] += 1
                    top16([sc_sb[:, j % 2, b, :] for b in range(3)], [sv[:, b, j, :] for b in range(3)],
                          [si[:, b, j, :] for b in range(3)], [stmp[:, j % 2, b, :] for b in range(3)], s_free)
                st.settle()
                st.mark(dve.tensor_copy(sif, si))
                sv5 = sv.rearrange("p b (h c) k -> p b h c k", c=2)
                sif5 = sif.rearrange("p b (h c) k -> p b h c k", c=2)
                for b in range(3):
                    st.mark(dve.tensor_tensor(
                        cand[:, b].rearrange("p h (a k) -> p h a k", a=16),
                        sv5[:, b, :, 0, :].unsqueeze(3).to_broadcast([P, 8, 16, 16]),
                        sv5[:, b, :, 1, :].unsqueeze(2).to_broadcast([P, 8, 16, 16]), ALU.add))
                st.settle()
                for b in range(3):
                    top16([cand[:, b, h, :] for h in range(8)], [fv[:, b, h, :] for h in range(8)],
                          [fi[:, b, h, :] for h in range(8)], [ctmp[:, h, :] for h in range(8)])
                    st.settle()
                dve.tensor_tensor(ge, fv, fv[:, :, :, 0:1].to_broadcast([P, 3, 8, 16]), ALU.subtract)\
                   .then_inc(cand_max, 1)
                st.mark(dve.tensor_scalar(fa_u, fi, 4, None, ALU.logical_shift_right))
                st.mark(dve.tensor_scalar(fb_u, fi, 15, None, ALU.bitwise_and))
                st.settle()
                st.mark(dve.tensor_copy(fa, fa_u))
                st.mark(dve.tensor_copy(fb, fb_u))
                dve.wait_ge(e_ready, l + 1)
                st.link(dve.tensor_reduce(gsum, ge, AX, ALU.add))
                st.link(dve.reciprocal(gsum, gsum))
                st.mark(dve.tensor_tensor(routes[:, 2].rearrange("p b (h k) -> p b h k", k=16), ge,
                                          gsum.to_broadcast([P, 3, 8, 16]), ALU.mult))
                shape = [P, 8, 16, 16]
                pos = sm("iota", 0, 16).unsqueeze(1).unsqueeze(1).to_broadcast(shape)
                for b in range(3):
                    for oh, f, c in ((oh1, fa, 0), (oh2, fb, 1)):
                        st.mark(dve.tensor_tensor(oh, pos, f[:, b].unsqueeze(3).to_broadcast(shape), ALU.is_equal))
                    st.settle()
                    for oh, c in ((oh1, 0), (oh2, 1)):
                        st.mark(dve.tensor_tensor(oh, oh, sif5[:, b, :, c, :].unsqueeze(2).to_broadcast(shape),
                                                  ALU.mult))
                    st.settle()
                    for oh, c in ((oh1, 0), (oh2, 1)):
                        st.mark(dve.tensor_reduce(routes[:, c, b].rearrange("p (h k) -> p h k", k=16), oh, AX,
                                                  ALU.add))
                    st.settle()
                dve.tensor_copy(gsum, gsum).then_inc(route, 1)
                dve.wait_ge(route_e, 3 * l + 3)
                for half in range(NHALF):
                    N0 = (2 * l + half) * T
                    with dve.Fori(0, T // 16) as it:
                        for k in range(16):
                            sl = k % OHR
                            dve.wait_ge(tok_mm, it * 16 + (N0 + k + 1))
                            rt = [routeT[:, x, bass.ds(it * 16 + k, 1)] for x in range(3)]
                            dve.tensor_scalar(oh_i[:, sl, :], sm("iota"), rt[0], None, ALU.is_equal)\
                               .then_inc(oh_ready, 1)
                            dve.tensor_scalar(oh_j[:, sl, :], sm("iota", half * JH, (half + 1) * JH), rt[1], rt[2],
                                              ALU.is_equal, ALU.mult).then_inc(oh_ready, 1)
                    base = POS["e%d" % l] + half * 128
                    Q0 = NK * l + JH * half
                    with dve.Fori(0, JH // 2) as it:
                        for k in range(2):
                            dve.wait_ge(gelu_done, it * 2 + (Q0 + k + 3))
                            dve.wait_ge(w_used, it * 4 + (base + 2 * k - 1))
                            g = gate_m[:, bass.ds(it * 2 + k, 1), :].rearrange("p o t -> p (o t)")
                            dve.tensor_tensor(coef[:, k, :], ga[:, k, :], g, ALU.mult).then_inc(coef_ready, 1)
                for c in range(DC):
                    dve.wait_ge(out_t, 8 * l + c + 1)
                    residual(l, 40, c, bank[6 + c % 2], out_used)

            peer_dve(0)
            dve.wait_ge(out_used, 16)
            norm_dve()
            dve.wait_ge(pool_init, 7)
            for m in range(8):
                dve.wait_ge(glu_g, m + 1)
                dve.scalar_tensor_tensor(
                    zc[:, m, :, HALO:HALO + ROW], bank[2 * (m % 2)][:, 0:T].rearrange("p (r t) -> p r t", t=ROW),
                    sm("b_pw1", m, m + 1), glug[:, m % 2, :].rearrange("p (r t) -> p r t", t=ROW),
                    ALU.add, ALU.mult).then_inc(glu_done, 1)
            dve.wait_ge(halo_done, 2)
            dve.wait_ge(glu_done, 8)

            def row(a, m):
                return a[:, m, :].rearrange("p (r t) -> p r t", t=ROW)

            for m in range(8):
                dve.tensor_scalar(row(acc, m), zc[:, m, :, 0:ROW], sm("conv_k", m, m + 1), sm("conv_b", m, m + 1),
                                  ALU.mult, ALU.add).then_inc(conv_tap, 1)
            with dve.Fori(0, CONV_W - 1) as it:
                for m in range(8):
                    dve.wait_ge(conv_tap, it * 8 + (m + 1))
                    k0 = SM["conv_k"][0]
                    dve.scalar_tensor_tensor(row(acc, m), zc[:, m, :, bass.ds(it + 1, ROW)],
                                             small[:, bass.ds(it * 8 + (k0 + 8 + m), 1)], row(acc, m),
                                             ALU.mult, ALU.add).then_inc(conv_tap, 1)
            dve.wait_ge(conv_tap, 8 * CONV_W)
            dve.tensor_copy(gsum, gsum).then_inc(conv_done, 1)
            dve.wait_ge(st_mm, 17)
            dve.tensor_tensor(accs, acc, bank[4][:, 0:T].unsqueeze(1).to_broadcast([P, DC, T]), ALU.subtract)\
               .then_inc(st_in, 1)
            dve.wait_ge(st_in, 6)
            dve.wait_ge(st_rt, 9)
            st.link(dve.reciprocal(lrstd, lroot))
            dve.tensor_tensor(accs, accs, lrstd.unsqueeze(1).to_broadcast([P, DC, T]), ALU.mult).then_inc(st_in, 1)
            for m in range(8):
                dve.wait_ge(pw2_ev, m + 1)
                residual(1, 16, m, pw2t[:, m % 2, :], None).then_inc(res_done, 1)
            dve.wait_ge(res_done, 9)
            norm_dve()
            peer_dve(1)
            dve.wait_ge(out_used, 32)
            norm_dve(final=True)


def _constants():
    c = {}
    c["ident"] = np.eye(P)
    c["mean_d"] = np.full((P, P), 1.0 / D)
    c["mean_p"] = np.full((P, P), 1.0 / P)
    blk = (np.arange(P)[:, None] // HEAD == np.arange(P)[None, :] // HEAD) * 1.0
    c["head_sum"] = blk
    c["head_mean"] = blk / HEAD
    c["iota"] = np.tile(np.arange(P), (P, 1))
    s = (np.arange(P) % CHUNK)[:, None]
    t = np.arange(CHUNK)[None, :]
    c["strict"] = np.concatenate([s < t, s > t], 1)
    c["incl"] = np.concatenate([s <= t, s >= t], 1)
    bands = []
    for d in range(2):
        lo, hi = (s, t) if d == 0 else (t, s)
        for n in (1, 2, 4, 8, 16, 32):
            bands.append((lo // (2 * n) == hi // (2 * n)) & (lo // n % 2 == 0) & (hi // n % 2 == 1))
    c["bands"] = np.concatenate(bands, 1)
    c["eye64"] = (s == t)
    keep = np.ones((2, TS))
    for ch in range(NCH):
        keep[0, tcol(ch)] = 0
        keep[1, tcol(ch) + CHUNK - 1] = 0
    keep[:, T_CTX] = 0
    c["keep"] = np.tile(keep.reshape(1, -1), (P, 1))
    c["zeros"] = np.zeros((P, P))
    c["ones"] = np.ones((P, P))
    return {k: np.asarray(v, np.float32) for k, v in c.items()}


def _cols(v):
    return v.reshape(-1, P).T


def _tiles(w):
    n = w.shape[1] // P
    return w.reshape(DC, P, n, P).transpose(2, 1, 0, 3).reshape(n, P, D)


def kernel(**inputs):
    import concourse.bacc as _bacc
    from concourse.bass_utils import run_bass_kernel_spmd as _run

    a = {k: np.asarray(v) for k, v in inputs.items()}
    sm = _constants()
    cc = np.concatenate
    sm["b_mod"] = cc([_cols(a["b_mod"][l]) for l in range(2)], 1)
    sm["norm1"] = cc([_cols(a["norm1"][l]) for l in range(2)], 1)
    sm["norm2"] = cc([_cols(a["norm2"][l]) for l in range(2)], 1)
    sm["norm_f"] = _cols(a["norm_f"])
    sm["mu"] = _cols(a["mu_a"][0])
    sm["w0"] = cc([_cols(a["w0"][0, d]) for d in range(2)], 1)
    sm["a0"] = cc([_cols(a["a0"][0, d]) for d in range(2)], 1)
    for k in ("k_k", "k_a", "r_k", "lnx_g", "lnx_b", "lnv_g", "lnv_b", "b_pw1", "conv_b", "lnc_g", "lnc_b", "b_pw2"):
        sm[k] = _cols(a[k][0])
    sm["conv_k"] = cc([_cols(a["conv_k"][0, w]) for w in range(CONV_W)], 1)
    sm["w2"] = a["w2"][0].reshape(P, A_W)
    sm["a2"] = a["a2"][0].reshape(P, A_W)
    sm["g2"] = a["g2"][0]
    sm["w_sT"] = a["w_s"][0].transpose(2, 0, 1).reshape(P, 4 * P)
    b_s = np.zeros((P, 4 * P), np.float32)
    b_s[0] = a["b_s"][0].reshape(-1)
    sm["b_s"] = b_s
    sm["sk"] = a["sub_keys"].transpose(3, 0, 1, 2).reshape(P, 4 * P)
    sm["s0"] = a["state_rwkv"][0, 0].reshape(2, NP_, 2, HEAD, HEAD).transpose(2, 4, 0, 1, 3).reshape(P, 2 * NP_ * HEAD)
    cv = cc([a["c_ctx"].reshape(1, D), a["c"].reshape(1, D)], 0)
    sm["cvec"] = cv.reshape(2, DC, P).transpose(2, 1, 0).reshape(P, 16)
    for k, n in SMALL:
        assert sm[k].shape == (P, n), (k, sm[k].shape, n)
    small = np.ascontiguousarray(cc([sm[k] for k, _ in SMALL], 1))
    pw1 = _tiles(a["w_pw1"][0])
    pw1 = pw1.reshape(2, 8, P, D).transpose(1, 0, 2, 3).reshape(16, P, D)
    w = cc([_tiles(a["w_mod"][0]), _tiles(a["w_mod"][1]), _tiles(a["w_in_ab"][0]), _tiles(a["w_out_ab"][0]),
            _tiles(a["w_query"][0]), pw1, _tiles(a["w_pw2"][0]), _tiles(a["w_query"][1])], 0)
    e_u = np.ascontiguousarray(a["expert_u"].reshape(2, NK, NK, DC, P).transpose(0, 2, 4, 3, 1)).reshape(2, NK, P, D)
    x_t = np.ascontiguousarray(cc([a["x_prompt"][0], a["x_sample"][0]], 0).T)
    arrays = {"x_t": x_t, "small": small, "w_tiles": w, "e_u": e_u,
              "e_v": a["expert_v"].reshape(2, NK, NK, D)}

    nc = _bacc.Bacc("TRN2", target_bir_lowering=False, num_devices=1)
    ap = {k: nc.dram_tensor("in_" + k, v.shape, F32, kind="ExternalInput").ap() for k, v in arrays.items()}
    y_t = nc.dram_tensor("y_t", (D, T), F32, kind="ExternalOutput").ap()
    s_new = nc.dram_tensor("s_new", (2, NP_, P, HEAD), F32, kind="ExternalOutput").ap()
    build_trunk(nc, ap["x_t"], ap["small"], ap["w_tiles"], ap["e_u"],
                ap["e_v"].rearrange("l i j d -> l j i d"), y_t, s_new)
    r = _run(nc, [{"in_" + k: v for k, v in arrays.items()}], core_ids=[0]).results[0]
    y = r["y_t"].T
    s = r["s_new"].reshape(2, NP_, 2, HEAD, HEAD).transpose(0, 1, 2, 4, 3).reshape(1, 1, 2, 8, HEAD, HEAD)
    return (np.ascontiguousarray(y[None, :T_CTX]), np.ascontiguousarray(y[None, T_CTX:]), np.ascontiguousarray(s))
```

```python
from contextlib import ExitStack

import numpy as np

import concourse.bass as bass
from concourse import mybir

P = 128
D = 1024
DC = D // P
T_CTX, T_LAT = 128, 256
T = T_CTX + T_LAT
TB = T // P
GROUPS = ((0, T_CTX), (T_CTX, T))
A_W = 512
HEAD = 64
NP_ = A_W // P
A_CH = 15
IN_CH = 23
CHUNK = 64
NCH = T // CHUNK
TS = T + 1
LAT0 = T_CTX + 1
CONV_W, HALO = 31, 15
ROW = 64
NROW = T // ROW
ROWP = ROW + 2 * HALO
HEADS, TOPK, NK = 8, 16, 128
RING = 4
SPLIT = 4
QT = 4
JQ = NK // QT
GRP = T // JQ
SEQ_TILES = 16 + NK * 2

ALU = mybir.AluOpType
ACT = mybir.ActivationFunctionType
AX = mybir.AxisListType.X
F32 = mybir.dt.float32
F32R = mybir.dt.float32r
BF16 = mybir.dt.bfloat16
U32 = mybir.dt.uint32

EPS, LN_EPS, GN_EPS = 1e-6, 1e-5, 64e-5
DECAY = float(np.exp(-0.5))
LOWEST = -3.4e38


SMALL = [
    ("ident", 128), ("mean_d", 128), ("iota", 128), ("zeros", 128), ("b_mod", 96), ("norm1", 16), ("norm2", 16),
    ("norm_f", 8), ("b_pw1", 16), ("conv_k", 8 * CONV_W), ("conv_b", 8), ("lnc_g", 8), ("lnc_b", 8), ("b_pw2", 8),
    ("sk", 2 * 2 * P), ("cvec", 16),
]
MIXER = [
    ("mean_p", 128), ("head_sum", 128), ("head_mean", 128), ("strict", 128), ("incl", 128), ("bands", 12 * 64),
    ("eye64", 64), ("keep", 2 * TS), ("ones", 128), ("mu", 15), ("w0", 8), ("a0", 8), ("k_k", 4), ("k_a", 4),
    ("r_k", 4), ("lnx_g", 4), ("lnx_b", 4), ("lnv_g", 4), ("lnv_b", 4), ("w2", A_W), ("a2", A_W), ("g2", A_W),
    ("w_sT", 4 * P), ("b_s", 4 * P),
    ("s0", 2 * NP_ * HEAD),
]


def offsets(entries):
    at, out = 0, {}
    for name, n in entries:
        out[name] = (at, n)
        at += n
    return out, at


SM, NSMALL = offsets(SMALL)
MX, NMIXER = offsets(MIXER)


POS = {"mod": 0, "in": 96, "out": 119, "peer0": 127}
POS["pw1"] = POS["peer0"] + SEQ_TILES
POS["pw2"] = POS["pw1"] + 16
POS["peer1"] = POS["pw2"] + 8
N_DENSE0 = POS["peer0"]


START = [("q", j) for j in range(16)] + [("u", j) for j in range(JQ)]
T_MOD, T_IN, T_OUT, T_Q0, T_PW1, T_PW2, T_Q1 = 0, 96, 119, 127, 143, 159, 167
N_START = len(START)
PHASES = (
    (N_START, 1, None, 0),
    (N_START + JQ, 2, 0, 1),
    (N_START + 3 * JQ, 3, 1, 2),
    (N_START + 5 * JQ, None, 2, 3),
    (N_START + 6 * JQ, None, 3, None),
)


def val(i, a, b):
    return i * a + b


class Steps:

    def __init__(self, eng, sem):
        self.eng, self.sem, self.n = eng, sem, 0

    def mark(self, ins):
        self.n += 1
        ins.then_inc(self.sem, 1)

    def settle(self):
        self.eng.wait_ge(self.sem, self.n)

    def link(self, ins):
        self.mark(ins)
        self.settle()


def tcol(c):
    return c * CHUNK + (1 if c * CHUNK >= T_CTX else 0)


SEG = ((0, 0, T_CTX), (T_CTX, LAT0, T_LAT))

SCAN = (
    ((("lat", 2), ("ctx", 0)), (("lat", 3), ("ctx", 1)), (("lat", 4),), (("lat", 5),)),
    ((("lat", 5), ("ctx", 1)), (("lat", 4), ("ctx", 0)), (("lat", 3),), (("lat", 2),)),
)
LEVELS = (2, 4, 8, 16, 32)


def pair_jobs(d):
    jobs = [("LT", "V"), ("LAK", "V"), ("MRB", "V"), ("MRK", "V")]
    if d == 0:
        jobs.append(("VTOK", "A"))
    jobs.append(("D0", "V"))
    for n in LEVELS:
        jobs.append(("F%d" % n, "A"))
        if n != LEVELS[-1]:
            jobs.append(("G%d" % n, "V"))
        jobs.append(("GT%d" % n, "V"))
    jobs += [("BTOK", "A"), ("KTOK", "A")]
    return [(name, g, e) for name, e in jobs for g in range(3)]


def scan_jobs(d):
    out = []
    for s in range(4):
        out += [("X", s, "A"), ("U", s, "A"), ("S", s, "V"), ("Y", s, "V")]
    return out


RW_JOBS = []
for _d in range(2):
    RW_JOBS += [(_d,) + j for j in pair_jobs(_d)] + [(_d,) + j for j in scan_jobs(_d)]
RW_AT = {j[:3]: i for i, j in enumerate(RW_JOBS)}
RW_EV = []
_c = {"A": 0, "V": 0}
for _j in RW_JOBS:
    _c[_j[3]] += 1
    RW_EV.append((_j[3], _c[_j[3]]))


def build_trunk(nc, x_t, small_d, mixer_d, w_tiles, e_u, e_v, y_t, s_new, dbg=None):
    ctx = ExitStack()
    with ctx:
        def sb(name, cols, dt=F32):
            return ctx.enter_context(nc.sbuf_tensor(name, [P, cols], dt))

        def sem(name):
            return ctx.enter_context(nc.semaphore(name))

        x_sb = sb("x_sb", DC * T)
        x3 = x_sb[:, :].rearrange("p (c t) -> p c t", t=T)
        ring = sb("ring", RING * D)
        small = sb("small", NSMALL)
        modv = sb("modv", 192)
        scale = sb("scale", 2 * 2 * 16)
        silc = sb("silc", 16)
        epsb = sb("epsb", 4)
        ARENA = 31500
        with ExitStack() as mixers:
            h_sb = mixers.enter_context(nc.sbuf_tensor("h_sb", [P, DC * T + 4], F32))
            smallm = mixers.enter_context(nc.sbuf_tensor("smallm", [P, NMIXER], F32))
            arena = mixers.enter_context(nc.sbuf_tensor("arena", [P, ARENA], F32))
        h3 = h_sb[:, 0:DC * T].rearrange("p (c t) -> p c t", t=T)
        split = sb("split", SPLIT * 2 * D, F32R)
        h_parts = sb("h_parts", 2 * DC * T, F32R)
        hp4 = h_parts[:, :].rearrange("p (x c t) -> p x c t", x=2, t=T)
        coef_parts = sb("coef_parts", 2 * 2 * T, F32R)
        cp4 = coef_parts[:, :].rearrange("p (s x t) -> p s x t", s=2, t=T)
        routes_t = sb("routes_t", 2 * T)
        gate_t = sb("gate_t", 3 * T, BF16)
        hot_i = sb("hot_i", 2 * GRP * P, BF16)
        hot_j = sb("hot_j", GRP * JQ, BF16)
        hot_g = sb("hot_g", GRP * 3 * JQ, BF16)
        QW = JQ * T
        gated = sb("gated", 2 * QW)
        bank = [ctx.enter_context(nc.psum_tensor("bank%d" % i, [P, 512], F32)) for i in range(8)]

        def sm(name, a=0, b=None):
            buf, at = (small, SM) if name in SM else (smallm, MX)
            o, n = at[name]
            return buf[:, o + a:o + (n if b is None else b)]

        def ar(o, n):
            assert o + n <= ARENA, (o, n)
            return arena[:, o:o + n]

        mod4 = modv[:, :].rearrange("p (l c g) -> p l c g", l=2, g=2)
        scale5 = scale[:, :].rearrange("p (l n c g) -> p l n c g", l=2, n=2, g=2)

        s_x = sem("x_landed")
        s_small = sem("small_landed")
        w_land = [sem("w_landed%d" % i) for i in range(RING)]
        dense_used = sem("dense_tile_used")
        tile_used = sem("split_tile_used")
        hi_ready = sem("tile_rounded")
        lo_ready = sem("tile_rest_ready")
        s_mixer = sem("mixer_consts_landed")
        row_ready = sem("mod_rows_evacuated")
        row_mm = sem("mod_rows_transposed")
        hi_h = sem("h_rounded")
        lo_h = sem("h_rest_ready")
        chi = sem("coef_rounded")
        clo = sem("coef_rest_ready")
        mult_done = sem("group_gated")
        s_out = sem("stores_landed")
        pool_init = sem("pool_init")
        a_step = sem("act_step")
        v_step = sem("dve_step")
        g_step = sem("pool_step")
        silc_ready = sem("silc_ready")
        mod_evac = sem("mod_evacuated")
        mod_ready = sem("mod_ready")
        sq_ready = sem("squares_ready")
        ss_ready = sem("mean_square_ready")
        rt_ready = sem("root_ready")
        xn_ready = sem("x_normed")
        h_ready = sem("h_ready")
        z_evac = sem("z_evacuated")
        zs_ready = sem("z_shifted")
        act_ready = sem("act_readyputs_ready")
        kk_sq = sem("kk_squares")
        kk_ss = sem("kk_sums")
        kk_rt = sem("kk_roots")
        lw_mm = sem("lora_products")
        lw_ev = sem("lora_evacuated")
        lw_sum = sem("log_decay_summed")
        ex_ready = sem("exps_ready")
        sc_ready = sem("scaled_ready")
        rw_mm = sem("rwkv_job_product")
        rw_evA = sem("rwkv_job_evac_act")
        rw_evV = sem("rwkv_job_evac_dve")
        bands_used = sem("bands_done")
        lt_ready = sem("lt_ready")
        st_in = sem("stat_inputs")
        st_mm = sem("stat_products")
        st_rt = sem("stat_roots")
        gm_t = sem("gmlp_transposed")
        gm_te = sem("gmlp_transposed_evac")
        gm_mm = sem("gmlp_mixed")
        gm_ev = sem("gmlp_mixed_evac")
        mix_ready = sem("mixer_input_ready")
        conv_act = sem("conv_activated")
        gm_norm = sem("gmlp_normed")
        out_used = sem("expert_out_added")
        res_done = sem("residual_added")
        glu_g = sem("glu_gate_ready")
        glu_done = sem("glu_done")
        conv_done = sem("conv_done")
        conv_tap = sem("conv_taps_added")
        halo_done = sem("halo_done")
        pw2_ev = sem("pw2_evacuated")
        q_evac = sem("q_evacuated")
        s_mm = sem("scores_product")
        s_evac = sem("scores_evacuated")
        s_free = sem("scores_used")
        cand_max = sem("cand_max")
        e_ready = sem("gate_exp_ready")
        route = sem("routes_ready")
        route_t = sem("routes_transposed")
        route_e = sem("routes_evacuated")
        oh_ready = sem("one_hots_ready")
        col_ready = sem("one_hot_columns_ready")
        tok_mm = sem("token_gate_product")
        g_evac = sem("gate_matrix_evacuated")
        gelu_done = sem("gelu_done")
        coef_ready = sem("coef_ready")
        out_evac = sem("expert_out_evacuated")
        out_t = sem("expert_out_transposed")
        y_ready = sem("y_ready")

        sq3 = ar(0, 3072).rearrange("p (c t) -> p c t", t=T)
        root = ar(3072, T)
        rstd = ar(3072 + T, T)

        o = 0
        ZS = o
        zs = ar(o, A_CH * TS).rearrange("p (c t) -> p c t", t=TS); o += A_CH * TS
        ZP = o
        zp = ar(o, A_CH * (TS + 2)).rearrange("p (c t) -> p c t", t=TS + 2)
        GM = ZP + A_CH * (TS + 2)
        gu = ar(GM, 4 * T).rearrange("p (c t) -> p c t", t=T)
        gv = ar(GM + 1536, 4 * T).rearrange("p (c t) -> p c t", t=T)
        gc = ar(GM + 3072, 4 * T).rearrange("p (c t) -> p c t", t=T)
        gs = ar(GM + 4608, 4 * T).rearrange("p (c t) -> p c t", t=T)
        gtok = ar(GM + 6144, 12 * P)
        yb = h_sb[:, 1540:1540 + 4 * T].rearrange("p (c t) -> p c t", t=T)
        kdsum = h_sb[:, 0:1540].rearrange("p (c t) -> p c t", t=TS)
        zshift = ar(GM + 7680, 2 * TS).rearrange("p (c t) -> p c t", t=TS)
        o = ZP

        def take(n):
            nonlocal o
            r = ar(o, n)
            o += n
            return r

        def c4(a):
            return a.rearrange("p (c t) -> p c t", t=TS)

        at_, bt_, kt_, rt_ = (c4(take(1540)) for _ in range(4))
        lak, mrb, mrk, dT, vtok = (take(1536) for _ in range(5))
        lt_o = o
        ltm, dm, fm, em = (take(1536) for _ in range(4))
        btok, ktok = ltm, fm
        xs_, us_ = ar(lt_o + 1536, 512), ar(lt_o + 1536 + 512, 512)
        tmp1, tmp2, tmp3 = (c4(ar(lt_o + i * 1540, 1540)) for i in range(3))
        ysum = c4(take(1540))
        nkk = c4(take(1540))
        tmp0 = c4(take(1540))
        state = take(2 * 2 * 256)
        pC = take(24)
        th = zs[:, 12, :]
        sg = zs[:, 14, :]
        gy = at_
        gq = bt_
        gmean = kt_
        ya3 = ar(ZP + 1540, 4 * T)
        zc = ar(0, DC * NROW * ROWP).rearrange("p (c r t) -> p c r t", c=DC, t=ROWP)
        CO = DC * NROW * ROWP
        acc = ar(CO, DC * T).rearrange("p (c t) -> p c t", t=T)
        acq = ar(CO + 3072, DC * T).rearrange("p (c t) -> p c t", t=T)
        accs = ar(CO + 6144, DC * T).rearrange("p (c t) -> p c t", t=T)
        mean_sb = ar(CO + 9216, T)
        lroot = ar(CO + 9216 + T, T)
        lrstd = ar(CO + 9216 + 2 * T, T)
        glug = ar(CO + 9216 + 3 * T, 2 * T).rearrange("p (c t) -> p c t", t=T)
        pw2t = ar(CO + 9216 + 5 * T, 2 * T).rearrange("p (c t) -> p c t", t=T)
        buf4 = gated[:, :].rearrange("p (w j t) -> p w j t", w=2, t=T)
        oh_i = hot_i[:, :].rearrange("p (s t i) -> p s t i", s=2, i=P)
        oh_j = hot_j[:, :].rearrange("p (t j) -> p t j", j=JQ)
        oh_g = hot_g[:, :].rearrange("p (t y j) -> p t y j", t=GRP, y=3)
        routeT = routes_t[:, :].rearrange("p (k t) -> p k t", t=T)
        gateT = gate_t[:, :].rearrange("p (y t) -> p y t", t=T)
        gate_rest = hot_i[:, 0:2 * T].bitcast(F32)
        psq = gated[:, 0:3072].rearrange("p (c t) -> p c t", t=T)
        ph = gated[:, 3072:6144].rearrange("p (c t) -> p c t", t=T)
        proot = gated[:, 6144:6144 + T]
        prstd = gated[:, 6144 + T:6144 + 2 * T]
        otok = gated[:, 0:3072].rearrange("p (b c) -> p b c", b=3)
        o = QW

        def take(n):
            nonlocal o
            r = gated[:, o:o + n]
            o += n
            assert o <= 2 * QW
            return r

        sv = take(3 * 256).rearrange("p (b j k) -> p b j k", b=3, k=16)
        si = take(3 * 256).bitcast(U32).rearrange("p (b j k) -> p b j k", b=3, k=16)
        sif = take(3 * 256).rearrange("p (b j k) -> p b j k", b=3, k=16)
        both = take(4096)
        q_sb = both[:, 0:2 * T].rearrange("p (s t) -> p s t", t=T)
        sc_sb = both[:, 2 * T:4 * T].rearrange("p (s b k) -> p s b k", s=2, k=P)
        stmp = both[:, 4 * T:6 * T] if 6 * T <= 4096 else None
        stmp = stmp.rearrange("p (s b k) -> p s b k", s=2, k=P)
        cand = both[:, 0:2048].rearrange("p (h k) -> p h k", k=256)
        ctmp = both[:, 2048:4096].rearrange("p (h k) -> p h k", k=256)
        oh1 = both[:, 0:2048].rearrange("p (h k a) -> p h k a", h=8, a=16)
        oh2 = both[:, 2048:4096].rearrange("p (h k a) -> p h k a", h=8, a=16)
        fv = take(T).rearrange("p (b h k) -> p b h k", b=3, k=16)
        fi = take(T).bitcast(U32).rearrange("p (b h k) -> p b h k", b=3, k=16)
        fa_u = take(T).bitcast(U32).rearrange("p (b h k) -> p b h k", b=3, k=16)
        fb_u = take(T).bitcast(U32).rearrange("p (b h k) -> p b h k", b=3, k=16)
        fa = take(T).rearrange("p (b h k) -> p b h k", b=3, k=16)
        fb = take(T).rearrange("p (b h k) -> p b h k", b=3, k=16)
        ge = take(T).rearrange("p (b h k) -> p b h k", b=3, k=16)
        gsum = take(24).rearrange("p (b h k) -> p b h k", b=3, k=1)
        routes = take(3 * T).rearrange("p (k b x) -> p k b x", k=3, b=3)
        mrow = arena[0:2, ZS:ZS + 2 * D]

        def norm_bufs(which):
            return (sq3, h3, root, rstd) if which == 0 else (psq, ph, proot, prstd)

        block = ctx.enter_context(nc.Block())

        @block.sync
        def _(sp):
            def put(n, src, free, count):
                if free is not None:
                    sp.wait_ge(free, count)
                sl = n % RING
                sp.dma_start(ring[:, sl * D:(sl + 1) * D], src).then_inc(w_land[sl], 16)

            def load(n, src):
                m = n - RING
                if m < 0:
                    put(n, src, None, 0)
                elif m < N_DENSE0:
                    put(n, src, dense_used, m + 1)
                elif m < POS["pw1"]:
                    put(n, src, lo_ready, m - N_DENSE0 + 1)
                elif m < POS["peer1"]:
                    put(n, src, dense_used, N_DENSE0 + m - POS["pw1"] + 1)
                else:
                    put(n, src, lo_ready, SEQ_TILES + m - POS["peer1"] + 1)

            def experts(l, wq):
                base = POS["peer%d" % l]
                E0 = SEQ_TILES * l
                for k, (kind, j) in enumerate(START):
                    load(base + k, w_tiles[wq + j] if kind == "q" else e_u[l, j])
                for first, uq, vq, _ in PHASES:
                    kinds = [(e_u, uq)] * (uq is not None) + [(e_v, vq)] * (vq is not None)
                    steps = 4 // len(kinds)
                    with sp.Fori(0, JQ // steps) as it:
                        for k in range(4):
                            src, q = kinds[k % len(kinds)]
                            j = val(it, steps, q * JQ + k // len(kinds))
                            put(base + first + k, src[l, bass.ds(j, 1), :, :].rearrange("o i d -> (o i) d"),
                                lo_ready, val(it, 4, E0 + first + k - RING + 1))

            sp.dma_start(small[:, :], small_d).then_inc(s_small, 16)
            for n in range(4):
                load(n, w_tiles[n])
            sp.dma_start(x3, x_t.rearrange("(c p) t -> p c t", p=P)).then_inc(s_x, 16)
            sp.dma_start(smallm[:, :], mixer_d).then_inc(s_mixer, 16)
            for n in range(4, N_DENSE0):
                load(n, w_tiles[n])
            sp.wait_ge(rw_evV, RW_EV[RW_AT[(1, "S", 1)]][1])
            for d in range(2):
                sp.dma_start(s_new[d].rearrange("q p i -> p q i"), sm("s0", d * 256, (d + 1) * 256)
                             .rearrange("p (q i) -> p q i", i=HEAD)).then_inc(s_out, 16)
            experts(0, T_Q0)
            for n in range(POS["pw1"], POS["peer1"]):
                load(n, w_tiles[n - POS["pw1"] + T_PW1])
            experts(1, T_Q1)
            sp.wait_ge(y_ready, 1)
            sp.dma_start(y_t.rearrange("(c p) t -> p c t", p=P), ph).then_inc(s_out, 16)
            nst = 3
            if dbg is not None:
                sp.dma_start(dbg, arena[:, :]).then_inc(s_out, 16)
                nst = 4
            sp.wait_ge(s_out, 16 * nst)

        @block.gpsimd
        def _(pool):
            pool.memset(zp[:, :, 0:1], 0.0).then_inc(pool_init, 1)
            pool.memset(zp[:, :, T_CTX + 1:T_CTX + 2], 0.0).then_inc(pool_init, 1)
            pool.memset(zp[:, :, TS + 1:TS + 2], 0.0).then_inc(pool_init, 1)
            pool.memset(epsb[:, 0:1], EPS).then_inc(pool_init, 1)
            pool.memset(epsb[:, 1:2], LN_EPS).then_inc(pool_init, 1)
            pool.memset(epsb[:, 2:3], GN_EPS).then_inc(pool_init, 1)

            def rests(l):
                pool.wait_ge(hi_h, l + 1)
                pool.tensor_tensor(hp4[:, 1], ph, hp4[:, 0].bitcast(F32), ALU.subtract).then_inc(lo_h, 1)
                n0, e0 = POS["peer%d" % l], SEQ_TILES * l
                with pool.Fori(0, SEQ_TILES // 4) as it:
                    for k in range(4):
                        r, p_ = (n0 + k) % RING, (e0 + k) % SPLIT
                        pool.wait_ge(hi_ready, val(it, 4, e0 + k + 1))
                        pool.tensor_tensor(split[:, (2 * p_ + 1) * D:(2 * p_ + 2) * D], ring[:, r * D:(r + 1) * D],
                                           split[:, 2 * p_ * D:(2 * p_ + 1) * D].bitcast(F32), ALU.subtract)\
                            .then_inc(lo_ready, 1)

            rests(0)
            pool.wait_ge(h_ready, 24)
            pool.memset(zc[:, :, :, :], 0.0).then_inc(pool_init, 1)
            rests(1)

        @block.scalar
        def _(act):
            st = Steps(act, a_step)
            norm_n = [0]

            def norm_act(l, which):
                u = norm_n[0]
                norm_n[0] += 1
                sq3, h3, root = norm_bufs(which)[:3]
                act.activation(sq3, x3, ACT.Square).then_inc(sq_ready, 1)
                act.wait_ge(ss_ready, u + 1)
                act.activation(root, bank[0][:, 0:T], ACT.Sqrt, bias=epsb[:, 0:1]).then_inc(rt_ready, 1)
                if which < 2:
                    act.wait_ge(xn_ready, u + 1)
                    for c in range(DC):
                        for g, (a, b) in enumerate(GROUPS):
                            ins = act.activation(h3[:, c, a:b], sq3[:, c, a:b], ACT.Identity,
                                                 scale=scale5[:, l, which, c, g:g + 1],
                                                 bias=mod4[:, l, 24 * which + c, g:g + 1])
                        ins.then_inc(h_ready, 1)

            act.sem_inc(gelu_done, 2)
            act.wait_ge(s_small, 16)
            act.activation(silc[:, :], sm("cvec"), ACT.Silu).then_inc(silc_ready, 1)
            act.wait_ge(s_x, 16)
            act.wait_ge(pool_init, 6)
            for k in range(12):
                act.wait_ge(dense_used, 8 * k + 8)
                if k >= 2:
                    act.wait_ge(row_mm, k - 1)
                for hf in range(2):
                    ins = act.activation(mrow[:, (k % 2) * D + hf * 512:(k % 2) * D + (hf + 1) * 512],
                                         bank[2 * (k % 2) + hf][0:2, :], ACT.Copy)
                ins.then_inc(row_ready, 1)
            act.wait_ge(mod_ready, 3)
            norm_act(0, 0)
            for m in range(IN_CH):
                act.wait_ge(dense_used, POS["in"] + m + 1)
                ps = bank[m % 4]
                if m < A_CH:
                    st.mark(act.activation(zp[:, m, 1:1 + T_CTX], ps[:, 0:T_CTX], ACT.Copy))
                    act.activation(zp[:, m, 1 + LAT0:1 + TS], ps[:, T_CTX:T], ACT.Copy).then_inc(z_evac, 1)
                else:
                    dst = gu[:, m - 15, :] if m < 19 else gv[:, m - 19, :]
                    act.activation(dst, ps[:, 0:T], ACT.Copy).then_inc(z_evac, 1)
            for g in range(4):
                act.wait_ge(st_in, g + 1)
                act.activation(gs[:, g, :], gc[:, g, :], ACT.Square).then_inc(act_ready, 1)
            for g in range(4):
                act.wait_ge(st_mm, 4 + g + 1)
                act.activation(gs[:, g, :], bank[4 + g][:, 0:T], ACT.Sqrt, bias=epsb[:, 1:2]).then_inc(st_rt, 1)
            for g in range(4):
                act.wait_ge(gm_t, g + 1)
                act.activation(gtok[:, g * T:(g + 1) * T], bank[g][:, 0:T], ACT.Copy).then_inc(gm_te, 1)
            act.wait_ge(zs_ready, A_CH)
            act.wait_ge(gm_ev, 4)
            act.activation(th, zs[:, 12, :], ACT.Tanh).then_inc(act_ready, 1)
            act.activation(sg, zs[:, 14, :], ACT.Sigmoid).then_inc(act_ready, 1)
            act.wait_ge(kk_sq, 1)
            act.activation(tmp2, nkk, ACT.Square).then_inc(act_ready, 1)
            for p in range(4):
                act.wait_ge(kk_ss, p + 1)
                act.activation(tmp1[:, p, :], bank[p][:, 0:TS], ACT.Sqrt).then_inc(kk_rt, 1)
            for d in range(2):
                if d == 1:
                    act.wait_ge(rw_mm, RW_AT[(0, "Y", 3)] + 1)
                else:
                    act.wait_ge(lw_sum, 1)
                for p in range(4):
                    act.wait_ge(lw_mm, 8 * d + 2 * p + 1)
                    act.activation(tmp1[:, p, :], bank[p][:, 0:TS], ACT.Sigmoid,
                                   bias=sm("w0", 4 * d + p, 4 * d + p + 1)).then_inc(lw_ev, 1)
                    act.wait_ge(lw_mm, 8 * d + 2 * p + 2)
                    act.activation(tmp2[:, p, :], bank[4 + p][:, 0:TS], ACT.Sigmoid,
                                   bias=sm("a0", 4 * d + p, 4 * d + p + 1)).then_inc(lw_ev, 1)
                act.wait_ge(lw_sum, 2 * d + 2)
                act.activation(rt_, tmp3, ACT.Exp, scale=-DECAY).then_inc(ex_ready, 1)
                act.activation(kt_, tmp3, ACT.Exp, scale=DECAY).then_inc(ex_ready, 1)
                act.wait_ge(lw_sum, 2 * d + 3)
                act.activation(at_, tmp1, ACT.Exp, scale=-DECAY).then_inc(ex_ready, 1)
                for j, (dd, name, g, e) in enumerate(RW_JOBS):
                    if dd != d or e != "A":
                        continue
                    act.wait_ge(rw_mm, j + 1)
                    ps = bank[j % 8]
                    if name == "VTOK":
                        dst = vtok[:, g * 512:(g + 1) * 512]
                    elif name == "BTOK":
                        dst = btok[:, g * 512:(g + 1) * 512]
                    elif name == "KTOK":
                        dst = ktok[:, g * 512:(g + 1) * 512]
                    elif name[0] == "F":
                        dst = fm[:, g * 512:(g + 1) * 512]
                    elif name == "X":
                        dst = xs_[:, :]
                    else:
                        dst = us_[:, :]
                    if name in ("X", "U"):
                        w = 256 * len(SCAN[d][g])
                        act.activation(dst[:, 0:w], ps[:, 0:w], ACT.Copy).then_inc(rw_evA, 1)
                    else:
                        act.activation(dst, ps[:, :], ACT.Copy).then_inc(rw_evA, 1)
            act.wait_ge(st_in, 5)
            act.activation(gq, gy, ACT.Square).then_inc(act_ready, 1)
            for p in range(4):
                act.wait_ge(st_mm, 12 + p + 1)
                act.activation(gmean[:, p, :], bank[4 + p][:, 0:TS], ACT.Sqrt, bias=epsb[:, 2:3]).then_inc(st_rt, 1)
            act.wait_ge(res_done, 1)
            norm_act(0, 1)

            def round_tile(l, e, sem_count=None, it=None):
                n = POS["peer%d" % l] + e
                r, p_ = n % RING, (SEQ_TILES * l + e) % SPLIT
                i = 0 if it is None else it
                act.wait_ge(w_land[r], val(i, 16, 16 * (n // RING + 1)))
                act.wait_ge(tile_used, val(i, 4, SEQ_TILES * l + e + 1))
                act.activation(split[:, 2 * p_ * D:(2 * p_ + 1) * D], ring[:, r * D:(r + 1) * D], ACT.Copy)\
                   .then_inc(hi_ready, 1)

            def peer_act(l):
                E0, U0, V0, M0 = SEQ_TILES * l, NK * l, NK * l, NK * l
                act.wait_ge(h_ready, 16 * l + 16)
                if l == 0:
                    act.wait_ge(s_out, 32)
                act.activation(hp4[:, 0], ph, ACT.Copy).then_inc(hi_h, 1)
                for e in range(SPLIT):
                    round_tile(l, e)
                for e, (kind, j) in enumerate(START):
                    act.wait_ge(tile_used, E0 + e + 1 + SPLIT)
                    if kind == "q":
                        if j >= 2:
                            act.wait_ge(s_mm, 16 * l + j - 1)
                        act.activation(q_sb[:, j % 2, :], bank[j % 2][:, 0:T], ACT.Copy).then_inc(q_evac, 1)
                    else:
                        act.activation(buf4[:, 0, j, :], bank[6 + j % 2][:, 0:T], ACT.Gelu).then_inc(gelu_done, 1)
                    round_tile(l, e + SPLIT)
                    if 1 <= e <= 16:
                        scores(l, e - 1)
                    if e == N_START - 8:
                        act.wait_ge(cand_max, l + 1)
                        act.activation(ge, ge, ACT.Exp).then_inc(e_ready, 1)
                for k in range(3):
                    act.wait_ge(route_t, 3 * l + k + 1)
                    act.activation(routeT[:, k, :] if k < 2 else gateT[:, 0, :], bank[2 + k][:, 0:T], ACT.Copy)\
                           .then_inc(route_e, 1)
                last_e = SEQ_TILES
                for first, uq, vq, gq_ in PHASES:
                    w = 2 if uq is not None and vq is not None else 1
                    steps = 4 // w

                    def coef_hi(i, s):
                        v = val(i, steps, V0 + vq * JQ + s)
                        sl = s % 2
                        act.activation(cp4[:, sl, 0, :],
                                       buf4[:, vq % 2, bass.ds(val(i, steps, s), 1), :].rearrange("p o t -> p (o t)"),
                                       ACT.Copy).then_inc(chi, 1)

                    def body(i, last):
                        for s in range(steps):
                            e = first + w * s
                            if uq is not None:
                                act.wait_ge(tile_used, val(i, 4, E0 + e + 1 + SPLIT))
                                if vq is not None:
                                    act.wait_ge(clo, val(i, steps, V0 + vq * JQ + s + 1))
                                round_tile(l, e + SPLIT, it=i)
                                ub = 6 if vq is not None else (6, 5)[s % 2]
                                act.activation(buf4[:, uq % 2, bass.ds(val(i, steps, s), 1), :]
                                               .rearrange("p o t -> p (o t)"), bank[ub][:, 0:T], ACT.Gelu)\
                                   .then_inc(gelu_done, 1)
                                e += 1
                            if vq is not None:
                                if not (last and s == steps - 1):
                                    coef_hi(i, s + 1)
                                if not (last and vq == QT - 1):
                                    act.wait_ge(tile_used, val(i, 4, E0 + e + 1 + SPLIT))
                                    round_tile(l, e + SPLIT, it=i)
                                else:
                                    act.wait_ge(tile_used, val(i, 4, E0 + e + 1 + SPLIT))

                    if vq is not None:
                        act.wait_ge(mult_done, M0 + (vq + 1) * JQ + 2)
                        coef_hi(0, 0)
                    n = JQ // steps
                    with act.Fori(0, n - 1) as it:
                        body(it, False)
                    body(n - 1, True)
                for b in range(3):
                    for hf in range(2):
                        act.activation(otok[:, b, hf * 512:(hf + 1) * 512], bank[2 * b + hf][:, :], ACT.Copy)\
                           .then_inc(out_evac, 1)

            def scores(l, j):
                act.wait_ge(s_mm, 16 * l + j + 1)
                if 16 * l + j >= 2:
                    act.wait_ge(s_free, 16 * l + j - 1)
                act.activation(sc_sb[:, j % 2, :, :], bank[2 + j % 2][:, 0:T].rearrange("p (b k) -> p b k", k=P),
                               ACT.Copy).then_inc(s_evac, 1)

            peer_act(0)
            act.wait_ge(out_used, 16)
            norm_act(1, 0)
            for m in range(8):
                act.wait_ge(dense_used, N_DENSE0 + 2 * m + 2)
                if m >= 2:
                    act.wait_ge(glu_done, m - 1)
                act.activation(glug[:, m % 2, :], bank[2 * (m % 2) + 1][:, 0:T], ACT.Sigmoid,
                               bias=sm("b_pw1", 8 + m, 9 + m)).then_inc(glu_g, 1)
            act.wait_ge(glu_done, 8)
            act.activation(zc[:, :, 0, HALO + ROW:ROWP], zc[:, :, 1, HALO:2 * HALO], ACT.Copy).then_inc(halo_done, 1)
            act.activation(zc[:, :, 1, 0:HALO], zc[:, :, 0, ROW:HALO + ROW], ACT.Copy).then_inc(halo_done, 1)
            act.wait_ge(st_in, 6)
            act.activation(acq, accs, ACT.Square).then_inc(act_ready, 1)
            act.wait_ge(st_mm, 18)
            act.activation(lroot, bank[5][:, 0:T], ACT.Sqrt, bias=epsb[:, 1:2]).then_inc(st_rt, 1)
            act.wait_ge(st_in, 7)
            for c in range(DC):
                act.activation(h3[:, c, :], accs[:, c, :], ACT.Silu, scale=sm("lnc_g", c, c + 1),
                               bias=sm("lnc_b", c, c + 1)).then_inc(conv_act, 1)
            for m in range(8):
                act.wait_ge(dense_used, N_DENSE0 + 16 + m + 1)
                if m >= 2:
                    act.wait_ge(res_done, m)
                act.activation(pw2t[:, m % 2, :], bank[m % 4][:, 0:T], ACT.Identity,
                               bias=sm("b_pw2", m, m + 1)).then_inc(pw2_ev, 1)
            act.wait_ge(res_done, 9)
            norm_act(1, 1)
            peer_act(1)
            act.wait_ge(out_used, 32)
            norm_act(0, 2)

        @block.tensor
        def _(pe):
            norm_n = [0]

            def landed(n):
                pe.wait_ge(w_land[n % RING], 16 * (n // RING + 1))

            def wt(n, c):
                o = (n % RING) * D + c * P
                return ring[:, o:o + P]

            def norm_pe(which=0):
                sq3 = norm_bufs(which)[0]
                u = norm_n[0]
                norm_n[0] += 1
                pe.wait_ge(sq_ready, u + 1)
                for c in range(DC):
                    mm = pe.matmul(bank[0][:, 0:T], sm("mean_d"), sq3[:, c, :], start=(c == 0), stop=(c == DC - 1))
                mm.then_inc(ss_ready, 1)

            def linear(n, out, rhs):
                landed(n)
                for c in range(DC):
                    mm = pe.matmul(out, wt(n, c), rhs[c], start=(c == 0), stop=(c == DC - 1))
                mm.then_inc(dense_used, 1)

            hs = [h3[:, c, :] for c in range(DC)]
            pe.sem_inc(tok_mm, 2)
            pe.sem_inc(tile_used, SPLIT)
            pe.wait_ge(silc_ready, 1)
            sil = silc[:, :].rearrange("p (c g) -> p c g", g=2)

            def mod_rows(k):
                if k >= 2:
                    pe.wait_ge(row_ready, k - 1)
                for c in range(DC):
                    n = 8 * k + c
                    landed(n)
                    for hf in range(2):
                        o = (n % RING) * D + hf * 512
                        mm = pe.matmul(bank[2 * (k % 2) + hf][0:2, :], sil[:, c, :], ring[:, o:o + 512],
                                       start=(c == 0), stop=(c == DC - 1))
                    mm.then_inc(dense_used, 1)

            def mod_turn(k):
                pe.wait_ge(row_ready, k + 1)
                for c in range(8):
                    o = 2 * (8 * k + c)
                    mm = pe.matmul(bank[7][:, o:o + 2], mrow[:, (k % 2) * D + c * P:(k % 2) * D + (c + 1) * P],
                                   sm("ident", 0, 2)[0:2], start=True, stop=True)
                mm.then_inc(row_mm, 1)

            for k in range(12):
                mod_rows(k)
                if k >= 1:
                    mod_turn(k - 1)
            mod_turn(11)
            norm_pe()
            pe.wait_ge(h_ready, 8)
            for m in range(IN_CH):
                if m >= 4:
                    pe.wait_ge(z_evac, m - 3)
                linear(POS["in"] + m, bank[m % 4][:, 0:T], hs)
            pe.wait_ge(z_evac, IN_CH)
            pe.wait_ge(s_mixer, 16)
            for g in range(4):
                pe.matmul(bank[g][:, 0:T], sm("mean_p"), gv[:, g, :], start=True, stop=True).then_inc(st_mm, 1)
            for g in range(4):
                pe.wait_ge(act_ready, g + 1)
                pe.matmul(bank[4 + g][:, 0:T], sm("mean_p"), gs[:, g, :], start=True, stop=True).then_inc(st_mm, 1)
            for g in range(4):
                pe.wait_ge(gm_norm, g + 1)
                for b in range(3):
                    mm = pe.transpose(bank[g][:, b * P:(b + 1) * P], gc[:, g, b * P:(b + 1) * P], sm("ident"))
                mm.then_inc(gm_t, 1)
            for g in range(4):
                pe.wait_ge(gm_te, g + 1)
                for b in range(3):
                    out = bank[4 + g][:, b * P:(b + 1) * P]
                    pe.matmul(out, gtok[:, g * T + b * P:g * T + (b + 1) * P], sm("w_sT", g * P, (g + 1) * P),
                              start=True, stop=False)
                    mm = pe.matmul(out, sm("ones")[0:1], sm("b_s", g * P, (g + 1) * P)[0:1], start=False,
                                   stop=True)
                mm.then_inc(gm_mm, 1)
            pe.wait_ge(act_ready, 7)
            pe.wait_ge(gm_ev, 4)
            for p in range(4):
                pe.matmul(bank[p][:, 0:TS], sm("head_sum"), tmp2[:, p, :], start=True, stop=True).then_inc(kk_ss, 1)

            def H(hp):
                return slice(hp * 64, hp * 64 + 64)

            for d in range(2):
                q = slice(d * 64, d * 64 + 64)
                if d == 0:
                    pe.wait_ge(kk_rt, 4)
                else:
                    pe.wait_ge(rw_evA, RW_EV[RW_AT[(0, "U", 3)]][1])
                    pe.wait_ge(rw_evV, RW_EV[RW_AT[(0, "Y", 3)]][1])
                for p in range(4):
                    pe.matmul(bank[p][:, 0:TS], sm("w2", p * P, (p + 1) * P)[q], th[q], start=True, stop=True)\
                      .then_inc(lw_mm, 1)
                    pe.matmul(bank[4 + p][:, 0:TS], sm("a2", p * P, (p + 1) * P)[q], zs[q, 13, :], start=True,
                              stop=True).then_inc(lw_mm, 1)
                pe.wait_ge(lw_ev, 8 * d + 8)
                pe.wait_ge(sc_ready, d + 1)
                eye = sm("eye64")
                for j, (dd, name, g, e) in enumerate(RW_JOBS):
                    if dd != d:
                        continue
                    if j >= 8:
                        who, cnt = RW_EV[j - 8]
                        pe.wait_ge(rw_evA if who == "A" else rw_evV, cnt)
                    ps = bank[j % 8]

                    def unit(a, w, hp):
                        return a[H(hp), g * 512 + w * 64:g * 512 + w * 64 + 64]

                    def tok(a, w, hp):
                        c0 = tcol(2 * g + w // 4)
                        return a[H(hp), w % 4, c0:c0 + 64]

                    if name in ("X", "U", "S", "Y"):
                        s = g
                        for ci, (chain, c) in enumerate(SCAN[d][s]):
                            which = 0 if chain == "lat" else 1
                            g3, w0 = c // 2, (c % 2) * 4
                            for p in range(4):
                                w = w0 + p
                                c0 = tcol(c)
                                col = (ci * 4 + p) * 64
                                for hp in range(2):
                                    hh = H(hp)
                                    out = ps[hh, col:col + 64]
                                    so = (which * 2 + s % 2) * 256 + p * 64
                                    s_in = state[hh, so:so + 64]

                                    def un(a):
                                        return a[hh, g3 * 512 + w * 64:g3 * 512 + w * 64 + 64]

                                    if name == "X":
                                        if p == 0 and hp == 0 and ci == 0:
                                            pe.wait_ge(rw_evA, RW_EV[RW_AT[(d, "KTOK", 2)]][1])
                                            if s > 0:
                                                pe.wait_ge(rw_evV, RW_EV[RW_AT[(d, "S", s - 1)]][1])
                                        pe.matmul(out, at_[hh, p, c0:c0 + 64], s_in, start=True, stop=False)
                                        mm = pe.matmul(out, un(lak), un(vtok), start=False, stop=True)
                                    elif name == "U":
                                        if p == 0 and hp == 0 and ci == 0:
                                            pe.wait_ge(rw_evA, RW_EV[RW_AT[(d, "X", s)]][1])
                                        mm = pe.matmul(out, un(dT), xs_[hh, col:col + 64], start=True, stop=True)
                                    elif name == "S":
                                        if p == 0 and hp == 0 and ci == 0:
                                            pe.wait_ge(rw_evA, RW_EV[RW_AT[(d, "U", s)]][1])
                                        pe.matmul(out, eye[hh], s_in, start=True, stop=False)
                                        pe.matmul(out, un(btok), us_[hh, col:col + 64], start=False, stop=False)
                                        mm = pe.matmul(out, un(ktok), un(vtok), start=False, stop=True)
                                    else:
                                        pe.matmul(out, s_in, rt_[hh, p, c0:c0 + 64], start=True, stop=False)
                                        pe.matmul(out, us_[hh, col:col + 64], un(mrb), start=False, stop=False)
                                        mm = pe.matmul(out, un(vtok), un(mrk), start=False, stop=True)
                        mm.then_inc(rw_mm, 1)
                        continue
                    if name == "D0":
                        pe.wait_ge(lt_ready, 18 * d + g + 1)
                    if name[0] == "F":
                        lev = LEVELS.index(int(name[1:]))
                        pe.wait_ge(lt_ready, 18 * d + 3 * (lev + 1) + g + 1)
                    if name[0] == "G":
                        n = name.lstrip("GT")
                        pe.wait_ge(rw_evA, RW_EV[RW_AT[(d, "F" + n, g)]][1])
                    if name in ("BTOK", "KTOK"):
                        pe.wait_ge(rw_evV, RW_EV[RW_AT[(d, "GT32", 2)]][1])
                    for w in range(8):
                        for hp in range(2):
                            out = ps[H(hp), w * 64:w * 64 + 64]
                            if name == "LT":
                                a, b = tok(bt_, w, hp), tok(at_, w, hp)
                            elif name == "LAK":
                                a, b = tok(kt_, w, hp), tok(at_, w, hp)
                            elif name == "MRB":
                                a, b = tok(bt_, w, hp), tok(rt_, w, hp)
                            elif name == "MRK":
                                a, b = tok(kt_, w, hp), tok(rt_, w, hp)
                            elif name == "VTOK":
                                a, b = zs[H(hp), 8 + w % 4, tcol(2 * g + w // 4):tcol(2 * g + w // 4) + 64], eye[H(hp)]
                            elif name == "BTOK":
                                a, b = tok(bt_, w, hp), eye[H(hp)]
                            elif name == "KTOK":
                                a, b = tok(kt_, w, hp), eye[H(hp)]
                            elif name == "D0":
                                a, b = unit(em, w, hp), eye[H(hp)]
                            elif name[0] == "F":
                                a, b = unit(em, w, hp), unit(dm, w, hp)
                            elif name[:2] == "GT":
                                a, b = unit(fm, w, hp), unit(dT, w, hp)
                            else:
                                a, b = unit(dT, w, hp), unit(fm, w, hp)
                            mm = pe.matmul(out, a, b, start=True, stop=True)
                    mm.then_inc(rw_mm, 1)
            pe.wait_ge(rw_evV, RW_EV[RW_AT[(1, "Y", 3)]][1])
            pe.wait_ge(rw_evA, RW_EV[RW_AT[(1, "U", 3)]][1])
            for p in range(4):
                pe.matmul(bank[p][:, 0:TS], sm("head_mean"), ysum[:, p, :], start=True, stop=True).then_inc(st_mm, 1)
            pe.wait_ge(act_ready, 8)
            for p in range(4):
                pe.matmul(bank[4 + p][:, 0:TS], sm("head_mean"), gq[:, p, :], start=True, stop=True)\
                  .then_inc(st_mm, 1)
            pe.wait_ge(sc_ready, 3)
            for p in range(4):
                pe.matmul(bank[p][:, 0:TS], sm("head_sum"), tmp0[:, p, :], start=True, stop=True).then_inc(kk_ss, 1)
            pe.wait_ge(st_rt, 8)
            for p in range(4):
                pe.matmul(bank[4 + p][:, 0:TS], sm("g2", p * P, (p + 1) * P), sg, start=True, stop=True)\
                  .then_inc(kk_ss, 1)
            pe.wait_ge(mix_ready, 1)
            ys = [ya3[:, c * T:(c + 1) * T] for c in range(4)] + [yb[:, c, :] for c in range(4)]
            for m in range(8):
                linear(POS["out"] + m, bank[m][:, 0:T], ys)
            pe.wait_ge(res_done, 1)
            norm_pe(1)

            def peer_pe(l):
                E0, U0, V0, M0 = SEQ_TILES * l, NK * l, NK * l, NK * l

                def part(e, x, a, b):
                    o = (2 * ((E0 + e) % SPLIT) + x) * D
                    return split[:, o + a:o + b]

                def product(e, out, chunks):
                    for c in chunks:
                        for x, y in ((0, 0), (0, 1), (1, 0)):
                            mm = pe.matmul(out, part(e, x, c * P, (c + 1) * P), hp4[:, y, c, :],
                                           start=(c == 0 and x == 0 and y == 0), stop=(c == DC - 1 and x == 1))
                    return mm

                def score(j):
                    c = j % 2
                    pe.wait_ge(q_evac, 16 * l + j + 1)
                    if 16 * l + j >= 2:
                        pe.wait_ge(s_evac, 16 * l + j - 1)
                    for b in range(3):
                        mm = pe.matmul(bank[2 + j % 2][:, b * P:(b + 1) * P], q_sb[:, j % 2, b * P:(b + 1) * P],
                                       sm("sk", (2 * l + c) * P, (2 * l + c + 1) * P), start=True, stop=True)
                    mm.then_inc(s_mm, 1)

                pe.wait_ge(lo_h, l + 1)
                for e, (kind, j) in enumerate(START):
                    pe.wait_ge(lo_ready, E0 + e + 1)
                    if kind == "q":
                        if j >= 2:
                            pe.wait_ge(q_evac, 16 * l + j - 1)
                        product(e, bank[j % 2][:, 0:T], range(DC)).then_inc(tile_used, 1)
                    else:
                        pe.wait_ge(gelu_done, U0 + j + 1)
                        product(e, bank[6 + j % 2][:, 0:T], range(DC)).then_inc(tile_used, 1)
                    if 1 <= e <= 16:
                        score(e - 1)
                pe.wait_ge(route, 7 * l + 7)
                for k in range(3):
                    for b in range(3):
                        mm = pe.transpose(bank[2 + k][:, b * P:(b + 1) * P], routes[:, k, b, :], sm("ident"))
                    mm.then_inc(route_t, 1)

                for first, uq, vq, gq_ in PHASES:
                    w = 2 if uq is not None and vq is not None else 1
                    steps = 4 // w
                    if vq == 0:
                        pe.wait_ge(gelu_done, U0 + 2 * JQ + 2)
                        pe.wait_ge(mult_done, M0 + JQ + 2)
                        for b in range(6):
                            pe.matmul(bank[b][:, :], sm("zeros"), x_sb[:, 0:512], start=True, stop=True)

                    def tokens(i, s, k):
                        gb = 7 if (vq is not None) else (7, 4)[s % 2]
                        if k == 0:
                            pe.wait_ge(mult_done, val(i, steps, M0 + gq_ * JQ + s + (2 if vq is not None else 1)))
                            pe.wait_ge(oh_ready, val(i, 2 * steps, 2 * (M0 + gq_ * JQ + s + 1)))
                        for x in range(4 * k, 4 * k + 4):
                            for y in range(3):
                                mm = pe.matmul(bank[gb][:, x * JQ:(x + 1) * JQ], oh_i[:, s % 2, x, :],
                                               oh_g[:, x, y, :], start=(y == 0), stop=(y == 2))
                        if k == 2:
                            mm.then_inc(tok_mm, 1)

                    def values(e, sl, half):
                        outs = [(b, hf) for b in range(3) for hf in range(2)]
                        for b, hf in outs[3 * half:3 * half + 3]:
                            for x, y in ((0, 0), (0, 1), (1, 0)):
                                mm = pe.matmul(bank[2 * b + hf][:, :], cp4[:, sl, x, b * P:(b + 1) * P],
                                               part(e, y, hf * 512, (hf + 1) * 512), start=False, stop=True,
                                               skip_group_check=True)
                        return mm

                    def body(i):
                        for s in range(steps):
                            e = first + w * s
                            ub = 6 if vq is not None else (6, 5)[s % 2]
                            k = 0
                            if uq is not None:
                                pe.wait_ge(lo_ready, val(i, 4, E0 + e + 1))
                                pe.wait_ge(gelu_done, val(i, steps, U0 + uq * JQ + s + (2 if vq is not None else 1)))
                                product(e, bank[ub][:, 0:T], range(4))
                                tokens(i, s, 0)
                                product(e, bank[ub][:, 0:T], range(4, DC)).then_inc(tile_used, 1)
                                tokens(i, s, 1)
                                k = 2
                                e += 1
                            if vq is not None:
                                pe.wait_ge(lo_ready, val(i, 4, E0 + e + 1))
                                pe.wait_ge(clo, val(i, steps, V0 + vq * JQ + s + 1))
                                values(e, s % 2, 0)
                                if gq_ is not None:
                                    tokens(i, s, k)
                                    k += 1
                                values(e, s % 2, 1).then_inc(tile_used, 1)
                            if gq_ is not None:
                                for k in range(k, 3):
                                    tokens(i, s, k)

                    if gq_ is not None:
                        pe.wait_ge(route_e, 3 * l + 3)
                    with pe.Fori(0, JQ // steps) as it:
                        body(it)
                pe.wait_ge(out_evac, 6 * l + 6)
                for c in range(DC):
                    if c >= 2:
                        pe.wait_ge(out_used, 16 * l + 2 * c - 2)
                    for b in range(3):
                        mm = pe.transpose(bank[6 + c % 2][:, b * P:(b + 1) * P], otok[:, b, c * P:(c + 1) * P],
                                          sm("ident"))
                    mm.then_inc(out_t, 1)

            pe.wait_ge(h_ready, 16)
            peer_pe(0)
            pe.wait_ge(out_used, 16)
            norm_pe()
            pe.wait_ge(h_ready, 24)
            for m in range(8):
                for w in range(2):
                    if m >= 2:
                        pe.wait_ge(glu_done, m - 1)
                    linear(POS["pw1"] + 2 * m + w, bank[2 * (m % 2) + w][:, 0:T], hs)
            pe.wait_ge(conv_tap, 8 * CONV_W)
            for c in range(DC):
                mm = pe.matmul(bank[4][:, 0:T], sm("mean_d"), acc[:, c, :], start=(c == 0), stop=(c == DC - 1))
            mm.then_inc(st_mm, 1)
            pe.wait_ge(act_ready, 9)
            for c in range(DC):
                mm = pe.matmul(bank[5][:, 0:T], sm("mean_d"), acq[:, c, :], start=(c == 0), stop=(c == DC - 1))
            mm.then_inc(st_mm, 1)
            pe.wait_ge(conv_act, 8)
            for m in range(8):
                if m >= 4:
                    pe.wait_ge(pw2_ev, m - 3)
                linear(POS["pw2"] + m, bank[m % 4][:, 0:T], hs)
            pe.wait_ge(res_done, 9)
            norm_pe(1)
            pe.wait_ge(h_ready, 32)
            peer_pe(1)
            pe.wait_ge(out_used, 32)
            norm_pe(2)

        @block.vector
        def _(dve):
            st = Steps(dve, v_step)
            norm_n = [0]
            dve.sem_inc(mult_done, 2)

            def bc(ap, shape):
                return ap.to_broadcast(shape)

            def norm_dve(which=0):
                sq3, h3, root, rstd = norm_bufs(which)
                final = which == 2
                u = norm_n[0]
                norm_n[0] += 1
                dve.wait_ge(rt_ready, u + 1)
                st.link(dve.reciprocal(rstd, root))
                ins = dve.tensor_tensor(sq3, x3, rstd.unsqueeze(1).to_broadcast([P, DC, T]), ALU.mult)
                if not final:
                    ins.then_inc(xn_ready, 1)
                    return
                st.link(ins)
                dve.tensor_tensor(h3, sq3, sm("norm_f").unsqueeze(2).to_broadcast([P, DC, T]), ALU.mult)\
                   .then_inc(y_ready, 1)

            dve.wait_ge(row_mm, 12)
            st.link(dve.tensor_tensor(modv[:, :].rearrange("p (c g) -> p c g", g=2),
                                      bank[7][:, 0:192].rearrange("p (c g) -> p c g", g=2),
                                      sm("b_mod").unsqueeze(2).to_broadcast([P, 96, 2]), ALU.add))
            for l in range(2):
                for n in range(2):
                    ins = dve.scalar_tensor_tensor(
                        scale5[:, l, n], mod4[:, l, 24 * n + 8:24 * n + 16], 1.0,
                        sm("norm%d" % (n + 1), 8 * l, 8 * l + 8).unsqueeze(2).to_broadcast([P, 8, 2]),
                        ALU.add, ALU.mult)
                    if (l, n) != (0, 0):
                        ins.then_inc(mod_ready, 1)
            norm_dve()

            dve.wait_ge(pool_init, 3)
            dve.wait_ge(s_mixer, 16)
            for m in range(A_CH):
                dve.wait_ge(z_evac, m + 1)
                t = zshift[:, m % 2, :]
                z = zp[:, m, 1:1 + TS]
                st.link(dve.tensor_tensor(t, zp[:, m, 0:TS], zp[:, m, 2:2 + TS], ALU.add))
                st.link(dve.scalar_tensor_tensor(t, t, 0.5, z, ALU.mult, ALU.subtract))
                dve.scalar_tensor_tensor(zs[:, m, :], t, sm("mu", m, m + 1), z, ALU.mult, ALU.add)\
                   .then_inc(zs_ready, 1)

            for g in range(4):
                dve.wait_ge(st_mm, g + 1)
                dve.tensor_tensor(gc[:, g, :], gv[:, g, :], bank[g][:, 0:T], ALU.subtract).then_inc(st_in, 1)
            for g in range(4):
                dve.wait_ge(st_rt, g + 1)
                st.link(dve.reciprocal(gs[:, g, :], gs[:, g, :]))
                st.link(dve.tensor_tensor(gc[:, g, :], gc[:, g, :], gs[:, g, :], ALU.mult))
                dve.tensor_scalar(gc[:, g, :], gc[:, g, :], sm("lnv_g", g, g + 1), sm("lnv_b", g, g + 1),
                                  ALU.mult, ALU.add).then_inc(gm_norm, 1)
            for g in range(4):
                dve.wait_ge(gm_mm, g + 1)
                dve.tensor_tensor(yb[:, g, :], gu[:, g, :], bank[4 + g][:, 0:T], ALU.mult).then_inc(gm_ev, 1)

            dve.wait_ge(zs_ready, A_CH)
            for p in range(4):
                ins = dve.tensor_scalar(nkk[:, p, :], zs[:, 4 + p, :], sm("k_k", p, p + 1), None, ALU.mult)
            ins.then_inc(kk_sq, 1)
            dve.wait_ge(kk_rt, 4)
            st.link(dve.tensor_scalar(tmp1, tmp1, 1e-12, None, ALU.max))
            st.link(dve.reciprocal(tmp1, tmp1))
            dve.scalar_tensor_tensor(nkk, nkk, -1.0, tmp1, ALU.mult, ALU.mult).then_inc(lw_sum, 1)
            dve.memset(ysum[:, :, T_CTX:LAT0], 0.0)

            for d in range(2):
                dve.wait_ge(lw_ev, 8 * d + 8)
                step = 1 if d == 0 else -1
                for p in range(4):
                    ins = dve.tensor_tensor_scan(tmp3[:, p, ::step], sm("keep", d * TS, (d + 1) * TS)[:, ::step],
                                                 tmp1[:, p, ::step], 0.0, ALU.mult, ALU.add)
                ins.then_inc(lw_sum, 1)
                dve.wait_ge(lw_sum, 2 * d + 2)
                dve.tensor_tensor(tmp1, tmp3, tmp1, ALU.subtract).then_inc(lw_sum, 1)
                st.mark(dve.scalar_tensor_tensor(bt_, nkk, -1.0, tmp2, ALU.mult, ALU.mult))
                st.settle()
                for p in range(4):
                    st.mark(dve.tensor_scalar(tmp2[:, p, :], tmp2[:, p, :], -1.0, sm("k_a", p, p + 1),
                                              ALU.add, ALU.mult))
                st.settle()
                st.link(dve.scalar_tensor_tensor(tmp2, tmp2, 1.0, zs[:, 4:8, :], ALU.add, ALU.mult))
                if d == 0:
                    st.link(dve.tensor_copy(kdsum, tmp2))
                else:
                    st.link(dve.tensor_tensor(kdsum, kdsum, tmp2, ALU.add))
                st4 = state.rearrange("p (w s x) -> p w s x", w=2, s=2)
                st.mark(dve.tensor_copy(st4[:, 0, 0, :], sm("s0", d * 256, d * 256 + 256)))
                st.mark(dve.memset(st4[:, 1, 0, :], 0.0))
                dve.wait_ge(ex_ready, 3 * d + 3)
                off = CHUNK - 1 if d == 0 else 0
                pC3 = pC.rearrange("p (c q) -> p c q", q=4)
                st.mark(dve.tensor_copy(pC3[:, 0:2, :], rt_[:, :, off:T_CTX:CHUNK].rearrange("p q c -> p c q")))
                st.mark(dve.tensor_copy(pC3[:, 2:6, :], rt_[:, :, LAT0 + off:TS:CHUNK].rearrange("p q c -> p c q")))
                st.mark(dve.tensor_tensor(bt_, bt_, kt_, ALU.mult))
                st.settle()
                dve.tensor_tensor(rt_, rt_, zs[:, 0:4, :], ALU.mult)
                dve.tensor_tensor(kt_, kt_, tmp2, ALU.mult)
                dve.tensor_tensor(at_, at_, nkk, ALU.mult).then_inc(sc_ready, 1)

                strict = sm("strict", 64 * d, 64 * d + 64).unsqueeze(1).to_broadcast([P, 8, 64])
                incl = sm("incl", 64 * d, 64 * d + 64).unsqueeze(1).to_broadcast([P, 8, 64])
                eye = sm("eye64").unsqueeze(1).to_broadcast([P, 8, 64])

                def band(lev):
                    o = (d * 6 + lev) * 64
                    return sm("bands", o, o + 64).unsqueeze(1).to_broadcast([P, 8, 64])

                for j, (dd, name, g, e) in enumerate(RW_JOBS):
                    if dd != d or e != "V":
                        continue
                    dve.wait_ge(rw_mm, j + 1)
                    ps = bank[j % 8]
                    ps3 = ps[:, :].rearrange("p (w t) -> p w t", t=64)

                    def grp(a):
                        return a[:, g * 512:(g + 1) * 512].rearrange("p (w t) -> p w t", t=64)

                    if name == "LT":
                        dve.tensor_tensor(grp(ltm), ps3, strict, ALU.mult).then_inc(rw_evV, 1)
                        dve.wait_ge(rw_evV, RW_EV[j][1])
                        dve.tensor_tensor(grp(em), grp(ltm), band(0), ALU.mult).then_inc(lt_ready, 1)
                    elif name == "LAK":
                        dve.tensor_tensor(grp(lak), ps3, strict, ALU.mult).then_inc(rw_evV, 1)
                    elif name == "MRB":
                        dve.tensor_tensor(grp(mrb), ps3, incl, ALU.mult).then_inc(rw_evV, 1)
                    elif name == "MRK":
                        dve.tensor_tensor(grp(mrk), ps3, incl, ALU.mult).then_inc(rw_evV, 1)
                    elif name == "D0":
                        dve.wait_ge(lt_ready, 18 * d + g + 1)
                        st.mark(dve.tensor_tensor(grp(dm), ps3, eye, ALU.add))
                        dve.tensor_tensor(grp(dT), grp(em), eye, ALU.add).then_inc(rw_evV, 1)
                        dve.wait_ge(rw_evV, RW_EV[j][1])
                        dve.tensor_tensor(grp(em), grp(ltm), band(1), ALU.mult).then_inc(lt_ready, 1)
                    elif name[:2] == "GT":
                        lev = LEVELS.index(int(name[2:]))
                        dve.tensor_tensor(grp(dT), grp(dT), ps3, ALU.add).then_inc(rw_evV, 1)
                        if lev + 1 < len(LEVELS):
                            dve.tensor_tensor(grp(em), grp(ltm), band(lev + 2), ALU.mult).then_inc(lt_ready, 1)
                    elif name[0] == "G":
                        dve.tensor_tensor(grp(dm), grp(dm), ps3, ALU.add).then_inc(rw_evV, 1)
                    elif name == "S":
                        s = g
                        n = len(SCAN[d][s])
                        for ci, (chain, c) in enumerate(SCAN[d][s]):
                            which = 0 if chain == "lat" else 1
                            if chain == "ctx" and s == 1:
                                dst = sm("s0", d * 256, d * 256 + 256)
                            else:
                                dst = st4[:, which, (s + 1) % 2, :]
                            ins = dve.tensor_tensor(
                                dst.rearrange("p (q i) -> p q i", i=HEAD),
                                ps[:, ci * 256:(ci + 1) * 256].rearrange("p (q i) -> p q i", i=HEAD),
                                pC3[:, c, :].unsqueeze(2).to_broadcast([P, 4, HEAD]), ALU.mult)
                            if ci < n - 1:
                                st.mark(ins)
                        ins.then_inc(rw_evV, 1)
                    else:
                        s = g
                        n = len(SCAN[d][s])
                        for ci, (chain, c) in enumerate(SCAN[d][s]):
                            c0 = tcol(c)
                            y = ysum[:, :, c0:c0 + 64]
                            yp = ps[:, ci * 256:(ci + 1) * 256].rearrange("p (q t) -> p q t", t=64)
                            if d == 0:
                                ins = dve.tensor_copy(y, yp)
                            else:
                                ins = dve.tensor_tensor(y, y, yp, ALU.add)
                            if ci < n - 1:
                                st.mark(ins)
                        ins.then_inc(rw_evV, 1)

            dve.wait_ge(rw_evV, RW_EV[RW_AT[(1, "Y", 3)]][1])
            st.settle()
            st.link(dve.tensor_tensor(tmp0, kdsum, zs[:, 0:4, :], ALU.mult))
            for p in range(4):
                ins = dve.tensor_scalar(tmp0[:, p, :], tmp0[:, p, :], sm("r_k", p, p + 1), None, ALU.mult)
            ins.then_inc(sc_ready, 1)
            for p in range(4):
                dve.wait_ge(st_mm, 8 + p + 1)
                ins = dve.tensor_tensor(gy[:, p, :], ysum[:, p, :], bank[p][:, 0:TS], ALU.subtract)
            ins.then_inc(st_in, 1)
            dve.wait_ge(st_in, 5)
            dve.wait_ge(st_rt, 8)
            st.link(dve.reciprocal(gmean, gmean))
            st.link(dve.tensor_tensor(gy, gy, gmean, ALU.mult))
            for p in range(4):
                st.mark(dve.tensor_scalar(gy[:, p, :], gy[:, p, :], sm("lnx_g", p, p + 1), sm("lnx_b", p, p + 1),
                                          ALU.mult, ALU.add))
            for p in range(4):
                dve.wait_ge(kk_ss, 4 + p + 1)
                st.mark(dve.tensor_tensor(rt_[:, p, :], zs[:, 8 + p, :], bank[p][:, 0:TS], ALU.mult))
            st.settle()
            st.link(dve.tensor_tensor(gy, gy, rt_, ALU.add))
            for p in range(4):
                dve.wait_ge(kk_ss, 8 + p + 1)
                for t0, c0, n in SEG:
                    ins = dve.tensor_tensor(ya3[:, p * T + t0:p * T + t0 + n], gy[:, p, c0:c0 + n],
                                            bank[4 + p][:, c0:c0 + n], ALU.mult)
            ins.then_inc(mix_ready, 1)

            def residual(l, gate, c, src, done):
                for g, (a, b) in enumerate(GROUPS):
                    ins = dve.scalar_tensor_tensor(x3[:, c, a:b], src[:, a:b], mod4[:, l, gate + c, g:g + 1],
                                                   x3[:, c, a:b], ALU.mult, ALU.add)
                    if done is not None:
                        ins.then_inc(done, 1)
                return ins

            for m in range(8):
                dve.wait_ge(dense_used, POS["out"] + m + 1)
                ins = residual(0, 16, m, bank[m], None)
            ins.then_inc(res_done, 1)
            dve.wait_ge(res_done, 1)
            norm_dve(1)

            def top16(rows, vals, idxs, tmps, free=None):
                for r, v in zip(rows, vals):
                    st.mark(dve.max(v[:, 0:8], r))
                st.settle()
                for r, v, i, t in zip(rows, vals, idxs, tmps):
                    st.mark(dve.max_index(i[:, 0:8], v[:, 0:8], r))
                    st.mark(dve.match_replace(t, v[:, 0:8], r, LOWEST))
                st.settle()
                for n, (v, t) in enumerate(zip(vals, tmps)):
                    ins = dve.max(v[:, 8:16], t)
                    if n == 0 and free is not None:
                        ins.then_inc(free, 1)
                        dve.wait_ge(free, free_n[0])
                    else:
                        st.mark(ins)
                st.settle()
                for v, i, t in zip(vals, idxs, tmps):
                    st.mark(dve.max_index(i[:, 8:16], v[:, 8:16], t))

            free_n = [0]

            def peer_dve(l):
                for j in range(16):
                    dve.wait_ge(s_evac, 16 * l + j + 1)
                    free_n[0] += 1
                    top16([sc_sb[:, j % 2, b, :] for b in range(3)], [sv[:, b, j, :] for b in range(3)],
                          [si[:, b, j, :] for b in range(3)], [stmp[:, j % 2, b, :] for b in range(3)], s_free)
                st.settle()
                st.mark(dve.tensor_copy(sif, si))
                sv5 = sv.rearrange("p b (h c) k -> p b h c k", c=2)
                sif5 = sif.rearrange("p b (h c) k -> p b h c k", c=2)
                for b in range(3):
                    st.link(dve.tensor_tensor(
                        cand.rearrange("p h (a k) -> p h a k", a=16),
                        sv5[:, b, :, 0, :].unsqueeze(3).to_broadcast([P, 8, 16, 16]),
                        sv5[:, b, :, 1, :].unsqueeze(2).to_broadcast([P, 8, 16, 16]), ALU.add))
                    top16([cand[:, h, :] for h in range(8)], [fv[:, b, h, :] for h in range(8)],
                          [fi[:, b, h, :] for h in range(8)], [ctmp[:, h, :] for h in range(8)])
                    st.settle()
                dve.tensor_tensor(ge, fv, fv[:, :, :, 0:1].to_broadcast([P, 3, 8, 16]), ALU.subtract)\
                   .then_inc(cand_max, 1)
                st.mark(dve.tensor_scalar(fa_u, fi, 4, None, ALU.logical_shift_right))
                st.mark(dve.tensor_scalar(fb_u, fi, 15, None, ALU.bitwise_and))
                st.settle()
                st.mark(dve.tensor_copy(fa, fa_u))
                st.mark(dve.tensor_copy(fb, fb_u))
                st.settle()
                shape = [P, 8, 16, 16]
                pos = sm("iota", 0, 16).unsqueeze(1).unsqueeze(1).to_broadcast(shape)
                for b in range(3):
                    for oh, f, c in ((oh1, fa, 0), (oh2, fb, 1)):
                        st.mark(dve.tensor_tensor(oh, pos, f[:, b].unsqueeze(3).to_broadcast(shape), ALU.is_equal))
                    st.settle()
                    for oh, c in ((oh1, 0), (oh2, 1)):
                        st.mark(dve.tensor_tensor(oh, oh, sif5[:, b, :, c, :].unsqueeze(2).to_broadcast(shape),
                                                  ALU.mult))
                    st.settle()
                    for oh, c in ((oh1, 0), (oh2, 1)):
                        dve.tensor_reduce(routes[:, c, b].rearrange("p (h k) -> p h k", k=16), oh, AX, ALU.add)\
                           .then_inc(route, 1)
                    dve.wait_ge(route, 7 * l + 2 * b + 2)
                dve.wait_ge(e_ready, l + 1)
                st.link(dve.tensor_reduce(gsum, ge, AX, ALU.add))
                st.link(dve.reciprocal(gsum, gsum))
                dve.tensor_tensor(routes[:, 2].rearrange("p b (h k) -> p b h k", k=16), ge,
                                  gsum.to_broadcast([P, 3, 8, 16]), ALU.mult).then_inc(route, 1)
                dve.wait_ge(route_e, 3 * l + 3)
                st.link(dve.tensor_tensor(gate_rest, bank[4][:, 0:T], gateT[:, 0, :], ALU.subtract))
                st.link(dve.tensor_copy(gateT[:, 1, :], gate_rest))
                st.link(dve.tensor_tensor(gate_rest, gate_rest, gateT[:, 1, :], ALU.subtract))
                st.link(dve.tensor_copy(gateT[:, 2, :], gate_rest))
                V0, M0, U0 = NK * l, NK * l, NK * l
                for first, uq, vq, gq_ in PHASES:
                    w = 2 if uq is not None and vq is not None else 1
                    steps = 4 // w
                    n = JQ // steps

                    def hots(i, s):
                        g = M0 + gq_ * JQ + s
                        t = bass.ds(val(i, steps * GRP, s * GRP), GRP)
                        dve.wait_ge(tok_mm, val(i, steps, g + 1))
                        dve.tensor_tensor(oh_i[:, s % 2], sm("iota").unsqueeze(1).to_broadcast([P, GRP, P]),
                                          routeT[:, 0, t].unsqueeze(2).to_broadcast([P, GRP, P]), ALU.is_equal)\
                           .then_inc(oh_ready, 1)
                        dve.wait_ge(oh_ready, val(i, 2 * steps, 2 * g + 1))
                        dve.tensor_tensor(oh_j, sm("iota", gq_ * JQ, (gq_ + 1) * JQ).unsqueeze(1)
                                          .to_broadcast([P, GRP, JQ]),
                                          routeT[:, 1, t].unsqueeze(2).to_broadcast([P, GRP, JQ]), ALU.is_equal)\
                           .then_inc(col_ready, 1)

                    def gated_cols(i, s):
                        t = bass.ds(val(i, steps * GRP, s * GRP), GRP)
                        dve.wait_ge(col_ready, val(i, steps, M0 + gq_ * JQ + s + 1))
                        dve.tensor_tensor(oh_g, oh_j.unsqueeze(2).to_broadcast([P, GRP, 3, JQ]),
                                          gateT[:, :, t].rearrange("p y t -> p t y").unsqueeze(3)
                                          .to_broadcast([P, GRP, 3, JQ]), ALU.mult).then_inc(oh_ready, 1)

                    def coef_lo(i, s):
                        sl = s % 2
                        dve.wait_ge(chi, val(i, steps, V0 + vq * JQ + s + 1))
                        dve.tensor_tensor(cp4[:, sl, 1, :],
                                          buf4[:, vq % 2, bass.ds(val(i, steps, s), 1), :].rearrange("p o t -> p (o t)"),
                                          cp4[:, sl, 0, :].bitcast(F32), ALU.subtract).then_inc(clo, 1)

                    def body(i, last):
                        for s in range(steps):
                            end = last and s == steps - 1
                            if gq_ is not None and not end:
                                hots(i, s + 1)
                            if vq is not None and not end:
                                coef_lo(i, s + 1)
                            if gq_ is not None:
                                gb = 7 if (vq is not None) else (7, 4)[s % 2]
                                dve.wait_ge(tok_mm, val(i, steps, M0 + gq_ * JQ + s + 3))
                                dst = buf4[:, gq_ % 2, :, bass.ds(val(i, steps * GRP, s * GRP), GRP)]
                                dve.tensor_tensor(dst, bank[gb][:, 0:JQ * GRP].rearrange("p (t j) -> p j t", j=JQ),
                                                  dst, ALU.mult).then_inc(mult_done, 1)
                                if not end:
                                    gated_cols(i, s + 1)

                    if gq_ is not None:
                        dve.wait_ge(gelu_done, U0 + (gq_ + 1) * JQ + 2)
                        hots(0, 0)
                        gated_cols(0, 0)
                    if vq is not None:
                        coef_lo(0, 0)
                    with dve.Fori(0, n - 1) as it:
                        body(it, False)
                    body(n - 1, True)
                for c in range(DC):
                    dve.wait_ge(out_t, 8 * l + c + 1)
                    residual(l, 40, c, bank[6 + c % 2], out_used)

            peer_dve(0)
            dve.wait_ge(out_used, 16)
            norm_dve()
            dve.wait_ge(pool_init, 7)
            for m in range(8):
                dve.wait_ge(glu_g, m + 1)
                dve.scalar_tensor_tensor(
                    zc[:, m, :, HALO:HALO + ROW], bank[2 * (m % 2)][:, 0:T].rearrange("p (r t) -> p r t", t=ROW),
                    sm("b_pw1", m, m + 1), glug[:, m % 2, :].rearrange("p (r t) -> p r t", t=ROW),
                    ALU.add, ALU.mult).then_inc(glu_done, 1)
            dve.wait_ge(halo_done, 2)
            dve.wait_ge(glu_done, 8)

            def row(a, m):
                return a[:, m, :].rearrange("p (r t) -> p r t", t=ROW)

            for m in range(8):
                dve.tensor_scalar(row(acc, m), zc[:, m, :, 0:ROW], sm("conv_k", m, m + 1), sm("conv_b", m, m + 1),
                                  ALU.mult, ALU.add).then_inc(conv_tap, 1)
            with dve.Fori(0, CONV_W - 1) as it:
                for m in range(8):
                    dve.wait_ge(conv_tap, it * 8 + (m + 1))
                    k0 = SM["conv_k"][0]
                    dve.scalar_tensor_tensor(row(acc, m), zc[:, m, :, bass.ds(it + 1, ROW)],
                                             small[:, bass.ds(it * 8 + (k0 + 8 + m), 1)], row(acc, m),
                                             ALU.mult, ALU.add).then_inc(conv_tap, 1)
            dve.wait_ge(st_mm, 17)
            dve.tensor_tensor(accs, acc, bank[4][:, 0:T].unsqueeze(1).to_broadcast([P, DC, T]), ALU.subtract)\
               .then_inc(st_in, 1)
            dve.wait_ge(st_in, 6)
            dve.wait_ge(st_rt, 9)
            st.link(dve.reciprocal(lrstd, lroot))
            dve.tensor_tensor(accs, accs, lrstd.unsqueeze(1).to_broadcast([P, DC, T]), ALU.mult).then_inc(st_in, 1)
            for m in range(8):
                dve.wait_ge(pw2_ev, m + 1)
                residual(1, 16, m, pw2t[:, m % 2, :], None).then_inc(res_done, 1)
            dve.wait_ge(res_done, 9)
            norm_dve(1)
            peer_dve(1)
            dve.wait_ge(out_used, 32)
            norm_dve(2)


def _constants():
    c = {}
    c["ident"] = np.eye(P)
    c["mean_d"] = np.full((P, P), 1.0 / D)
    c["mean_p"] = np.full((P, P), 1.0 / P)
    blk = (np.arange(P)[:, None] // HEAD == np.arange(P)[None, :] // HEAD) * 1.0
    c["head_sum"] = blk
    c["head_mean"] = blk / HEAD
    c["iota"] = np.tile(np.arange(P), (P, 1))
    s = (np.arange(P) % CHUNK)[:, None]
    t = np.arange(CHUNK)[None, :]
    c["strict"] = np.concatenate([s < t, s > t], 1)
    c["incl"] = np.concatenate([s <= t, s >= t], 1)
    bands = []
    for d in range(2):
        lo, hi = (s, t) if d == 0 else (t, s)
        for n in (1, 2, 4, 8, 16, 32):
            bands.append((lo // (2 * n) == hi // (2 * n)) & (lo // n % 2 == 0) & (hi // n % 2 == 1))
    c["bands"] = np.concatenate(bands, 1)
    c["eye64"] = (s == t)
    keep = np.ones((2, TS))
    for ch in range(NCH):
        keep[0, tcol(ch)] = 0
        keep[1, tcol(ch) + CHUNK - 1] = 0
    keep[:, T_CTX] = 0
    c["keep"] = np.tile(keep.reshape(1, -1), (P, 1))
    c["zeros"] = np.zeros((P, P))
    c["ones"] = np.ones((P, P))
    return {k: np.asarray(v, np.float32) for k, v in c.items()}


def _cols(v):
    return v.reshape(-1, P).T


def _tiles(w):
    n = w.shape[1] // P
    return w.reshape(DC, P, n, P).transpose(2, 1, 0, 3).reshape(n, P, D)


def kernel(**inputs):
    import concourse.bacc as _bacc
    from concourse.bass_utils import run_bass_kernel_spmd as _run

    a = {k: np.asarray(v) for k, v in inputs.items()}
    sm = _constants()
    cc = np.concatenate
    sm["b_mod"] = cc([_cols(a["b_mod"][l]) for l in range(2)], 1)
    sm["norm1"] = cc([_cols(a["norm1"][l]) for l in range(2)], 1)
    sm["norm2"] = cc([_cols(a["norm2"][l]) for l in range(2)], 1)
    sm["norm_f"] = _cols(a["norm_f"])
    sm["mu"] = _cols(a["mu_a"][0])
    sm["w0"] = cc([_cols(a["w0"][0, d]) for d in range(2)], 1)
    sm["a0"] = cc([_cols(a["a0"][0, d]) for d in range(2)], 1)
    for k in ("k_k", "k_a", "r_k", "lnx_g", "lnx_b", "lnv_g", "lnv_b", "b_pw1", "conv_b", "lnc_g", "lnc_b", "b_pw2"):
        sm[k] = _cols(a[k][0])
    sm["conv_k"] = cc([_cols(a["conv_k"][0, w]) for w in range(CONV_W)], 1)
    sm["w2"] = a["w2"][0].reshape(P, A_W)
    sm["a2"] = a["a2"][0].reshape(P, A_W)
    sm["g2"] = a["g2"][0]
    sm["w_sT"] = a["w_s"][0].transpose(2, 0, 1).reshape(P, 4 * P)
    b_s = np.zeros((P, 4 * P), np.float32)
    b_s[0] = a["b_s"][0].reshape(-1)
    sm["b_s"] = b_s
    sm["sk"] = a["sub_keys"].transpose(3, 0, 1, 2).reshape(P, 4 * P)
    sm["s0"] = a["state_rwkv"][0, 0].reshape(2, NP_, 2, HEAD, HEAD).transpose(2, 4, 0, 1, 3).reshape(P, 2 * NP_ * HEAD)
    cv = cc([a["c_ctx"].reshape(1, D), a["c"].reshape(1, D)], 0)
    sm["cvec"] = cv.reshape(2, DC, P).transpose(2, 1, 0).reshape(P, 16)
    for k, n in SMALL + MIXER:
        assert sm[k].shape == (P, n), (k, sm[k].shape, n)
    small, mixer = (np.ascontiguousarray(cc([sm[k] for k, _ in part], 1)) for part in (SMALL, MIXER))
    pw1 = _tiles(a["w_pw1"][0])
    pw1 = pw1.reshape(2, 8, P, D).transpose(1, 0, 2, 3).reshape(16, P, D)
    mod = [a["w_mod"][l].reshape(DC, P, 6, D).transpose(2, 0, 1, 3).reshape(48, P, D) for l in range(2)]
    w = cc(mod + [_tiles(a["w_in_ab"][0]), _tiles(a["w_out_ab"][0]),
            _tiles(a["w_query"][0]), pw1, _tiles(a["w_pw2"][0]), _tiles(a["w_query"][1])], 0)
    e_u = np.ascontiguousarray(a["expert_u"].reshape(2, NK, NK, DC, P).transpose(0, 2, 4, 3, 1)).reshape(2, NK, P, D)
    x_t = np.ascontiguousarray(cc([a["x_prompt"][0], a["x_sample"][0]], 0).T)
    arrays = {"x_t": x_t, "small": small, "mixer": mixer, "w_tiles": w, "e_u": e_u,
              "e_v": a["expert_v"].reshape(2, NK, NK, D)}

    nc = _bacc.Bacc("TRN2", target_bir_lowering=False, num_devices=1)
    ap = {k: nc.dram_tensor("in_" + k, v.shape, F32, kind="ExternalInput").ap() for k, v in arrays.items()}
    y_t = nc.dram_tensor("y_t", (D, T), F32, kind="ExternalOutput").ap()
    s_new = nc.dram_tensor("s_new", (2, NP_, P, HEAD), F32, kind="ExternalOutput").ap()
    build_trunk(nc, ap["x_t"], ap["small"], ap["mixer"], ap["w_tiles"], ap["e_u"],
                ap["e_v"].rearrange("l i j d -> l j i d"), y_t, s_new)
    r = _run(nc, [{"in_" + k: v for k, v in arrays.items()}], core_ids=[0]).results[0]
    y = r["y_t"].T
    s = r["s_new"].reshape(2, NP_, 2, HEAD, HEAD).transpose(0, 1, 2, 4, 3).reshape(1, 1, 2, 8, HEAD, HEAD)
    return (np.ascontiguousarray(y[None, :T_CTX]), np.ascontiguousarray(y[None, T_CTX:]), np.ascontiguousarray(s))
```

```python
from contextlib import ExitStack

import numpy as np

import concourse.bass as bass
from concourse import mybir

P = 128
D = 1024
DC = D // P
T_CTX, T_LAT = 128, 256
T = T_CTX + T_LAT
GROUPS = ((0, T_CTX), (T_CTX, T))
A_W = 512
HEAD = 64
NP_ = A_W // P
A_CH = 15
IN_CH = 23
CHUNK = 64
NCH = T // CHUNK
TS = T + 1
LAT0 = T_CTX + 1
CONV_W, HALO = 31, 15
ROW = 64
NROW = T // ROW
ROWP = ROW + 2 * HALO
DVE_TAPS = 19
POOL_TAPS = CONV_W - DVE_TAPS
TAP_STEP, TAP_ROUND = 4, 4
NK = 128
RING = 4
SPLIT = 4
IN_SPLIT = 3
QT = 4
JQ = NK // QT
GRP = T // JQ
SEQ_TILES = 16 + NK * 2

ALU = mybir.AluOpType
ACT = mybir.ActivationFunctionType
AX = mybir.AxisListType.X
F32 = mybir.dt.float32
F32R = mybir.dt.float32r
BF16 = mybir.dt.bfloat16
U32 = mybir.dt.uint32

EPS, LN_EPS, GN_EPS = 1e-6, 1e-5, 64e-5
DECAY = float(np.exp(-0.5))
LOWEST = -3.4e38


SMALL = [
    ("ident", 128), ("mean_d", 128), ("iota", 128), ("zeros", 128), ("b_mod", 96), ("norm1", 16), ("norm2", 16),
    ("norm_f", 8), ("b_pw1", 16), ("conv_k", 8 * CONV_W), ("conv_b", 8), ("lnc_g", 8), ("lnc_b", 8), ("b_pw2", 8),
    ("sk", 2 * 2 * P), ("cvec", 16),
]
MIXER = [
    ("mean_p", 128), ("head_sum", 128), ("head_mean", 128), ("strict", 128), ("incl", 128), ("bands", 12 * 64),
    ("eye64", 64), ("keep", 2 * TS), ("ones", 128), ("mu", 15), ("w0", 8), ("a0", 8), ("k_k", 4), ("k_a", 4),
    ("r_k", 4), ("lnx_g", 4), ("lnx_b", 4), ("lnv_g", 4), ("lnv_b", 4), ("w2", A_W), ("a2", A_W), ("g2", A_W),
    ("w_sT", 4 * P), ("b_s", 4 * P),
    ("s0", 2 * NP_ * HEAD),
]


def offsets(entries):
    at, out = 0, {}
    for name, n in entries:
        out[name] = (at, n)
        at += n
    return out, at


SM, NSMALL = offsets(SMALL)
MX, NMIXER = offsets(MIXER)


STREAM = [("mod%d" % _k, DC) for _k in range(6)] + [("in", IN_CH), ("mod6", DC), ("mod7", DC), ("mod8", DC),
                                                ("mod9", DC), ("out", 8), ("peer0", SEQ_TILES), ("pw1", 16),
                                                ("mod10", DC), ("mod11", DC), ("pw2", 8), ("peer1", SEQ_TILES)]
POS, _at = {}, 0
for _part, _n in STREAM:
    POS[_part] = _at
    _at += _n
N_DENSE0 = POS["peer0"]
N_DENSE = POS["peer1"] - SEQ_TILES
T_Q0, T_PW1, T_Q1 = N_DENSE0, N_DENSE0 + 16, N_DENSE + 16


EARLY = 2


def dense(n):
    return n + 1 - (SEQ_TILES if n >= POS["pw1"] else 0)


START = [("q", j) for j in range(16)] + [("u", j) for j in range(JQ)]
N_START = len(START)
PHASES = (
    (N_START, 1, None, 0),
    (N_START + JQ, 2, 0, 1),
    (N_START + 3 * JQ, 3, 1, 2),
    (N_START + 5 * JQ, None, 2, 3),
    (N_START + 6 * JQ, None, 3, None),
)


def val(i, a, b):
    return i * a + b


class Steps:

    def __init__(self, eng, sem):
        self.eng, self.sem, self.n = eng, sem, 0

    def mark(self, ins):
        self.n += 1
        ins.then_inc(self.sem, 1)

    def settle(self):
        self.eng.wait_ge(self.sem, self.n)

    def link(self, ins):
        self.mark(ins)
        self.settle()


def tcol(c):
    return c * CHUNK + (1 if c * CHUNK >= T_CTX else 0)


SEG = ((0, 0, T_CTX), (T_CTX, LAT0, T_LAT))

SCAN = (
    ((("lat", 2), ("ctx", 0)), (("lat", 3), ("ctx", 1)), (("lat", 4),), (("lat", 5),)),
    ((("lat", 5), ("ctx", 1)), (("lat", 4), ("ctx", 0)), (("lat", 3),), (("lat", 2),)),
)
MOD_COL = 448
PARTS = ((0, 0), (0, 1), (1, 0))
LEVELS = (2, 4, 8, 16, 32)


def pair_jobs(d):
    jobs = [("LT", "V"), ("LAK", "V"), ("MRB", "V"), ("MRK", "V")]
    if d == 0:
        jobs.append(("VTOK", "A"))
    jobs.append(("D0", "V"))
    for n in LEVELS:
        jobs.append(("F%d" % n, "A"))
        jobs.append(("GT%d" % n, "V"))
        if n != LEVELS[-1]:
            jobs.append(("TR%d" % n, "A"))
    jobs += [("BTOK", "A"), ("KTOK", "A")]
    return [(name, g, e) for name, e in jobs for g in range(3)]


def scan_jobs(d):
    out = []
    for s in range(4):
        out += [("X", s, "A"), ("U", s, "A"), ("S", s, "V"), ("Y", s, "V")]
    return out


RW_JOBS = []
for _d in range(2):
    RW_JOBS += [(_d,) + j for j in pair_jobs(_d)] + [(_d,) + j for j in scan_jobs(_d)]
RW_AT = {j[:3]: i for i, j in enumerate(RW_JOBS)}
RW_EV = []
_c = {"A": 0, "V": 0}
for _j in RW_JOBS:
    _c[_j[3]] += 1
    RW_EV.append((_j[3], _c[_j[3]]))


def build_trunk(nc, x_t, small_d, mixer_d, w_tiles, e_u, e_v, y_t, s_new):
    ctx = ExitStack()
    with ctx:
        def sb(name, cols, dt=F32):
            return ctx.enter_context(nc.sbuf_tensor(name, [P, cols], dt))

        def sem(name):
            return ctx.enter_context(nc.semaphore(name))

        x_sb = sb("x_sb", DC * T)
        x3 = x_sb[:, :].rearrange("p (c t) -> p c t", t=T)
        ring = sb("ring", RING * D)
        small = sb("small", NSMALL)
        modv = sb("modv", 192)
        scale = sb("scale", 2 * 2 * 16)
        silc = sb("silc", 16)
        epsb = sb("epsb", 4)
        IN_AT = 20032
        MROW = 2 * D
        ARENA = 44096 - NMIXER - DC * T - 4
        with ExitStack() as mixers:
            h_sb = mixers.enter_context(nc.sbuf_tensor("h_sb", [P, DC * T + 4], F32))
            smallm = mixers.enter_context(nc.sbuf_tensor("smallm", [P, NMIXER], F32))
            arena = mixers.enter_context(nc.sbuf_tensor("arena", [P, ARENA], F32))
        with ExitStack() as parts:
            parts.enter_context(nc.sbuf_tensor("before_parts", [P, DC * T + 4 + NMIXER + IN_AT], F32))
            in_split = parts.enter_context(nc.sbuf_tensor("in_split", [P, IN_SPLIT * 2 * D], F32R))
            in_h = parts.enter_context(nc.sbuf_tensor("in_h", [P, 2 * DC * T], F32R))
        assert IN_AT + IN_SPLIT * 2 * D + 2 * DC * T <= ARENA - MROW
        in_hp = in_h[:, :].rearrange("p (x c t) -> p x c t", x=2, t=T)
        h3 = h_sb[:, 0:DC * T].rearrange("p (c t) -> p c t", t=T)
        split = sb("split", SPLIT * 2 * D, F32R)
        h_parts = sb("h_parts", 2 * DC * T, F32R)
        hp4 = h_parts[:, :].rearrange("p (x c t) -> p x c t", x=2, t=T)
        coef_parts = sb("coef_parts", 2 * 2 * T, F32R)
        cp4 = coef_parts[:, :].rearrange("p (s x t) -> p s x t", s=2, t=T)
        routes_t = sb("routes_t", 2 * T)
        gate_t = sb("gate_t", 3 * T, BF16)
        hot_i = sb("hot_i", 2 * GRP * P, BF16)
        hot_j = sb("hot_j", GRP * JQ, BF16)
        hot_g = sb("hot_g", GRP * 3 * JQ, BF16)
        gate_sum = sb("gate_sum", GRP // 2 * JQ)
        QW = JQ * T
        gated = sb("gated", 2 * QW)
        bank = [ctx.enter_context(nc.psum_tensor("bank%d" % i, [P, 512], F32)) for i in range(8)]

        def sm(name, a=0, b=None):
            buf, at = (small, SM) if name in SM else (smallm, MX)
            o, n = at[name]
            return buf[:, o + a:o + (n if b is None else b)]

        def ar(o, n):
            assert o + n <= ARENA, (o, n)
            return arena[:, o:o + n]

        mod4 = modv[:, :].rearrange("p (l c g) -> p l c g", l=2, g=2)
        scale5 = scale[:, :].rearrange("p (l n c g) -> p l n c g", l=2, n=2, g=2)

        s_x = sem("x_landed")
        s_small = sem("small_landed")
        w_land = [sem("w_landed%d" % i) for i in range(RING)]
        dense_used = sem("dense_tile_used")
        tile_used = sem("split_tile_used")
        hi_ready = sem("tile_rounded")
        lo_ready = sem("tile_rest_ready")
        s_mixer = sem("mixer_consts_landed")
        row_ready = sem("mod_rows_evacuated")
        row_mm = sem("mod_rows_transposed")
        in_hi = sem("in_tile_rounded")
        in_lo = sem("in_tile_rest_ready")
        in_h_hi = sem("in_h_rounded")
        in_h_lo = sem("in_h_rest_ready")
        hi_h = sem("h_rounded")
        lo_h = sem("h_rest_ready")
        chi = sem("coef_rounded")
        clo = sem("coef_rest_ready")
        mult_done = sem("group_gated")
        half_mm = sem("half_group_gate_product")
        half_done = sem("half_group_gated")
        sum_ready = sem("gate_sum_ready")
        s_out = sem("stores_landed")
        pool_init = sem("pool_init")
        a_step = sem("act_step")
        v_step = sem("dve_step")
        silc_ready = sem("silc_ready")
        mod_ready = sem("mod_scale_ready")
        mod_added = sem("mod_bias_added")
        sq_ready = sem("squares_ready")
        ss_ready = sem("mean_square_ready")
        rt_ready = sem("root_ready")
        xn_ready = sem("x_normed")
        h_ready = sem("h_ready")
        z_evac = sem("z_evacuated")
        zs_ready = sem("z_shifted")
        act_ready = sem("act_inputs_ready")
        kk_sq = sem("kk_squares")
        kk_ss = sem("kk_sums")
        kk_rt = sem("kk_roots")
        lw_mm = sem("lora_products")
        lw_ev = sem("lora_evacuated")
        lw_sum = sem("log_decay_summed")
        ex_ready = sem("exps_ready")
        sc_ready = sem("scaled_ready")
        rw_mm = sem("rwkv_job_product")
        rw_evA = sem("rwkv_job_evac_act")
        rw_evV = sem("rwkv_job_evac_dve")
        lt_ready = sem("lt_ready")
        st_in = sem("stat_inputs")
        st_mm = sem("stat_products")
        st_rt = sem("stat_roots")
        gm_t = sem("gmlp_transposed")
        gm_te = sem("gmlp_transposed_evac")
        gm_mm = sem("gmlp_mixed")
        gm_ev = sem("gmlp_mixed_evac")
        mix_ready = sem("mixer_input_ready")
        bonus_read = sem("bonus_read")
        conv_act = sem("conv_activated")
        gm_norm = sem("gmlp_normed")
        out_used = sem("expert_out_added")
        res_done = sem("residual_added")
        glu_g = sem("glu_gate_ready")
        glu_done = sem("glu_done")
        conv_tap = sem("conv_taps_added")
        prod_ready = sem("conv_products_ready")
        pool_tap = sem("conv_products_added")
        conv_done = sem("conv_chunks_done")
        halo_done = sem("halo_done")
        pw2_ev = sem("pw2_evacuated")
        q_evac = sem("q_evacuated")
        s_mm = sem("scores_product")
        s_evac = sem("scores_evacuated")
        s_free = sem("scores_used")
        cand_max = sem("cand_max")
        e_ready = sem("gate_exp_ready")
        route = sem("routes_ready")
        route_t = sem("routes_transposed")
        route_e = sem("routes_evacuated")
        oh_ready = sem("one_hots_ready")
        col_ready = sem("one_hot_columns_ready")
        tok_mm = sem("token_gate_product")
        gelu_done = sem("gelu_done")
        out_evac = sem("expert_out_evacuated")
        out_t = sem("expert_out_transposed")
        y_ready = sem("y_ready")

        sq3 = ar(0, 3072).rearrange("p (c t) -> p c t", t=T)
        root = ar(3072, T)
        rstd = ar(3072 + T, T)

        o = 0
        zs = ar(o, A_CH * TS).rearrange("p (c t) -> p c t", t=TS); o += A_CH * TS
        ZP = o
        zp = ar(o, A_CH * (TS + 2)).rearrange("p (c t) -> p c t", t=TS + 2)
        GM = ZP + A_CH * (TS + 2)
        gu = ar(GM, 4 * T).rearrange("p (c t) -> p c t", t=T)
        gv = ar(GM + 1536, 4 * T).rearrange("p (c t) -> p c t", t=T)
        gc = ar(GM + 3072, 4 * T).rearrange("p (c t) -> p c t", t=T)
        gs = ar(GM + 4608, 4 * T).rearrange("p (c t) -> p c t", t=T)
        gtok = ar(GM + 6144, 12 * P)
        yb = h_sb[:, 1540:1540 + 4 * T].rearrange("p (c t) -> p c t", t=T)
        kdsum = h_sb[:, 0:1540].rearrange("p (c t) -> p c t", t=TS)
        zshift = ar(GM + 7680, 2 * TS).rearrange("p (c t) -> p c t", t=TS)
        o = ZP

        def take(n):
            nonlocal o
            r = ar(o, n)
            o += n
            return r

        def c4(a):
            return a.rearrange("p (c t) -> p c t", t=TS)

        at_, bt_, kt_, rt_ = (c4(take(1540)) for _ in range(4))
        lak, mrb, mrk, dT, vtok = (take(1536) for _ in range(5))
        lt_o = o
        ltm, dm, fm, em = (take(1536) for _ in range(4))
        btok, ktok = ltm, fm
        xs_, us_ = ar(lt_o + 1536, 512), ar(lt_o + 1536 + 512, 512)
        tmp1, tmp2, tmp3 = (c4(ar(lt_o + i * 1540, 1540)) for i in range(3))
        ysum = c4(take(1540))
        nkk = c4(take(1540))
        tmp0 = c4(take(1540))
        state = take(2 * 2 * 256)
        pC = take(24)
        th = zs[:, 12, :]
        sg = zs[:, 14, :]
        gy = at_
        gq = bt_
        gmean = kt_
        ya3 = ar(ZP + 1540, 4 * T)
        zc = ar(0, DC * NROW * ROWP).rearrange("p (c r t) -> p c r t", c=DC, t=ROWP)
        CO = DC * NROW * ROWP
        acc = ar(CO, DC * T).rearrange("p (c t) -> p c t", t=T)
        acq = ar(CO + 3072, DC * T).rearrange("p (c t) -> p c t", t=T)
        accs = ar(CO + 6144, DC * T).rearrange("p (c t) -> p c t", t=T)
        lroot = ar(CO + 9216 + T, T)
        lrstd = ar(CO + 9216 + 2 * T, T)
        glug = ar(CO + 9216 + 3 * T, 2 * T).rearrange("p (c t) -> p c t", t=T)
        pw2t = ar(CO + 9216 + 5 * T, 2 * T).rearrange("p (c t) -> p c t", t=T)
        prod = ar(CO + 9216 + 7 * T, 2 * POOL_TAPS * T).rearrange("p (s w t) -> p s w t", s=2, t=T)
        buf4 = gated[:, :].rearrange("p (w j t) -> p w j t", w=2, t=T)
        oh_i = hot_i[:, :].rearrange("p (s t i) -> p s t i", s=2, i=P)
        oh_j = hot_j[:, :].rearrange("p (t j) -> p t j", j=JQ)
        oh_g = hot_g[:, :].rearrange("p (t y j) -> p t y j", t=GRP, y=3)
        routeT = routes_t[:, :].rearrange("p (k t) -> p k t", t=T)
        gateT = gate_t[:, :].rearrange("p (y t) -> p y t", t=T)
        gate_rest = hot_i[:, 0:2 * T].bitcast(F32)
        psq = gated[:, 0:3072].rearrange("p (c t) -> p c t", t=T)
        ph = gated[:, 3072:6144].rearrange("p (c t) -> p c t", t=T)
        fsq = gated[:, QW:QW + 3072].rearrange("p (c t) -> p c t", t=T)
        proot = gated[:, 6144:6144 + T]
        prstd = gated[:, 6144 + T:6144 + 2 * T]
        otok = gated[:, 0:3072].rearrange("p (b c) -> p b c", b=3)
        o = QW

        def take(n):
            nonlocal o
            r = gated[:, o:o + n]
            o += n
            assert o <= 2 * QW
            return r

        sv = take(3 * 256).rearrange("p (b j k) -> p b j k", b=3, k=16)
        si = take(3 * 256).bitcast(U32).rearrange("p (b j k) -> p b j k", b=3, k=16)
        sif = take(3 * 256).rearrange("p (b j k) -> p b j k", b=3, k=16)
        both = take(4096)
        q_sb = both[:, 0:2 * T].rearrange("p (s t) -> p s t", t=T)
        sc_sb = both[:, 2 * T:4 * T].rearrange("p (s b k) -> p s b k", s=2, k=P)
        stmp = both[:, 4 * T:6 * T].rearrange("p (s b k) -> p s b k", s=2, k=P)
        cand = both[:, 0:2048].rearrange("p (h k) -> p h k", k=256)
        ctmp = both[:, 2048:4096].rearrange("p (h k) -> p h k", k=256)
        oh1 = both[:, 0:2048].rearrange("p (h k a) -> p h k a", h=8, a=16)
        oh2 = both[:, 2048:4096].rearrange("p (h k a) -> p h k a", h=8, a=16)
        fv = take(T).rearrange("p (b h k) -> p b h k", b=3, k=16)
        fi = take(T).bitcast(U32).rearrange("p (b h k) -> p b h k", b=3, k=16)
        fa_u = take(T).bitcast(U32).rearrange("p (b h k) -> p b h k", b=3, k=16)
        fb_u = take(T).bitcast(U32).rearrange("p (b h k) -> p b h k", b=3, k=16)
        fa = take(T).rearrange("p (b h k) -> p b h k", b=3, k=16)
        fb = take(T).rearrange("p (b h k) -> p b h k", b=3, k=16)
        ge = take(T).rearrange("p (b h k) -> p b h k", b=3, k=16)
        gsum = take(24).rearrange("p (b h k) -> p b h k", b=3, k=1)
        routes = take(3 * T).rearrange("p (k b x) -> p k b x", k=3, b=3)
        mrow = arena[0:2, ARENA - MROW:ARENA]

        def norm_bufs(which):
            return ((sq3, h3, root, rstd), (psq, ph, proot, prstd), (fsq, ph, proot, prstd))[which]

        def row(a, m):
            return a[:, m, :].rearrange("p (r t) -> p r t", t=ROW)

        block = ctx.enter_context(nc.Block())

        @block.sync
        def _(sp):
            def put(n, src, free, count):
                if free is not None:
                    sp.wait_ge(free, count)
                sl = n % RING
                sp.dma_start(ring[:, sl * D:(sl + 1) * D], src).then_inc(w_land[sl], 16)

            def load(n, src):
                m = n - RING
                if m < 0:
                    put(n, src, None, 0)
                elif m < N_DENSE0:
                    put(n, src, dense_used, dense(m))
                elif m < POS["pw1"]:
                    put(n, src, lo_ready, m - N_DENSE0 + 1)
                elif m < POS["peer1"]:
                    put(n, src, dense_used, dense(m))
                else:
                    put(n, src, lo_ready, SEQ_TILES + m - POS["peer1"] + 1)

            def experts(l, wq):
                base = POS["peer%d" % l]
                E0 = SEQ_TILES * l
                for k, (kind, j) in enumerate(START):
                    load(base + k, w_tiles[wq + j] if kind == "q" else e_u[l, j])
                for first, uq, vq, _ in PHASES:
                    kinds = [(e_u, uq)] * (uq is not None) + [(e_v, vq)] * (vq is not None)
                    steps = 4 // len(kinds)
                    with sp.Fori(0, JQ // steps) as it:
                        for k in range(4):
                            src, q = kinds[k % len(kinds)]
                            j = val(it, steps, q * JQ + k // len(kinds))
                            put(base + first + k, src[l, bass.ds(j, 1), :, :].rearrange("o i d -> (o i) d"),
                                lo_ready, val(it, 4, E0 + first + k - RING + 1))

            sp.dma_start(small[:, :], small_d).then_inc(s_small, 16)
            xd = x_t.rearrange("(c p) t -> p c t", p=P)
            half = NMIXER // 2
            for n in range(N_DENSE0):
                load(n, w_tiles[n])
                if n in (16, 24):
                    c = 0 if n == 16 else 4
                    sp.dma_start(x3[:, c:c + 4], xd[:, c:c + 4]).then_inc(s_x, 16)
                if n == 32:
                    sp.dma_start(smallm[:, 0:half], mixer_d[:, 0:half]).then_inc(s_mixer, 16)
                if n == 40:
                    sp.dma_start(smallm[:, half:], mixer_d[:, half:]).then_inc(s_mixer, 16)
            sp.wait_ge(rw_evV, RW_EV[RW_AT[(1, "S", 1)]][1])
            for d in range(2):
                sp.dma_start(s_new[d].rearrange("q p i -> p q i"), sm("s0", d * 256, (d + 1) * 256)
                             .rearrange("p (q i) -> p q i", i=HEAD)).then_inc(s_out, 16)
            experts(0, T_Q0)
            for n in range(POS["pw1"], POS["peer1"]):
                load(n, w_tiles[n - POS["pw1"] + T_PW1])
            experts(1, T_Q1)
            for c in range(0, DC, 2):
                sp.wait_ge(y_ready, c + 2)
                sp.dma_start(y_t.rearrange("(c p) t -> p c t", p=P)[:, c:c + 2], ph[:, c:c + 2]).then_inc(s_out, 16)
            sp.wait_ge(s_out, 16 * (2 + DC // 2))

        @block.gpsimd
        def _(pool):
            pool.memset(zp[:, :, 0:1], 0.0).then_inc(pool_init, 1)
            pool.memset(zp[:, :, T_CTX + 1:T_CTX + 2], 0.0).then_inc(pool_init, 1)
            pool.memset(zp[:, :, TS + 1:TS + 2], 0.0).then_inc(pool_init, 1)
            pool.memset(epsb[:, 0:1], EPS).then_inc(pool_init, 1)
            pool.memset(epsb[:, 1:2], LN_EPS).then_inc(pool_init, 1)
            pool.memset(epsb[:, 2:3], GN_EPS).then_inc(pool_init, 1)

            def rests(l):
                n0, e0 = POS["peer%d" % l], SEQ_TILES * l

                def rest(k, i=0):
                    r, p_ = (n0 + k) % RING, (e0 + k) % SPLIT
                    pool.wait_ge(hi_ready, val(i, 4, e0 + k + 1))
                    pool.tensor_tensor(split[:, (2 * p_ + 1) * D:(2 * p_ + 2) * D], ring[:, r * D:(r + 1) * D],
                                       split[:, 2 * p_ * D:(2 * p_ + 1) * D].bitcast(F32), ALU.subtract)\
                        .then_inc(lo_ready, 1)

                rest(0)
                for c in range(DC):
                    pool.wait_ge(hi_h, DC * l + c + 1)
                    pool.tensor_tensor(hp4[:, 1, c], ph[:, c], hp4[:, 0, c].bitcast(F32), ALU.subtract)\
                        .then_inc(lo_h, 1)
                for k in range(1, 4):
                    rest(k)
                with pool.Fori(0, SEQ_TILES // 4 - 1) as it:
                    for k in range(4, 8):
                        rest(k, it)

            for m in range(IN_CH):
                if m == 1:
                    for c in range(DC):
                        pool.wait_ge(in_h_hi, c + 1)
                        pool.tensor_tensor(in_hp[:, 1, c], h3[:, c], in_hp[:, 0, c].bitcast(F32), ALU.subtract)\
                            .then_inc(in_h_lo, 1)
                r, o = (POS["in"] + m) % RING * D, m % IN_SPLIT * 2 * D
                pool.wait_ge(in_hi, m + 1)
                pool.tensor_tensor(in_split[:, o + D:o + 2 * D], ring[:, r:r + D], in_split[:, o:o + D].bitcast(F32),
                                   ALU.subtract).then_inc(in_lo, 1)
            rests(0)
            pool.wait_ge(h_ready, 24)
            pool.memset(zc[:, :, :, :], 0.0).then_inc(pool_init, 1)
            for m in range(DC):
                pool.wait_ge(prod_ready, POOL_TAPS * (m + 1))
                pr = prod[:, m % 2]
                q = POOL_TAPS // 4
                pool.tensor_tensor(pr[:, 0:2 * q], pr[:, 0:2 * q], pr[:, 2 * q:4 * q], ALU.add).then_inc(pool_tap, 1)
                pool.wait_ge(pool_tap, 4 * m + 1)
                pool.tensor_tensor(pr[:, 0:q], pr[:, 0:q], pr[:, q:2 * q], ALU.add).then_inc(pool_tap, 1)
                pool.wait_ge(pool_tap, 4 * m + 2)
                pool.tensor_tensor(pr[:, 0], pr[:, 0], pr[:, 1], ALU.add).then_inc(pool_tap, 1)
                pool.wait_ge(pool_tap, 4 * m + 3)
                pool.tensor_tensor(acq[:, m, :], pr[:, 0], pr[:, 2], ALU.add).then_inc(pool_tap, 1)
            rests(1)

        @block.scalar
        def _(act):
            st = Steps(act, a_step)
            norm_n = [0]

            def mod_evac(k):
                act.wait_ge(dense_used, dense(POS["mod%d" % k] + 7))
                if k >= 2:
                    act.wait_ge(row_mm, k - 1)
                for hf in range(2):
                    ins = act.activation(mrow[:, (k % 2) * D + hf * 512:(k % 2) * D + (hf + 1) * 512],
                                         bank[2 * (k % 2) + hf][0:2, :], ACT.Copy)
                ins.then_inc(row_ready, 1)

            def round_tile(l, e, it=None):
                n = POS["peer%d" % l] + e
                r, p_ = n % RING, (SEQ_TILES * l + e) % SPLIT
                i = 0 if it is None else it
                act.wait_ge(w_land[r], val(i, 16, 16 * (n // RING + 1)))
                act.wait_ge(tile_used, val(i, 4, SEQ_TILES * l + e + 1))
                act.activation(split[:, 2 * p_ * D:(2 * p_ + 1) * D], ring[:, r * D:(r + 1) * D], ACT.Copy)\
                   .then_inc(hi_ready, 1)

            def in_round(m):
                n = POS["in"] + m
                act.wait_ge(w_land[n % RING], 16 * (n // RING + 1))
                o = m % IN_SPLIT * 2 * D
                act.activation(in_split[:, o:o + D], ring[:, n % RING * D:(n % RING + 1) * D], ACT.Copy)\
                   .then_inc(in_hi, 1)

            def norm_act(l, which, ready=None, count=None):
                u = norm_n[0]
                norm_n[0] += 1
                sq3, h3, root = norm_bufs(which)[:3]
                for c in range(DC):
                    if ready is not None:
                        act.wait_ge(ready, count(c))
                    act.activation(sq3[:, c, :], x3[:, c, :], ACT.Square).then_inc(sq_ready, 1)
                act.wait_ge(ss_ready, u + 1)
                act.activation(root, bank[0][:, 0:T], ACT.Sqrt, bias=epsb[:, 0:1]).then_inc(rt_ready, 1)
                if which < 2:
                    act.wait_ge(mod_ready, 2 * l + which + 1)
                    if (l, which) == (0, 0):
                        for m in range(IN_SPLIT):
                            in_round(m)
                    if which == 1 and l == 0:
                        act.wait_ge(s_out, 32)
                    if which == 1:
                        for e in range(EARLY):
                            round_tile(l, e)
                    for c in range(DC):
                        act.wait_ge(xn_ready, DC * u + c + 1)
                        a, b = GROUPS[1]
                        act.activation(h3[:, c, a:b], sq3[:, c, a:b], ACT.Identity,
                                       scale=scale5[:, l, which, c, 1:2],
                                       bias=mod4[:, l, 24 * which + c, 1:2]).then_inc(h_ready, 1)
                        if (l, which) == (0, 0):
                            act.wait_ge(h_ready, c + 1)
                            act.activation(in_hp[:, 0, c], h3[:, c], ACT.Copy).then_inc(in_h_hi, 1)
                        if which == 1:
                            act.wait_ge(h_ready, DC * (2 * l + 1) + c + 1)
                            act.activation(hp4[:, 0, c], ph[:, c], ACT.Copy).then_inc(hi_h, 1)

            act.sem_inc(gelu_done, 2)
            act.wait_ge(s_small, 16)
            act.activation(silc[:, :], sm("cvec"), ACT.Silu).then_inc(silc_ready, 1)
            act.wait_ge(pool_init, 6)
            for k in range(6):
                mod_evac(k)
            act.wait_ge(s_x, 32)
            norm_act(0, 0)
            for m in range(IN_CH):
                act.wait_ge(dense_used, dense(POS["in"] + m))
                if m + IN_SPLIT < IN_CH:
                    in_round(m + IN_SPLIT)
                ps = bank[m % 4]
                if m < A_CH:
                    st.mark(act.activation(zp[:, m, 1:1 + T_CTX], ps[:, 0:T_CTX], ACT.Copy))
                    act.activation(zp[:, m, 1 + LAT0:1 + TS], ps[:, T_CTX:T], ACT.Copy).then_inc(z_evac, 1)
                else:
                    dst = gu[:, m - 15, :] if m < 19 else gv[:, m - 19, :]
                    act.activation(dst, ps[:, 0:T], ACT.Copy).then_inc(z_evac, 1)
            for g in range(4):
                act.wait_ge(st_in, g + 1)
                act.activation(gs[:, g, :], gc[:, g, :], ACT.Square).then_inc(act_ready, 1)
            for g in range(4):
                act.wait_ge(st_mm, 4 + g + 1)
                act.activation(gs[:, g, :], bank[4 + g][:, 0:T], ACT.Sqrt, bias=epsb[:, 1:2]).then_inc(st_rt, 1)
            mod_evac(6)
            for g in range(4):
                act.wait_ge(gm_t, g + 1)
                act.activation(gtok[:, g * T:(g + 1) * T], bank[g][:, 0:T], ACT.Copy).then_inc(gm_te, 1)
            act.wait_ge(zs_ready, A_CH)
            act.wait_ge(gm_ev, 4)
            act.activation(th, zs[:, 12, :], ACT.Tanh).then_inc(act_ready, 1)
            act.activation(sg, zs[:, 14, :], ACT.Sigmoid).then_inc(act_ready, 1)
            act.wait_ge(kk_sq, 1)
            act.activation(tmp2, nkk, ACT.Square).then_inc(act_ready, 1)
            mod_evac(7)
            for p in range(4):
                act.wait_ge(kk_ss, p + 1)
                act.activation(tmp1[:, p, :], bank[p][:, 0:TS], ACT.Sqrt).then_inc(kk_rt, 1)
            for d in range(2):
                if d == 1:
                    act.wait_ge(rw_mm, RW_AT[(0, "Y", 3)] + 1)
                else:
                    act.wait_ge(lw_sum, 1)
                for p in range(4):
                    act.wait_ge(lw_mm, 8 * d + 2 * p + 1)
                    act.activation(tmp1[:, p, :], bank[p][:, 0:TS], ACT.Sigmoid,
                                   bias=sm("w0", 4 * d + p, 4 * d + p + 1)).then_inc(lw_ev, 1)
                    act.wait_ge(lw_mm, 8 * d + 2 * p + 2)
                    act.activation(tmp2[:, p, :], bank[4 + p][:, 0:TS], ACT.Sigmoid,
                                   bias=sm("a0", 4 * d + p, 4 * d + p + 1)).then_inc(lw_ev, 1)
                act.wait_ge(lw_sum, 2 * d + 2)
                act.activation(rt_, tmp3, ACT.Exp, scale=-DECAY).then_inc(ex_ready, 1)
                act.activation(kt_, tmp3, ACT.Exp, scale=DECAY).then_inc(ex_ready, 1)
                act.wait_ge(lw_sum, 2 * d + 3)
                act.activation(at_, tmp1, ACT.Exp, scale=-DECAY).then_inc(ex_ready, 1)
                mod_evac(8 + d)
                for j, (dd, name, g, e) in enumerate(RW_JOBS):
                    if dd != d or e != "A":
                        continue
                    act.wait_ge(rw_mm, j + 1)
                    ps = bank[j % 8]
                    if name == "VTOK":
                        dst = vtok[:, g * 512:(g + 1) * 512]
                    elif name == "BTOK":
                        dst = btok[:, g * 512:(g + 1) * 512]
                    elif name == "KTOK":
                        dst = ktok[:, g * 512:(g + 1) * 512]
                    elif name[0] == "F":
                        dst = fm[:, g * 512:(g + 1) * 512]
                    elif name[:2] == "TR":
                        dst = dm[:, g * 512:(g + 1) * 512]
                    elif name == "X":
                        dst = xs_[:, :]
                    else:
                        dst = us_[:, :]
                    if name in ("X", "U"):
                        w = 256 * len(SCAN[d][g])
                        act.activation(dst[:, 0:w], ps[:, 0:w], ACT.Copy).then_inc(rw_evA, 1)
                    else:
                        act.activation(dst, ps[:, :], ACT.Copy).then_inc(rw_evA, 1)
            act.wait_ge(st_in, 5)
            act.activation(gq, gy, ACT.Square).then_inc(act_ready, 1)
            for p in range(4):
                act.wait_ge(st_mm, 12 + p + 1)
                act.activation(gmean[:, p, :], bank[4 + p][:, 0:TS], ACT.Sqrt, bias=epsb[:, 2:3]).then_inc(st_rt, 1)
            norm_act(0, 1, res_done, lambda c: c + 1)

            def peer_act(l):
                E0, U0, V0, M0 = SEQ_TILES * l, NK * l, NK * l, NK * l
                for e in range(EARLY, SPLIT):
                    round_tile(l, e)
                for e, (kind, j) in enumerate(START):
                    act.wait_ge(tile_used, E0 + e + 1 + SPLIT)
                    if kind == "q":
                        if j >= 2:
                            act.wait_ge(s_mm, 16 * l + j - 1)
                        act.activation(q_sb[:, j % 2, :], bank[j % 2][:, 0:T], ACT.Copy).then_inc(q_evac, 1)
                    else:
                        act.activation(buf4[:, 0, j, :], bank[6 + j % 2][:, 0:T], ACT.Gelu).then_inc(gelu_done, 1)
                    round_tile(l, e + SPLIT)
                    if 1 <= e <= 16:
                        scores(l, e - 1)
                    if e == N_START - 8:
                        act.wait_ge(cand_max, l + 1)
                        act.activation(ge, ge, ACT.Exp).then_inc(e_ready, 1)
                for k in range(3):
                    act.wait_ge(route_t, 3 * l + k + 1)
                    act.activation(routeT[:, k, :] if k < 2 else gateT[:, 0, :], bank[2 + k][:, 0:T], ACT.Copy)\
                           .then_inc(route_e, 1)
                for first, uq, vq, gq_ in PHASES:
                    w = 2 if uq is not None and vq is not None else 1
                    steps = 4 // w
                    H0 = 2 * JQ * l + JQ * (vq or 0)

                    def coef_hi(i, s):
                        v = val(i, steps, V0 + vq * JQ + s)
                        sl = s % 2
                        act.activation(cp4[:, sl, 0, :],
                                       buf4[:, vq % 2, bass.ds(val(i, steps, s), 1), :].rearrange("p o t -> p (o t)"),
                                       ACT.Copy).then_inc(chi, 1)

                    def body(i, last):
                        for s in range(steps):
                            e = first + w * s
                            if uq is not None:
                                act.wait_ge(tile_used, val(i, 4, E0 + e + 1 + SPLIT))
                                if vq is not None:
                                    act.wait_ge(clo, val(i, steps, V0 + vq * JQ + s + 1))
                                round_tile(l, e + SPLIT, it=i)
                                ub = 6 if vq is not None else (6, 5)[s % 2]
                                act.activation(buf4[:, uq % 2, bass.ds(val(i, steps, s), 1), :]
                                               .rearrange("p o t -> p (o t)"), bank[ub][:, 0:T], ACT.Gelu)\
                                   .then_inc(gelu_done, 1)
                                e += 1
                            if vq is not None:
                                if not (last and s == steps - 1):
                                    coef_hi(i, s + 1)
                                if not (last and vq == QT - 1):
                                    act.wait_ge(tile_used, val(i, 4, E0 + e + 1 + SPLIT))
                                    round_tile(l, e + SPLIT, it=i)
                                else:
                                    act.wait_ge(tile_used, val(i, 4, E0 + e + 1 + SPLIT))

                    if vq is not None:
                        act.wait_ge(mult_done, M0 + (vq + 1) * JQ + 2)
                        coef_hi(0, 0)
                    n = JQ // steps
                    with act.Fori(0, n - 1) as it:
                        body(it, False)
                    body(n - 1, True)
                for b in range(3):
                    for hf in range(2):
                        act.activation(otok[:, b, hf * 512:(hf + 1) * 512], bank[2 * b + hf][:, :], ACT.Copy)\
                           .then_inc(out_evac, 1)

            def scores(l, j):
                act.wait_ge(s_mm, 16 * l + j + 1)
                if 16 * l + j >= 2:
                    act.wait_ge(s_free, 16 * l + j - 1)
                act.activation(sc_sb[:, j % 2, :, :], bank[2 + j % 2][:, 0:T].rearrange("p (b k) -> p b k", k=P),
                               ACT.Copy).then_inc(s_evac, 1)

            peer_act(0)
            norm_act(1, 0, out_used, lambda c: 2 * c + 2)
            for m in range(8):
                act.wait_ge(dense_used, dense(POS["pw1"] + 2 * m + 1))
                act.activation(glug[:, m % 2, :], bank[2 * (m % 2) + 1][:, 0:T], ACT.Sigmoid,
                               bias=sm("b_pw1", 8 + m, 9 + m)).then_inc(glu_g, 1)
                act.wait_ge(glu_done, m + 1)
                act.activation(zc[:, m, 0, HALO + ROW:ROWP], zc[:, m, 1, HALO:2 * HALO], ACT.Copy)\
                   .then_inc(halo_done, 1)
                act.activation(zc[:, m, 1, 0:HALO], zc[:, m, 0, ROW:HALO + ROW], ACT.Copy).then_inc(halo_done, 1)
                act.wait_ge(halo_done, 2 * m + 2)
                if m >= 2:
                    act.wait_ge(pool_tap, 4 * m - 4)
                with act.Fori(0, POOL_TAPS // TAP_STEP) as it:
                    for t in range(TAP_STEP):
                        w = DVE_TAPS + t
                        act.activation(prod[:, m % 2, bass.ds(it * TAP_STEP + t, 1), :].rearrange(
                                           "p o (r t) -> p (o r) t", t=ROW),
                                       zc[:, m, :, bass.ds(it * TAP_STEP + w, ROW)], ACT.Copy,
                                       scale=small[:, bass.ds(it * (DC * TAP_STEP) + (SM["conv_k"][0] + DC * w + m),
                                                              1)]).then_inc(prod_ready, 1)
            mod_evac(10)
            for c in range(DC):
                act.wait_ge(st_in, 6 + c)
                act.activation(acq[:, c, :], accs[:, c, :], ACT.Square).then_inc(act_ready, 1)
            act.wait_ge(st_mm, 18)
            act.activation(lroot, bank[5][:, 0:T], ACT.Sqrt, bias=epsb[:, 1:2]).then_inc(st_rt, 1)
            for c in range(DC):
                act.wait_ge(st_in, 14 + c)
                act.activation(h3[:, c, :], accs[:, c, :], ACT.Silu, scale=sm("lnc_g", c, c + 1),
                               bias=sm("lnc_b", c, c + 1)).then_inc(conv_act, 1)
            mod_evac(11)
            for m in range(8):
                act.wait_ge(dense_used, dense(POS["pw2"] + m))
                if m >= 2:
                    act.wait_ge(res_done, DC + m - 1)
                act.activation(pw2t[:, m % 2, :], bank[m % 4][:, 0:T], ACT.Identity,
                               bias=sm("b_pw2", m, m + 1)).then_inc(pw2_ev, 1)
            norm_act(1, 1, res_done, lambda c: DC + c + 1)
            peer_act(1)
            norm_act(0, 2, out_used, lambda c: 16 + 2 * c + 2)

        @block.tensor
        def _(pe):
            norm_n = [0]

            def landed(n):
                pe.wait_ge(w_land[n % RING], 16 * (n // RING + 1))

            def wt(n, c):
                o = (n % RING) * D + c * P
                return ring[:, o:o + P]

            def norm_pe(which=0):
                sq3 = norm_bufs(which)[0]
                u = norm_n[0]
                norm_n[0] += 1
                for c in range(DC):
                    pe.wait_ge(sq_ready, DC * u + c + 1)
                    mm = pe.matmul(bank[0][:, 0:T], sm("mean_d"), sq3[:, c, :], start=(c == 0), stop=(c == DC - 1))
                mm.then_inc(ss_ready, 1)

            def linear(n, out, rhs, ready=None, before=0):
                landed(n)
                for c in range(DC):
                    if ready is not None:
                        pe.wait_ge(ready, before + c + 1)
                    mm = pe.matmul(out, wt(n, c), rhs[c], start=(c == 0), stop=(c == DC - 1))
                mm.then_inc(dense_used, 1)

            hs = [h3[:, c, :] for c in range(DC)]
            pe.sem_inc(tok_mm, 2)
            pe.sem_inc(tile_used, SPLIT)
            pe.wait_ge(silc_ready, 1)
            sil = silc[:, :].rearrange("p (c g) -> p c g", g=2)

            def mod_rows(k):
                if k >= 2:
                    pe.wait_ge(row_ready, k - 1)
                for c in range(DC):
                    n = POS["mod%d" % k] + c
                    landed(n)
                    for hf in range(2):
                        o = (n % RING) * D + hf * 512
                        mm = pe.matmul(bank[2 * (k % 2) + hf][0:2, :], sil[:, c, :], ring[:, o:o + 512],
                                       start=(c == 0), stop=(c == DC - 1))
                    mm.then_inc(dense_used, 1)

            def mod_turn(k):
                pe.wait_ge(row_ready, k + 1)
                if k >= 1:
                    pe.wait_ge(mod_added, k)
                for c in range(8):
                    o = MOD_COL + 2 * c
                    mm = pe.matmul(bank[7][:, o:o + 2], mrow[:, (k % 2) * D + c * P:(k % 2) * D + (c + 1) * P],
                                   sm("ident", 0, 2)[0:2], start=True, stop=True)
                mm.then_inc(row_mm, 1)

            for k in range(6):
                mod_rows(k)
                if k >= 1:
                    mod_turn(k - 1)
            mod_turn(5)
            norm_pe()
            for m in range(IN_CH):
                if m >= 4:
                    pe.wait_ge(z_evac, m - 3)
                pe.wait_ge(in_lo, m + 1)
                for c in range(DC):
                    if m == 0:
                        pe.wait_ge(in_h_lo, c + 1)
                    for x, y in PARTS:
                        o = (m % IN_SPLIT * 2 + x) * D + c * P
                        mm = pe.matmul(bank[m % 4][:, 0:T], in_split[:, o:o + P], in_hp[:, y, c, :],
                                       start=(c == 0 and x == 0 and y == 0), stop=(c == DC - 1 and x == 1))
                mm.then_inc(dense_used, 1)
            pe.wait_ge(z_evac, IN_CH)
            pe.wait_ge(s_mixer, 32)
            for g in range(4):
                pe.matmul(bank[g][:, 0:T], sm("mean_p"), gv[:, g, :], start=True, stop=True).then_inc(st_mm, 1)
            for g in range(4):
                pe.wait_ge(act_ready, g + 1)
                pe.matmul(bank[4 + g][:, 0:T], sm("mean_p"), gs[:, g, :], start=True, stop=True).then_inc(st_mm, 1)
            pe.wait_ge(st_in, 4)
            mod_rows(6)
            pe.wait_ge(row_ready, 7)
            for g in range(4):
                pe.wait_ge(gm_norm, g + 1)
                for b in range(3):
                    mm = pe.transpose(bank[g][:, b * P:(b + 1) * P], gc[:, g, b * P:(b + 1) * P], sm("ident"))
                mm.then_inc(gm_t, 1)
            for g in range(4):
                pe.wait_ge(gm_te, g + 1)
                for b in range(3):
                    out = bank[4 + g][:, b * P:(b + 1) * P]
                    pe.matmul(out, gtok[:, g * T + b * P:g * T + (b + 1) * P], sm("w_sT", g * P, (g + 1) * P),
                              start=True, stop=False)
                    mm = pe.matmul(out, sm("ones")[0:1], sm("b_s", g * P, (g + 1) * P)[0:1], start=False,
                                   stop=True)
                mm.then_inc(gm_mm, 1)
            mod_rows(7)
            pe.wait_ge(act_ready, 7)
            pe.wait_ge(gm_ev, 4)
            pe.wait_ge(row_ready, 8)
            for p in range(4):
                pe.matmul(bank[p][:, 0:TS], sm("head_sum"), tmp2[:, p, :], start=True, stop=True).then_inc(kk_ss, 1)
            mod_turn(6)
            mod_turn(7)
            pe.wait_ge(mod_added, 8)

            def H(hp):
                return slice(hp * 64, hp * 64 + 64)

            for d in range(2):
                q = slice(d * 64, d * 64 + 64)
                if d == 0:
                    pe.wait_ge(kk_rt, 4)
                else:
                    pe.wait_ge(rw_evA, RW_EV[RW_AT[(0, "U", 3)]][1])
                    pe.wait_ge(rw_evV, RW_EV[RW_AT[(0, "Y", 3)]][1])
                for p in range(4):
                    pe.matmul(bank[p][:, 0:TS], sm("w2", p * P, (p + 1) * P)[q], th[q], start=True, stop=True)\
                      .then_inc(lw_mm, 1)
                    pe.matmul(bank[4 + p][:, 0:TS], sm("a2", p * P, (p + 1) * P)[q], zs[q, 13, :], start=True,
                              stop=True).then_inc(lw_mm, 1)
                pe.wait_ge(lw_ev, 8 * d + 8)
                mod_rows(8 + d)
                mod_turn(8 + d)
                pe.wait_ge(sc_ready, d + 1)
                pe.wait_ge(mod_added, 9 + d)
                eye = sm("eye64")
                for j, (dd, name, g, e) in enumerate(RW_JOBS):
                    if dd != d:
                        continue
                    if j >= 8:
                        who, cnt = RW_EV[j - 8]
                        pe.wait_ge(rw_evA if who == "A" else rw_evV, cnt)
                    ps = bank[j % 8]

                    def unit(a, w, hp):
                        return a[H(hp), g * 512 + w * 64:g * 512 + w * 64 + 64]

                    def tok(a, w, hp):
                        c0 = tcol(2 * g + w // 4)
                        return a[H(hp), w % 4, c0:c0 + 64]

                    if name in ("X", "U", "S", "Y"):
                        s = g
                        for ci, (chain, c) in enumerate(SCAN[d][s]):
                            which = 0 if chain == "lat" else 1
                            g3, w0 = c // 2, (c % 2) * 4
                            for p in range(4):
                                w = w0 + p
                                c0 = tcol(c)
                                col = (ci * 4 + p) * 64
                                for hp in range(2):
                                    hh = H(hp)
                                    out = ps[hh, col:col + 64]
                                    so = (which * 2 + s % 2) * 256 + p * 64
                                    s_in = state[hh, so:so + 64]

                                    def un(a):
                                        return a[hh, g3 * 512 + w * 64:g3 * 512 + w * 64 + 64]

                                    if name == "X":
                                        if p == 0 and hp == 0 and ci == 0:
                                            pe.wait_ge(rw_evA, RW_EV[RW_AT[(d, "KTOK", 2)]][1])
                                            if s > 0:
                                                pe.wait_ge(rw_evV, RW_EV[RW_AT[(d, "S", s - 1)]][1])
                                        pe.matmul(out, at_[hh, p, c0:c0 + 64], s_in, start=True, stop=False)
                                        mm = pe.matmul(out, un(lak), un(vtok), start=False, stop=True)
                                    elif name == "U":
                                        if p == 0 and hp == 0 and ci == 0:
                                            pe.wait_ge(rw_evA, RW_EV[RW_AT[(d, "X", s)]][1])
                                        mm = pe.matmul(out, un(dT), xs_[hh, col:col + 64], start=True, stop=True)
                                    elif name == "S":
                                        if p == 0 and hp == 0 and ci == 0:
                                            pe.wait_ge(rw_evA, RW_EV[RW_AT[(d, "U", s)]][1])
                                        pe.matmul(out, un(btok), us_[hh, col:col + 64], start=True, stop=False)
                                        mm = pe.matmul(out, un(ktok), un(vtok), start=False, stop=True)
                                    else:
                                        pe.matmul(out, s_in, rt_[hh, p, c0:c0 + 64], start=True, stop=False)
                                        pe.matmul(out, us_[hh, col:col + 64], un(mrb), start=False, stop=False)
                                        mm = pe.matmul(out, un(vtok), un(mrk), start=False, stop=True)
                        mm.then_inc(rw_mm, 1)
                        continue
                    if name == "D0":
                        pe.wait_ge(lt_ready, 18 * d + g + 1)
                    if name[0] == "F":
                        lev = LEVELS.index(int(name[1:]))
                        pe.wait_ge(lt_ready, 18 * d + 3 * (lev + 1) + g + 1)
                        if lev:
                            pe.wait_ge(rw_evA, RW_EV[RW_AT[(d, "TR%d" % LEVELS[lev - 1], g)]][1])
                    if name[:2] == "GT":
                        pe.wait_ge(rw_evA, RW_EV[RW_AT[(d, "F" + name[2:], g)]][1])
                    if name[:2] == "TR":
                        pe.wait_ge(rw_evV, RW_EV[RW_AT[(d, "GT" + name[2:], g)]][1])
                    if name in ("BTOK", "KTOK"):
                        pe.wait_ge(rw_evV, RW_EV[RW_AT[(d, "GT32", 2)]][1])
                    for w in range(8):
                        for hp in range(2):
                            out = ps[H(hp), w * 64:w * 64 + 64]
                            if name == "LT":
                                a, b = tok(bt_, w, hp), tok(at_, w, hp)
                            elif name == "LAK":
                                a, b = tok(kt_, w, hp), tok(at_, w, hp)
                            elif name == "MRB":
                                a, b = tok(bt_, w, hp), tok(rt_, w, hp)
                            elif name == "MRK":
                                a, b = tok(kt_, w, hp), tok(rt_, w, hp)
                            elif name == "VTOK":
                                a, b = zs[H(hp), 8 + w % 4, tcol(2 * g + w // 4):tcol(2 * g + w // 4) + 64], eye[H(hp)]
                            elif name == "BTOK":
                                a, b = tok(bt_, w, hp), eye[H(hp)]
                            elif name == "KTOK":
                                a, b = tok(kt_, w, hp), eye[H(hp)]
                            elif name == "D0":
                                a, b = unit(em, w, hp), eye[H(hp)]
                            elif name[0] == "F":
                                a, b = unit(em, w, hp), unit(dm, w, hp)
                            elif name[:2] == "GT":
                                a, b = unit(fm, w, hp), unit(dT, w, hp)
                            else:
                                a, b = unit(dT, w, hp), eye[H(hp)]
                            if hp == 0 and (name == "D0" or name[:2] == "TR" or name[1:] == "TOK"):
                                mm = pe.transpose(out, a, b)
                            else:
                                mm = pe.matmul(out, a, b, start=True, stop=True)
                    mm.then_inc(rw_mm, 1)
            pe.wait_ge(rw_evV, RW_EV[RW_AT[(1, "Y", 3)]][1])
            pe.wait_ge(rw_evA, RW_EV[RW_AT[(1, "U", 3)]][1])
            for p in range(4):
                pe.matmul(bank[p][:, 0:TS], sm("head_mean"), ysum[:, p, :], start=True, stop=True).then_inc(st_mm, 1)
            pe.wait_ge(act_ready, 8)
            for p in range(4):
                pe.matmul(bank[4 + p][:, 0:TS], sm("head_mean"), gq[:, p, :], start=True, stop=True)\
                  .then_inc(st_mm, 1)
            pe.wait_ge(sc_ready, 3)
            for p in range(4):
                pe.matmul(bank[p][:, 0:TS], sm("head_sum"), tmp0[:, p, :], start=True, stop=True).then_inc(kk_ss, 1)
            pe.wait_ge(st_rt, 8)
            for p in range(4):
                pe.matmul(bank[4 + p][:, 0:TS], sm("g2", p * P, (p + 1) * P), sg, start=True, stop=True)\
                  .then_inc(kk_ss, 1)
            pe.wait_ge(bonus_read, 4)
            for m in range(RING):
                n = POS["out"] + m
                landed(n)
                for c in range(4, DC):
                    pe.matmul(bank[m][:, 0:T], wt(n, c), yb[:, c - 4, :], start=(c == 4), stop=False)
            for m in range(RING):
                for c in range(4):
                    if m == 0:
                        pe.wait_ge(mix_ready, c + 1)
                    mm = pe.matmul(bank[m][:, 0:T], wt(POS["out"] + m, c), ya3[:, c * T:(c + 1) * T], start=False,
                                   stop=(c == 3))
                mm.then_inc(dense_used, 1)
            ys = [ya3[:, c * T:(c + 1) * T] for c in range(4)] + [yb[:, c, :] for c in range(4)]
            for m in range(RING, 8):
                linear(POS["out"] + m, bank[m][:, 0:T], ys)
            norm_pe(1)
            pe.wait_ge(res_done, 8)

            def peer_pe(l):
                E0, U0, V0, M0 = SEQ_TILES * l, NK * l, NK * l, NK * l

                def part(e, x, a, b):
                    o = (2 * ((E0 + e) % SPLIT) + x) * D
                    return split[:, o + a:o + b]

                def product(e, out, chunks):
                    for c in chunks:
                        for x, y in PARTS:
                            mm = pe.matmul(out, part(e, x, c * P, (c + 1) * P), hp4[:, y, c, :],
                                           start=(c == 0 and x == 0 and y == 0), stop=(c == DC - 1 and x == 1))
                    return mm

                def score(j):
                    c = j % 2
                    pe.wait_ge(q_evac, 16 * l + j + 1)
                    if 16 * l + j >= 2:
                        pe.wait_ge(s_evac, 16 * l + j - 1)
                    for b in range(3):
                        mm = pe.matmul(bank[2 + j % 2][:, b * P:(b + 1) * P], q_sb[:, j % 2, b * P:(b + 1) * P],
                                       sm("sk", (2 * l + c) * P, (2 * l + c + 1) * P), start=True, stop=True)
                    mm.then_inc(s_mm, 1)

                for e, (kind, j) in enumerate(START):
                    pe.wait_ge(lo_ready, E0 + e + 1)
                    if e == 0:
                        for c in range(DC - 1):
                            pe.wait_ge(lo_h, DC * l + c + 1)
                            product(e, bank[0][:, 0:T], [c])
                        pe.wait_ge(lo_h, DC * l + DC)
                        product(e, bank[0][:, 0:T], [DC - 1]).then_inc(tile_used, 1)
                        continue
                    if kind == "q":
                        if j >= 2:
                            pe.wait_ge(q_evac, 16 * l + j - 1)
                        product(e, bank[j % 2][:, 0:T], range(DC)).then_inc(tile_used, 1)
                    else:
                        pe.wait_ge(gelu_done, U0 + j + 1)
                        product(e, bank[6 + j % 2][:, 0:T], range(DC)).then_inc(tile_used, 1)
                    if 1 <= e <= 16:
                        score(e - 1)
                pe.wait_ge(route, 7 * l + 7)
                for k in range(3):
                    for b in range(3):
                        mm = pe.transpose(bank[2 + k][:, b * P:(b + 1) * P], routes[:, k, b, :], sm("ident"))
                    mm.then_inc(route_t, 1)

                for first, uq, vq, gq_ in PHASES:
                    w = 2 if uq is not None and vq is not None else 1
                    steps = 4 // w
                    H0 = 2 * JQ * l + JQ * (vq or 0)
                    if vq == 0:
                        pe.wait_ge(gelu_done, U0 + 2 * JQ + 2)
                        pe.wait_ge(mult_done, M0 + JQ + 2)
                        for b in range(6):
                            pe.matmul(bank[b][:, :], sm("zeros"), x_sb[:, 0:512], start=True, stop=True)

                    def tokens(i, s):
                        gb = 7 if (vq is not None) else (7, 4)[s % 2]
                        pe.wait_ge(mult_done, val(i, steps, M0 + gq_ * JQ + s + (2 if vq is not None else 1)))
                        pe.wait_ge(oh_ready, val(i, 2 * steps, 2 * (M0 + gq_ * JQ + s + 1)))
                        for x in range(GRP):
                            for y in range(3):
                                mm = pe.matmul(bank[gb][:, x * JQ:(x + 1) * JQ], oh_i[:, s % 2, x, :],
                                               oh_g[:, x, y, :], start=(y == 0), stop=(y == 2))
                        mm.then_inc(tok_mm, 1)

                    def half_tokens(i, s, h):
                        g = M0 + gq_ * JQ + s
                        if h == 0:
                            pe.wait_ge(mult_done, val(i, steps, g + 2))
                            pe.wait_ge(oh_ready, val(i, 2 * steps, 2 * (g + 1)))
                        else:
                            pe.wait_ge(half_done, val(i, steps, H0 + s + 1))
                        for x in range(GRP // 2):
                            o, t = x * 2 * JQ, h * GRP // 2 + x
                            pe.matmul(bank[7][:, o:o + 2 * JQ], oh_i[:, s % 2, t, :],
                                      oh_g[:, t, 0:2, :].rearrange("p y j -> p (y j)"), start=True, stop=False)
                            mm = pe.matmul(bank[7][:, o:o + JQ], oh_i[:, s % 2, t, :], oh_g[:, t, 2, :],
                                           start=False, stop=True)
                        mm.then_inc(tok_mm if h else half_mm, 1)

                    def values(e, sl):
                        for b in range(3):
                            for hf in range(2):
                                for x, y in PARTS:
                                    mm = pe.matmul(bank[2 * b + hf][:, :], cp4[:, sl, x, b * P:(b + 1) * P],
                                                   part(e, y, hf * 512, (hf + 1) * 512), start=False, stop=True,
                                                   skip_group_check=True)
                        mm.then_inc(tile_used, 1)

                    def body(i):
                        for s in range(steps):
                            e = first + w * s
                            ub = 6 if vq is not None else (6, 5)[s % 2]
                            if uq is not None:
                                pe.wait_ge(lo_ready, val(i, 4, E0 + e + 1))
                                pe.wait_ge(gelu_done, val(i, steps, U0 + uq * JQ + s + (2 if vq is not None else 1)))
                                product(e, bank[ub][:, 0:T], range(DC)).then_inc(tile_used, 1)
                                if w == 2:
                                    half_tokens(i, s, 0)
                                e += 1
                            if vq is not None:
                                pe.wait_ge(lo_ready, val(i, 4, E0 + e + 1))
                                pe.wait_ge(clo, val(i, steps, V0 + vq * JQ + s + 1))
                                values(e, s % 2)
                            if w == 2:
                                half_tokens(i, s, 1)
                            elif gq_ is not None:
                                tokens(i, s)

                    if gq_ is not None:
                        pe.wait_ge(route_e, 3 * l + 3)
                    with pe.Fori(0, JQ // steps) as it:
                        body(it)
                pe.wait_ge(out_evac, 6 * l + 6)
                for c in range(DC):
                    if c >= 2:
                        pe.wait_ge(out_used, 16 * l + 2 * c - 2)
                    for b in range(3):
                        mm = pe.transpose(bank[6 + c % 2][:, b * P:(b + 1) * P], otok[:, b, c * P:(c + 1) * P],
                                          sm("ident"))
                    mm.then_inc(out_t, 1)

            peer_pe(0)
            norm_pe()

            def mean(c):
                pe.wait_ge(conv_done, c + 1)
                return pe.matmul(bank[4][:, 0:T], sm("mean_d"), acc[:, c, :], start=(c == 0), stop=(c == DC - 1))

            pe.wait_ge(out_used, 16)
            for m in range(8):
                for w in range(2):
                    if m >= 2:
                        pe.wait_ge(glu_done, m - 1)
                    linear(POS["pw1"] + 2 * m + w, bank[2 * (m % 2) + w][:, 0:T], hs,
                           h_ready if m == w == 0 else None, 2 * DC)
                if m >= 3:
                    mean(m - 3)
            pe.wait_ge(glu_done, 7)
            mod_rows(10)
            for c in range(DC - 3, DC):
                mm = mean(c)
            mm.then_inc(st_mm, 1)
            for c in range(DC):
                pe.wait_ge(act_ready, 9 + c)
                mm = pe.matmul(bank[5][:, 0:T], sm("mean_d"), acq[:, c, :], start=(c == 0), stop=(c == DC - 1))
            mm.then_inc(st_mm, 1)
            mod_turn(10)
            mod_rows(11)
            pe.wait_ge(conv_act, 8)
            mod_turn(11)
            for m in range(8):
                if m >= 4:
                    pe.wait_ge(pw2_ev, m - 3)
                linear(POS["pw2"] + m, bank[m % 4][:, 0:T], hs)
            norm_pe(1)
            pe.wait_ge(res_done, 16)
            peer_pe(1)
            norm_pe(2)

        @block.vector
        def _(dve):
            st = Steps(dve, v_step)
            norm_n = [0]
            dve.sem_inc(mult_done, 2)

            def bc(ap, shape):
                return ap.to_broadcast(shape)

            def norm_dve(l, which):
                sq3, h3, root, rstd = norm_bufs(which)
                final = which == 2
                u = norm_n[0]
                norm_n[0] += 1
                dve.wait_ge(rt_ready, u + 1)
                st.link(dve.reciprocal(rstd, root))
                if final:
                    for c in range(DC):
                        dve.scalar_tensor_tensor(h3[:, c, :], x3[:, c, :], sm("norm_f", c, c + 1), rstd,
                                                 ALU.mult, ALU.mult).then_inc(y_ready, 1)
                    return
                dve.wait_ge(mod_ready, 2 * l + which + 1)
                a, b = GROUPS[0]
                first = st.n
                for c in range(DC + 1):
                    if c < DC:
                        st.mark(dve.tensor_tensor(sq3[:, c, :], x3[:, c, :], rstd, ALU.mult))
                    if c >= 1:
                        dve.wait_ge(v_step, first + c)
                        dve.tensor_scalar(h3[:, c - 1, a:b], sq3[:, c - 1, a:b], scale5[:, l, which, c - 1, 0:1],
                                          mod4[:, l, 24 * which + c - 1, 0:1], ALU.mult, ALU.add)\
                           .then_inc(xn_ready, 1)

            def mod_add(k):
                dve.wait_ge(row_mm, k + 1)
                o = MOD_COL
                dve.tensor_tensor(modv[:, 16 * k:16 * k + 16].rearrange("p (c g) -> p c g", g=2),
                                  bank[7][:, o:o + 16].rearrange("p (c g) -> p c g", g=2),
                                  sm("b_mod", 8 * k, 8 * k + 8).unsqueeze(2).to_broadcast([P, 8, 2]), ALU.add)\
                   .then_inc(mod_added, 1)
                dve.wait_ge(mod_added, k + 1)
                l, n = k // 6, k % 6 // 3
                if k % 3 == 1:
                    dve.scalar_tensor_tensor(
                        scale5[:, l, n], mod4[:, l, 24 * n + 8:24 * n + 16], 1.0,
                        sm("norm%d" % (n + 1), 8 * l, 8 * l + 8).unsqueeze(2).to_broadcast([P, 8, 2]),
                        ALU.add, ALU.mult).then_inc(mod_ready, 1)

            for k in range(6):
                mod_add(k)
            norm_dve(0, 0)

            dve.wait_ge(pool_init, 3)
            dve.wait_ge(s_mixer, 32)
            for m in range(A_CH):
                dve.wait_ge(z_evac, m + 1)
                t = zshift[:, m % 2, :]
                z = zp[:, m, 1:1 + TS]
                st.link(dve.tensor_tensor(t, zp[:, m, 0:TS], zp[:, m, 2:2 + TS], ALU.add))
                st.link(dve.scalar_tensor_tensor(t, t, 0.5, z, ALU.mult, ALU.subtract))
                dve.scalar_tensor_tensor(zs[:, m, :], t, sm("mu", m, m + 1), z, ALU.mult, ALU.add)\
                   .then_inc(zs_ready, 1)

            for g in range(4):
                dve.wait_ge(st_mm, g + 1)
                dve.tensor_tensor(gc[:, g, :], gv[:, g, :], bank[g][:, 0:T], ALU.subtract).then_inc(st_in, 1)
            for g in range(4):
                dve.wait_ge(st_rt, g + 1)
                st.link(dve.reciprocal(gs[:, g, :], gs[:, g, :]))
                st.link(dve.tensor_tensor(gc[:, g, :], gc[:, g, :], gs[:, g, :], ALU.mult))
                dve.tensor_scalar(gc[:, g, :], gc[:, g, :], sm("lnv_g", g, g + 1), sm("lnv_b", g, g + 1),
                                  ALU.mult, ALU.add).then_inc(gm_norm, 1)
            for g in range(4):
                dve.wait_ge(gm_mm, g + 1)
                dve.tensor_tensor(yb[:, g, :], gu[:, g, :], bank[4 + g][:, 0:T], ALU.mult).then_inc(gm_ev, 1)

            dve.wait_ge(zs_ready, A_CH)
            for p in range(4):
                ins = dve.tensor_scalar(nkk[:, p, :], zs[:, 4 + p, :], sm("k_k", p, p + 1), None, ALU.mult)
            ins.then_inc(kk_sq, 1)
            mod_add(6)
            mod_add(7)
            dve.wait_ge(kk_rt, 4)
            st.link(dve.tensor_scalar(tmp1, tmp1, 1e-12, None, ALU.max))
            st.link(dve.reciprocal(tmp1, tmp1))
            dve.scalar_tensor_tensor(nkk, nkk, -1.0, tmp1, ALU.mult, ALU.mult).then_inc(lw_sum, 1)
            dve.memset(ysum[:, :, T_CTX:LAT0], 0.0)

            for d in range(2):
                dve.wait_ge(lw_ev, 8 * d + 8)
                step = 1 if d == 0 else -1
                for p in range(4):
                    ins = dve.tensor_tensor_scan(tmp3[:, p, ::step], sm("keep", d * TS, (d + 1) * TS)[:, ::step],
                                                 tmp1[:, p, ::step], 0.0, ALU.mult, ALU.add)
                ins.then_inc(lw_sum, 1)
                dve.wait_ge(lw_sum, 2 * d + 2)
                dve.tensor_tensor(tmp1, tmp3, tmp1, ALU.subtract).then_inc(lw_sum, 1)
                st.mark(dve.scalar_tensor_tensor(bt_, nkk, -1.0, tmp2, ALU.mult, ALU.mult))
                st.settle()
                for p in range(4):
                    st.mark(dve.tensor_scalar(tmp2[:, p, :], tmp2[:, p, :], -1.0, sm("k_a", p, p + 1),
                                              ALU.add, ALU.mult))
                st.settle()
                st.link(dve.scalar_tensor_tensor(tmp2, tmp2, 1.0, zs[:, 4:8, :], ALU.add, ALU.mult))
                if d == 0:
                    st.link(dve.tensor_copy(kdsum, tmp2))
                else:
                    st.link(dve.tensor_tensor(kdsum, kdsum, tmp2, ALU.add))
                st4 = state.rearrange("p (w s x) -> p w s x", w=2, s=2)
                st.mark(dve.tensor_copy(st4[:, 0, 0, :], sm("s0", d * 256, d * 256 + 256)))
                st.mark(dve.memset(st4[:, 1, 0, :], 0.0))
                dve.wait_ge(ex_ready, 3 * d + 3)
                off = CHUNK - 1 if d == 0 else 0
                pC3 = pC.rearrange("p (c q) -> p c q", q=4)
                st.mark(dve.tensor_copy(pC3[:, 0:2, :], rt_[:, :, off:T_CTX:CHUNK].rearrange("p q c -> p c q")))
                st.mark(dve.tensor_copy(pC3[:, 2:6, :], rt_[:, :, LAT0 + off:TS:CHUNK].rearrange("p q c -> p c q")))
                st.mark(dve.tensor_tensor(bt_, bt_, kt_, ALU.mult))
                st.settle()
                dve.tensor_tensor(rt_, rt_, zs[:, 0:4, :], ALU.mult)
                dve.tensor_tensor(kt_, kt_, tmp2, ALU.mult)
                dve.tensor_tensor(at_, at_, nkk, ALU.mult).then_inc(sc_ready, 1)

                mod_add(8 + d)
                strict = sm("strict", 64 * d, 64 * d + 64).unsqueeze(1).to_broadcast([P, 8, 64])
                incl = sm("incl", 64 * d, 64 * d + 64).unsqueeze(1).to_broadcast([P, 8, 64])
                eye = sm("eye64").unsqueeze(1).to_broadcast([P, 8, 64])

                def band(lev):
                    o = (d * 6 + lev) * 64
                    return sm("bands", o, o + 64).unsqueeze(1).to_broadcast([P, 8, 64])

                for j, (dd, name, g, e) in enumerate(RW_JOBS):
                    if dd != d or e != "V":
                        continue
                    dve.wait_ge(rw_mm, j + 1)
                    ps = bank[j % 8]
                    ps3 = ps[:, :].rearrange("p (w t) -> p w t", t=64)

                    def grp(a):
                        return a[:, g * 512:(g + 1) * 512].rearrange("p (w t) -> p w t", t=64)

                    if name == "LT":
                        dve.tensor_tensor(grp(ltm), ps3, strict, ALU.mult).then_inc(rw_evV, 1)
                        dve.wait_ge(rw_evV, RW_EV[j][1])
                        dve.tensor_tensor(grp(em), grp(ltm), band(0), ALU.mult).then_inc(lt_ready, 1)
                    elif name == "LAK":
                        dve.tensor_tensor(grp(lak), ps3, strict, ALU.mult).then_inc(rw_evV, 1)
                    elif name == "MRB":
                        dve.tensor_tensor(grp(mrb), ps3, incl, ALU.mult).then_inc(rw_evV, 1)
                    elif name == "MRK":
                        dve.tensor_tensor(grp(mrk), ps3, incl, ALU.mult).then_inc(rw_evV, 1)
                    elif name == "D0":
                        dve.wait_ge(lt_ready, 18 * d + g + 1)
                        st.mark(dve.tensor_tensor(grp(dm), ps3, eye, ALU.add))
                        dve.tensor_tensor(grp(dT), grp(em), eye, ALU.add).then_inc(rw_evV, 1)
                        dve.wait_ge(rw_evV, RW_EV[j][1])
                        dve.tensor_tensor(grp(em), grp(ltm), band(1), ALU.mult).then_inc(lt_ready, 1)
                    elif name[:2] == "GT":
                        lev = LEVELS.index(int(name[2:]))
                        dve.tensor_tensor(grp(dT), grp(dT), ps3, ALU.add).then_inc(rw_evV, 1)
                        if lev + 1 < len(LEVELS):
                            dve.tensor_tensor(grp(em), grp(ltm), band(lev + 2), ALU.mult).then_inc(lt_ready, 1)
                    elif name == "S":
                        s = g
                        n = len(SCAN[d][s])
                        for ci, (chain, c) in enumerate(SCAN[d][s]):
                            which = 0 if chain == "lat" else 1
                            if chain == "ctx" and s == 1:
                                dst = sm("s0", d * 256, d * 256 + 256)
                            else:
                                dst = st4[:, which, (s + 1) % 2, :]
                            st.link(dve.tensor_tensor(dst, ps[:, ci * 256:(ci + 1) * 256], st4[:, which, s % 2, :],
                                                      ALU.add))
                            ins = dve.tensor_tensor(
                                dst.rearrange("p (q i) -> p q i", i=HEAD), dst.rearrange("p (q i) -> p q i", i=HEAD),
                                pC3[:, c, :].unsqueeze(2).to_broadcast([P, 4, HEAD]), ALU.mult)
                            if ci < n - 1:
                                st.mark(ins)
                        ins.then_inc(rw_evV, 1)
                    else:
                        s = g
                        n = len(SCAN[d][s])
                        for ci, (chain, c) in enumerate(SCAN[d][s]):
                            c0 = tcol(c)
                            y = ysum[:, :, c0:c0 + 64]
                            yp = ps[:, ci * 256:(ci + 1) * 256].rearrange("p (q t) -> p q t", t=64)
                            if d == 0:
                                ins = dve.tensor_copy(y, yp)
                            else:
                                ins = dve.tensor_tensor(y, y, yp, ALU.add)
                            if ci < n - 1:
                                st.mark(ins)
                        ins.then_inc(rw_evV, 1)

            dve.wait_ge(rw_evV, RW_EV[RW_AT[(1, "Y", 3)]][1])
            st.settle()
            st.link(dve.tensor_tensor(tmp0, kdsum, zs[:, 0:4, :], ALU.mult))
            for p in range(4):
                ins = dve.tensor_scalar(tmp0[:, p, :], tmp0[:, p, :], sm("r_k", p, p + 1), None, ALU.mult)
            ins.then_inc(sc_ready, 1)
            for p in range(4):
                dve.wait_ge(st_mm, 8 + p + 1)
                ins = dve.tensor_tensor(gy[:, p, :], ysum[:, p, :], bank[p][:, 0:TS], ALU.subtract)
            ins.then_inc(st_in, 1)
            dve.wait_ge(st_in, 5)
            for p in range(4):
                dve.wait_ge(kk_ss, 4 + p + 1)
                dve.tensor_tensor(rt_[:, p, :], zs[:, 8 + p, :], bank[p][:, 0:TS], ALU.mult).then_inc(bonus_read, 1)
            for p in range(4):
                dve.wait_ge(st_rt, 4 + p + 1)
                st.link(dve.reciprocal(gmean[:, p, :], gmean[:, p, :]))
                st.link(dve.tensor_tensor(gy[:, p, :], gy[:, p, :], gmean[:, p, :], ALU.mult))
                st.link(dve.tensor_scalar(gy[:, p, :], gy[:, p, :], sm("lnx_g", p, p + 1), sm("lnx_b", p, p + 1),
                                          ALU.mult, ALU.add))
                st.link(dve.tensor_tensor(gy[:, p, :], gy[:, p, :], rt_[:, p, :], ALU.add))
                dve.wait_ge(kk_ss, 8 + p + 1)
                for t0, c0, n in SEG:
                    ins = dve.tensor_tensor(ya3[:, p * T + t0:p * T + t0 + n], gy[:, p, c0:c0 + n],
                                            bank[4 + p][:, c0:c0 + n], ALU.mult)
                    if t0 == 0:
                        st.mark(ins)
                ins.then_inc(mix_ready, 1)

            def residual(l, gate, c, src, done):
                for g, (a, b) in enumerate(GROUPS):
                    ins = dve.scalar_tensor_tensor(x3[:, c, a:b], src[:, a:b], mod4[:, l, gate + c, g:g + 1],
                                                   x3[:, c, a:b], ALU.mult, ALU.add)
                    if done is not None:
                        ins.then_inc(done, 1)
                return ins

            for m in range(8):
                dve.wait_ge(dense_used, dense(POS["out"] + m))
                residual(0, 16, m, bank[m], None).then_inc(res_done, 1)
            dve.wait_ge(res_done, 8)
            norm_dve(0, 1)

            def top16(rows, vals, idxs, tmps, free=None):
                for r, v in zip(rows, vals):
                    st.mark(dve.max(v[:, 0:8], r))
                st.settle()
                for r, v, i, t in zip(rows, vals, idxs, tmps):
                    st.mark(dve.max_index(i[:, 0:8], v[:, 0:8], r))
                    st.mark(dve.match_replace(t, v[:, 0:8], r, LOWEST))
                st.settle()
                for n, (v, t) in enumerate(zip(vals, tmps)):
                    ins = dve.max(v[:, 8:16], t)
                    if n == 0 and free is not None:
                        ins.then_inc(free, 1)
                        dve.wait_ge(free, free_n[0])
                    else:
                        st.mark(ins)
                st.settle()
                for v, i, t in zip(vals, idxs, tmps):
                    st.mark(dve.max_index(i[:, 8:16], v[:, 8:16], t))

            free_n = [0]

            def peer_dve(l):
                for j in range(16):
                    dve.wait_ge(s_evac, 16 * l + j + 1)
                    free_n[0] += 1
                    top16([sc_sb[:, j % 2, b, :] for b in range(3)], [sv[:, b, j, :] for b in range(3)],
                          [si[:, b, j, :] for b in range(3)], [stmp[:, j % 2, b, :] for b in range(3)], s_free)
                st.settle()
                st.mark(dve.tensor_copy(sif, si))
                sv5 = sv.rearrange("p b (h c) k -> p b h c k", c=2)
                sif5 = sif.rearrange("p b (h c) k -> p b h c k", c=2)
                for b in range(3):
                    st.link(dve.tensor_tensor(
                        cand.rearrange("p h (a k) -> p h a k", a=16),
                        sv5[:, b, :, 0, :].unsqueeze(3).to_broadcast([P, 8, 16, 16]),
                        sv5[:, b, :, 1, :].unsqueeze(2).to_broadcast([P, 8, 16, 16]), ALU.add))
                    top16([cand[:, h, :] for h in range(8)], [fv[:, b, h, :] for h in range(8)],
                          [fi[:, b, h, :] for h in range(8)], [ctmp[:, h, :] for h in range(8)])
                    st.settle()
                dve.tensor_tensor(ge, fv, fv[:, :, :, 0:1].to_broadcast([P, 3, 8, 16]), ALU.subtract)\
                   .then_inc(cand_max, 1)
                st.mark(dve.tensor_scalar(fa_u, fi, 4, None, ALU.logical_shift_right))
                st.mark(dve.tensor_scalar(fb_u, fi, 15, None, ALU.bitwise_and))
                st.settle()
                st.mark(dve.tensor_copy(fa, fa_u))
                st.mark(dve.tensor_copy(fb, fb_u))
                st.settle()
                shape = [P, 8, 16, 16]
                pos = sm("iota", 0, 16).unsqueeze(1).unsqueeze(1).to_broadcast(shape)
                for b in range(3):
                    for oh, f, c in ((oh1, fa, 0), (oh2, fb, 1)):
                        st.mark(dve.tensor_tensor(oh, pos, f[:, b].unsqueeze(3).to_broadcast(shape), ALU.is_equal))
                    st.settle()
                    for oh, c in ((oh1, 0), (oh2, 1)):
                        st.mark(dve.tensor_tensor(oh, oh, sif5[:, b, :, c, :].unsqueeze(2).to_broadcast(shape),
                                                  ALU.mult))
                    st.settle()
                    for oh, c in ((oh1, 0), (oh2, 1)):
                        dve.tensor_reduce(routes[:, c, b].rearrange("p (h k) -> p h k", k=16), oh, AX, ALU.add)\
                           .then_inc(route, 1)
                    dve.wait_ge(route, 7 * l + 2 * b + 2)
                dve.wait_ge(e_ready, l + 1)
                st.link(dve.tensor_reduce(gsum, ge, AX, ALU.add))
                st.link(dve.reciprocal(gsum, gsum))
                dve.tensor_tensor(routes[:, 2].rearrange("p b (h k) -> p b h k", k=16), ge,
                                  gsum.to_broadcast([P, 3, 8, 16]), ALU.mult).then_inc(route, 1)
                dve.wait_ge(route_e, 3 * l + 3)
                st.link(dve.tensor_tensor(gate_rest, bank[4][:, 0:T], gateT[:, 0, :], ALU.subtract))
                st.link(dve.tensor_copy(gateT[:, 1, :], gate_rest))
                st.link(dve.tensor_tensor(gate_rest, gate_rest, gateT[:, 1, :], ALU.subtract))
                st.link(dve.tensor_copy(gateT[:, 2, :], gate_rest))
                V0, M0, U0 = NK * l, NK * l, NK * l
                for first, uq, vq, gq_ in PHASES:
                    w = 2 if uq is not None and vq is not None else 1
                    steps = 4 // w
                    H0 = 2 * JQ * l + JQ * (vq or 0)
                    n = JQ // steps

                    def hots(i, s):
                        g = M0 + gq_ * JQ + s
                        t = bass.ds(val(i, steps * GRP, s * GRP), GRP)
                        dve.wait_ge(tok_mm, val(i, steps, g + 1))
                        dve.tensor_tensor(oh_i[:, s % 2], sm("iota").unsqueeze(1).to_broadcast([P, GRP, P]),
                                          routeT[:, 0, t].unsqueeze(2).to_broadcast([P, GRP, P]), ALU.is_equal)\
                           .then_inc(oh_ready, 1)
                        dve.wait_ge(oh_ready, val(i, 2 * steps, 2 * g + 1))
                        dve.tensor_tensor(oh_j, sm("iota", gq_ * JQ, (gq_ + 1) * JQ).unsqueeze(1)
                                          .to_broadcast([P, GRP, JQ]),
                                          routeT[:, 1, t].unsqueeze(2).to_broadcast([P, GRP, JQ]), ALU.is_equal)\
                           .then_inc(col_ready, 1)

                    def gated_cols(i, s):
                        t = bass.ds(val(i, steps * GRP, s * GRP), GRP)
                        dve.wait_ge(col_ready, val(i, steps, M0 + gq_ * JQ + s + 1))
                        dve.tensor_tensor(oh_g, oh_j.unsqueeze(2).to_broadcast([P, GRP, 3, JQ]),
                                          gateT[:, :, t].rearrange("p y t -> p t y").unsqueeze(3)
                                          .to_broadcast([P, GRP, 3, JQ]), ALU.mult).then_inc(oh_ready, 1)

                    def coef_lo(i, s):
                        sl = s % 2
                        dve.wait_ge(chi, val(i, steps, V0 + vq * JQ + s + 1))
                        dve.tensor_tensor(cp4[:, sl, 1, :],
                                          buf4[:, vq % 2, bass.ds(val(i, steps, s), 1), :]
                                          .rearrange("p o t -> p (o t)"),
                                          cp4[:, sl, 0, :].bitcast(F32), ALU.subtract).then_inc(clo, 1)

                    def gate_half(i, s, h):
                        n = val(i, steps, H0 + s + 1)
                        if h == 0:
                            dve.wait_ge(half_mm, n)
                        else:
                            dve.wait_ge(tok_mm, val(i, steps, M0 + gq_ * JQ + s + 3))
                        cols = bank[7][:, 0:GRP * JQ].rearrange("p (t y j) -> p j t y", y=2, j=JQ)
                        total = gate_sum[:, :].rearrange("p (j t) -> p j t", j=JQ)
                        dst = buf4[:, gq_ % 2, :, bass.ds(val(i, steps * GRP, s * GRP + h * GRP // 2), GRP // 2)]
                        dve.tensor_reduce(total, cols, AX, ALU.add).then_inc(sum_ready, 1)
                        dve.wait_ge(sum_ready, val(i, 2 * steps, 2 * H0 + 2 * s + h + 1))
                        dve.tensor_tensor(dst, total, dst, ALU.mult).then_inc(mult_done if h else half_done, 1)

                    def body(i, last):
                        for s in range(steps):
                            end = last and s == steps - 1
                            if gq_ is not None and not end:
                                hots(i, s + 1)
                            if vq is not None and not end:
                                coef_lo(i, s + 1)
                            if w == 2:
                                gate_half(i, s, 0)
                                gate_half(i, s, 1)
                                if not end:
                                    gated_cols(i, s + 1)
                                continue
                            if gq_ is not None:
                                gb = 7 if (vq is not None) else (7, 4)[s % 2]
                                dve.wait_ge(tok_mm, val(i, steps, M0 + gq_ * JQ + s + 3))
                                dst = buf4[:, gq_ % 2, :, bass.ds(val(i, steps * GRP, s * GRP), GRP)]
                                dve.tensor_tensor(dst, bank[gb][:, 0:JQ * GRP].rearrange("p (t j) -> p j t", j=JQ),
                                                  dst, ALU.mult).then_inc(mult_done, 1)
                                if not end:
                                    gated_cols(i, s + 1)

                    if vq is not None:
                        coef_lo(0, 0)
                    if gq_ is not None:
                        dve.wait_ge(gelu_done, U0 + (gq_ + 1) * JQ + 2)
                        hots(0, 0)
                        gated_cols(0, 0)
                    with dve.Fori(0, n - 1) as it:
                        body(it, False)
                    body(n - 1, True)
                for c in range(DC):
                    dve.wait_ge(out_t, 8 * l + c + 1)
                    residual(l, 40, c, bank[6 + c % 2], out_used)

            peer_dve(0)
            dve.wait_ge(out_used, 16)
            norm_dve(1, 0)
            dve.wait_ge(pool_init, 7)
            def conv(m, i, t):
                out = row((acc, accs)[t % 2], m)
                dve.wait_ge(conv_tap, val(i, TAP_ROUND, m * DVE_TAPS + t - 1))
                dve.scalar_tensor_tensor(out, zc[:, m, :, bass.ds(val(i, TAP_ROUND, t), ROW)],
                                         small[:, bass.ds(val(i, DC * TAP_ROUND, SM["conv_k"][0] + DC * t + m), 1)],
                                         out, ALU.mult, ALU.add).then_inc(conv_tap, 1)

            def conv_join(m):
                dve.wait_ge(pool_tap, 4 * (m + 1))
                dve.wait_ge(conv_tap, DVE_TAPS * (m + 1))
                st.link(dve.tensor_tensor(acc[:, m, :], acc[:, m, :], accs[:, m, :], ALU.add))
                dve.tensor_tensor(acc[:, m, :], acc[:, m, :], acq[:, m, :], ALU.add).then_inc(conv_done, 1)

            for m in range(DC):
                dve.wait_ge(glu_g, m + 1)
                dve.scalar_tensor_tensor(
                    zc[:, m, :, HALO:HALO + ROW], bank[2 * (m % 2)][:, 0:T].rearrange("p (r t) -> p r t", t=ROW),
                    sm("b_pw1", m, m + 1), glug[:, m % 2, :].rearrange("p (r t) -> p r t", t=ROW),
                    ALU.add, ALU.mult).then_inc(glu_done, 1)
                if m >= 2:
                    conv_join(m - 2)
                dve.wait_ge(halo_done, 2 * m + 2)
                dve.tensor_scalar(row(acc, m), zc[:, m, :, 0:ROW], sm("conv_k", m, m + 1), sm("conv_b", m, m + 1),
                                  ALU.mult, ALU.add).then_inc(conv_tap, 1)
                dve.tensor_scalar(row(accs, m), zc[:, m, :, 1:1 + ROW], sm("conv_k", DC + m, DC + m + 1), None,
                                  ALU.mult).then_inc(conv_tap, 1)
                conv(m, 0, 2)
                with dve.Fori(0, (DVE_TAPS - 3) // TAP_ROUND) as it:
                    for t in range(TAP_ROUND):
                        conv(m, it, 3 + t)
            conv_join(DC - 2)
            conv_join(DC - 1)
            dve.wait_ge(st_mm, 17)
            for c in range(DC):
                dve.tensor_tensor(accs[:, c, :], acc[:, c, :], bank[4][:, 0:T], ALU.subtract).then_inc(st_in, 1)
            dve.wait_ge(st_in, 13)
            dve.wait_ge(st_rt, 9)
            st.link(dve.reciprocal(lrstd, lroot))
            for c in range(DC):
                dve.tensor_tensor(accs[:, c, :], accs[:, c, :], lrstd, ALU.mult).then_inc(st_in, 1)
            mod_add(10)
            mod_add(11)
            for m in range(8):
                dve.wait_ge(pw2_ev, m + 1)
                residual(1, 16, m, pw2t[:, m % 2, :], None).then_inc(res_done, 1)
            dve.wait_ge(res_done, 16)
            norm_dve(1, 1)
            peer_dve(1)
            dve.wait_ge(out_used, 32)
            norm_dve(0, 2)


def _constants():
    c = {}
    c["ident"] = np.eye(P)
    c["mean_d"] = np.full((P, P), 1.0 / D)
    c["mean_p"] = np.full((P, P), 1.0 / P)
    blk = (np.arange(P)[:, None] // HEAD == np.arange(P)[None, :] // HEAD) * 1.0
    c["head_sum"] = blk
    c["head_mean"] = blk / HEAD
    c["iota"] = np.tile(np.arange(P), (P, 1))
    s = (np.arange(P) % CHUNK)[:, None]
    t = np.arange(CHUNK)[None, :]
    c["strict"] = np.concatenate([s < t, s > t], 1)
    c["incl"] = np.concatenate([s <= t, s >= t], 1)
    bands = []
    for d in range(2):
        lo, hi = (s, t) if d == 0 else (t, s)
        for n in (1, 2, 4, 8, 16, 32):
            bands.append((lo // (2 * n) == hi // (2 * n)) & (lo // n % 2 == 0) & (hi // n % 2 == 1))
    c["bands"] = np.concatenate(bands, 1)
    c["eye64"] = (s == t)
    keep = np.ones((2, TS))
    for ch in range(NCH):
        keep[0, tcol(ch)] = 0
        keep[1, tcol(ch) + CHUNK - 1] = 0
    keep[:, T_CTX] = 0
    c["keep"] = np.tile(keep.reshape(1, -1), (P, 1))
    c["zeros"] = np.zeros((P, P))
    c["ones"] = np.ones((P, P))
    return {k: np.asarray(v, np.float32) for k, v in c.items()}


def _cols(v):
    return v.reshape(-1, P).T


def _tiles(w):
    n = w.shape[1] // P
    return w.reshape(DC, P, n, P).transpose(2, 1, 0, 3).reshape(n, P, D)


def kernel(**inputs):
    import concourse.bacc as _bacc
    from concourse.bass_utils import run_bass_kernel_spmd as _run

    a = {k: np.asarray(v) for k, v in inputs.items()}
    sm = _constants()
    cc = np.concatenate
    sm["b_mod"] = cc([_cols(a["b_mod"][l]) for l in range(2)], 1)
    sm["norm1"] = cc([_cols(a["norm1"][l]) for l in range(2)], 1)
    sm["norm2"] = cc([_cols(a["norm2"][l]) for l in range(2)], 1)
    sm["norm_f"] = _cols(a["norm_f"])
    sm["mu"] = _cols(a["mu_a"][0])
    sm["w0"] = cc([_cols(a["w0"][0, d]) for d in range(2)], 1)
    sm["a0"] = cc([_cols(a["a0"][0, d]) for d in range(2)], 1)
    for k in ("k_k", "k_a", "r_k", "lnx_g", "lnx_b", "lnv_g", "lnv_b", "b_pw1", "conv_b", "lnc_g", "lnc_b", "b_pw2"):
        sm[k] = _cols(a[k][0])
    sm["conv_k"] = cc([_cols(a["conv_k"][0, w]) for w in range(CONV_W)], 1)
    sm["w2"] = a["w2"][0].reshape(P, A_W)
    sm["a2"] = a["a2"][0].reshape(P, A_W)
    sm["g2"] = a["g2"][0]
    sm["w_sT"] = a["w_s"][0].transpose(2, 0, 1).reshape(P, 4 * P)
    b_s = np.zeros((P, 4 * P), np.float32)
    b_s[0] = a["b_s"][0].reshape(-1)
    sm["b_s"] = b_s
    sm["sk"] = a["sub_keys"].transpose(3, 0, 1, 2).reshape(P, 4 * P)
    sm["s0"] = a["state_rwkv"][0, 0].reshape(2, NP_, 2, HEAD, HEAD).transpose(2, 4, 0, 1, 3).reshape(P, 2 * NP_ * HEAD)
    cv = cc([a["c_ctx"].reshape(1, D), a["c"].reshape(1, D)], 0)
    sm["cvec"] = cv.reshape(2, DC, P).transpose(2, 1, 0).reshape(P, 16)
    for k, n in SMALL + MIXER:
        assert sm[k].shape == (P, n), (k, sm[k].shape, n)
    small, mixer = (np.ascontiguousarray(cc([sm[k] for k, _ in part], 1)) for part in (SMALL, MIXER))
    pw1 = _tiles(a["w_pw1"][0])
    pw1 = pw1.reshape(2, 8, P, D).transpose(1, 0, 2, 3).reshape(16, P, D)
    mod = [a["w_mod"][l].reshape(DC, P, 6, D).transpose(2, 0, 1, 3).reshape(48, P, D) for l in range(2)]
    w = cc([mod[0], _tiles(a["w_in_ab"][0]), mod[1][0:32], _tiles(a["w_out_ab"][0]),
            _tiles(a["w_query"][0]), pw1, mod[1][32:48], _tiles(a["w_pw2"][0]),
            _tiles(a["w_query"][1])], 0)
    e_u = np.ascontiguousarray(a["expert_u"].reshape(2, NK, NK, DC, P).transpose(0, 2, 4, 3, 1)).reshape(2, NK, P, D)
    x_t = np.ascontiguousarray(cc([a["x_prompt"][0], a["x_sample"][0]], 0).T)
    arrays = {"x_t": x_t, "small": small, "mixer": mixer, "w_tiles": w, "e_u": e_u,
              "e_v": a["expert_v"].reshape(2, NK, NK, D)}

    nc = _bacc.Bacc("TRN2", target_bir_lowering=False, num_devices=1)
    ap = {k: nc.dram_tensor("in_" + k, v.shape, F32, kind="ExternalInput").ap() for k, v in arrays.items()}
    y_t = nc.dram_tensor("y_t", (D, T), F32, kind="ExternalOutput").ap()
    s_new = nc.dram_tensor("s_new", (2, NP_, P, HEAD), F32, kind="ExternalOutput").ap()
    build_trunk(nc, ap["x_t"], ap["small"], ap["mixer"], ap["w_tiles"], ap["e_u"],
                ap["e_v"].rearrange("l i j d -> l j i d"), y_t, s_new)
    r = _run(nc, [{"in_" + k: v for k, v in arrays.items()}], core_ids=[0]).results[0]
    y = r["y_t"].T
    s = r["s_new"].reshape(2, NP_, 2, HEAD, HEAD).transpose(0, 1, 2, 4, 3).reshape(1, 1, 2, 8, HEAD, HEAD)
    return (np.ascontiguousarray(y[None, :T_CTX]), np.ascontiguousarray(y[None, T_CTX:]), np.ascontiguousarray(s))
```
